# Optimizing a Trainium2 kernel written in Bass

```python
import jax, jax.numpy as jnp
from jax import lax
import numpy as np

D_MODEL = 1024
BATCH = 1
SEQ = 512
DEPTH = 1

DN_HEADS = 4
DN_HEAD_DIM = 128
DN_WIDTH = DN_HEADS * DN_HEAD_DIM
DN_CONV = 5
DN_CHUNK = 64
N_DIR = 2
SWA_Q_HEADS = 8
SWA_KV_HEADS = 2
SWA_HEAD_DIM = 64
SWA_WIDTH = SWA_Q_HEADS * SWA_HEAD_DIM
SWA_KV_WIDTH = SWA_KV_HEADS * SWA_HEAD_DIM
WINDOW = 128
BLOCK = 128
ROPE_THETA = 10000.0
EPS = 1e-6
MIX_WIDTH = DN_WIDTH + SWA_WIDTH
SPLITS = (DN_WIDTH, DN_WIDTH, DN_WIDTH, DN_WIDTH, N_DIR * DN_HEADS, N_DIR * DN_HEADS,
          SWA_WIDTH, SWA_KV_WIDTH, SWA_KV_WIDTH, SWA_WIDTH)
IN_WIDTH = 4 * DN_WIDTH + 2 * N_DIR * DN_HEADS + 2 * SWA_WIDTH + 2 * SWA_KV_WIDTH


def rms_norm(x, w):
    xf = x.astype(jnp.float32)
    y = xf * lax.rsqrt(jnp.mean(xf * xf, axis=-1, keepdims=True) + EPS)
    return (y * w.astype(jnp.float32)).astype(x.dtype)

def l2_norm(x):
    return x * lax.rsqrt(jnp.sum(x * x, axis=-1, keepdims=True) + EPS)

def rope_tables(seq, dim):
    inv_freq = ROPE_THETA ** (-jnp.arange(0, dim, 2, dtype=jnp.float32) / dim)
    ang = jnp.arange(seq, dtype=jnp.float32)[:, None] * inv_freq[None, :]
    ang = jnp.concatenate([ang, ang], axis=-1)
    return jnp.cos(ang), jnp.sin(ang)

def rotary(x, cos, sin):
    half = x.shape[-1] // 2
    rot = jnp.concatenate([-x[..., half:], x[..., :half]], axis=-1)
    return x * cos[:, None, :] + rot * sin[:, None, :]

def centred_depthwise_conv(x, w):
    pad = (w.shape[0] - 1) // 2
    return lax.conv_general_dilated(
        x, w[:, None, :].astype(x.dtype), window_strides=(1,), padding=[(pad, pad)],
        dimension_numbers=('NWC', 'WIO', 'NWC'), feature_group_count=x.shape[-1])

def gated_delta_rule_chunked(q, k, v, g, beta):
    b, t, h, dk = q.shape
    dv = v.shape[-1]
    c = DN_CHUNK
    n = t // c

    def to_chunks(a):
        return jnp.moveaxis(a.reshape(b, n, c, h, *a.shape[3:]), 3, 1)

    q, k, v, g, beta = (to_chunks(a) for a in (q, k, v, g, beta))
    g = jnp.cumsum(g, axis=-1)
    incl = jnp.tril(jnp.ones((c, c), dtype=bool))
    strict = jnp.tril(jnp.ones((c, c), dtype=bool), -1)
    decay = jnp.exp(jnp.where(incl, g[..., :, None] - g[..., None, :], -jnp.inf))
    k_beta = k * beta[..., None]
    m = jnp.where(strict, jnp.einsum('bhncd,bhnsd->bhncs', k_beta, k) * decay, 0.0)
    eye = jnp.eye(c, dtype=q.dtype)
    t_inv = lax.linalg.triangular_solve(eye + m, jnp.broadcast_to(eye, m.shape),
                                        left_side=True, lower=True, unit_diagonal=True)
    u = jnp.einsum('bhncs,bhnse->bhnce', t_inv, v * beta[..., None])
    w = jnp.einsum('bhncs,bhnsd->bhncd', t_inv, k_beta * jnp.exp(g)[..., None])
    a_intra = jnp.where(incl, jnp.einsum('bhncd,bhnsd->bhncs', q, k) * decay, 0.0)

    def step(state, inp):
        q_i, k_i, u_i, w_i, g_i, a_i = inp
        v_new = u_i - jnp.einsum('bhcd,bhde->bhce', w_i, state)
        o = (jnp.einsum('bhcd,bhde->bhce', q_i * jnp.exp(g_i)[..., None], state)
             + jnp.einsum('bhcs,bhse->bhce', a_i, v_new))
        g_last = g_i[..., -1]
        k_dec = k_i * jnp.exp(g_last[..., None] - g_i)[..., None]
        state = state * jnp.exp(g_last)[..., None, None] + jnp.einsum('bhcd,bhce->bhde', k_dec, v_new)
        return state, o

    xs = tuple(jnp.moveaxis(a, 2, 0) for a in (q, k, u, w, g, a_intra))
    state0 = jnp.zeros((b, h, dk, dv), dtype=q.dtype)
    _, o = lax.scan(step, state0, xs)
    o = jnp.moveaxis(o, 0, 2)
    return jnp.moveaxis(o, 1, 3).reshape(b, t, h, dv)

def gated_deltanet_bidir(q, k, v, beta_logit, decay_logit, conv_w, a_log, dt_bias):
    b, s, _ = q.shape
    qkv = jax.nn.silu(centred_depthwise_conv(jnp.concatenate([q, k, v], axis=-1), conv_w))
    q, k, v = jnp.split(qkv.astype(jnp.float32), 3, axis=-1)
    q = l2_norm(q.reshape(b, s, DN_HEADS, DN_HEAD_DIM)) * (DN_HEAD_DIM ** -0.5)
    k = l2_norm(k.reshape(b, s, DN_HEADS, DN_HEAD_DIM))
    v = v.reshape(b, s, DN_HEADS, DN_HEAD_DIM)
    beta = jax.nn.sigmoid(beta_logit.astype(jnp.float32).reshape(b, s, N_DIR, DN_HEADS))
    dl = decay_logit.astype(jnp.float32).reshape(b, s, N_DIR, DN_HEADS)
    g = -jnp.exp(a_log.astype(jnp.float32)) * jax.nn.softplus(dl + dt_bias.astype(jnp.float32))
    fwd = gated_delta_rule_chunked(q, k, v, g[:, :, 0], beta[:, :, 0])
    flip = lambda a: jnp.flip(a, axis=1)
    bwd = flip(gated_delta_rule_chunked(flip(q), flip(k), flip(v), flip(g[:, :, 1]), flip(beta[:, :, 1])))
    return fwd + bwd

def windowed_gqa_with_sinks(q, k, v, q_norm_w, k_norm_w, sinks):
    b, s, _ = q.shape
    nb = s // BLOCK
    nw = WINDOW // BLOCK
    span = BLOCK + 2 * WINDOW
    grp = SWA_Q_HEADS // SWA_KV_HEADS
    cos, sin = rope_tables(s, SWA_HEAD_DIM)
    q = rotary(rms_norm(q.astype(jnp.float32).reshape(b, s, SWA_Q_HEADS, SWA_HEAD_DIM), q_norm_w), cos, sin)
    k = rotary(rms_norm(k.astype(jnp.float32).reshape(b, s, SWA_KV_HEADS, SWA_HEAD_DIM), k_norm_w), cos, sin)
    v = v.astype(jnp.float32).reshape(b, s, SWA_KV_HEADS, SWA_HEAD_DIM)
    qb = q.reshape(b, nb, BLOCK, SWA_KV_HEADS, grp, SWA_HEAD_DIM)

    def band(a):
        ap = jnp.pad(a, ((0, 0), (WINDOW, WINDOW), (0, 0), (0, 0)))
        ab = ap.reshape(b, nb + 2 * nw, BLOCK, SWA_KV_HEADS, SWA_HEAD_DIM)
        return jnp.concatenate([ab[:, i:i + nb] for i in range(2 * nw + 1)], axis=2)

    kb, vb = band(k), band(v)
    scores = jnp.einsum('bnqhgd,bnkhd->bnhgqk', qb, kb) * (SWA_HEAD_DIM ** -0.5)
    q_pos = jnp.arange(nb)[:, None] * BLOCK + jnp.arange(BLOCK)[None, :]
    k_pos = jnp.arange(nb)[:, None] * BLOCK - WINDOW + jnp.arange(span)[None, :]
    rel = k_pos[:, None, :] - q_pos[:, :, None]
    valid = (jnp.abs(rel) <= WINDOW) & (k_pos[:, None, :] >= 0) & (k_pos[:, None, :] < s)
    scores = jnp.where(valid[None, :, None, None], scores, -jnp.inf)
    sink = sinks.astype(jnp.float32).reshape(SWA_KV_HEADS, grp)[None, None, :, :, None, None]
    mx = jnp.maximum(jnp.max(scores, axis=-1, keepdims=True), sink)
    p = jnp.exp(scores - mx)
    denom = jnp.sum(p, axis=-1, keepdims=True) + jnp.exp(sink - mx)
    out = jnp.einsum('bnhgqk,bnkhd->bnqhgd', p / denom, vb)
    return out.reshape(b, s, SWA_WIDTH)

def first_inputs(seed: int = 0) -> dict:
    key = jax.random.key(seed)
    ks = jax.random.split(key, 12)
    x = jax.random.normal(ks[0], (BATCH, SEQ, D_MODEL), jnp.float32)
    norm_w = 1.0 + 0.02 * jax.random.normal(ks[1], (DEPTH, D_MODEL), jnp.float32)
    w_in = jax.random.normal(ks[2], (DEPTH, D_MODEL, IN_WIDTH), jnp.float32) * D_MODEL ** -0.5
    dn_conv_w = jax.random.normal(ks[3], (DEPTH, DN_CONV, 3 * DN_WIDTH), jnp.float32) * DN_CONV ** -0.5
    dn_a_log = jnp.log(jax.random.uniform(ks[4], (DEPTH, N_DIR, DN_HEADS), jnp.float32, 1.0, 16.0))
    dt = jnp.exp(jax.random.uniform(ks[5], (DEPTH, N_DIR, DN_HEADS), jnp.float32,
                                    float(np.log(1e-3)), float(np.log(1e-1))))
    dn_dt_bias = dt + jnp.log(-jnp.expm1(-dt))
    dn_out_norm_w = 1.0 + 0.02 * jax.random.normal(ks[6], (DEPTH, DN_HEAD_DIM), jnp.float32)
    swa_q_norm_w = 1.0 + 0.02 * jax.random.normal(ks[7], (DEPTH, SWA_HEAD_DIM), jnp.float32)
    swa_k_norm_w = 1.0 + 0.02 * jax.random.normal(ks[8], (DEPTH, SWA_HEAD_DIM), jnp.float32)
    swa_sinks = jax.random.normal(ks[9], (DEPTH, SWA_Q_HEADS), jnp.float32)
    w_out = jax.random.normal(ks[10], (DEPTH, MIX_WIDTH, D_MODEL), jnp.float32) * MIX_WIDTH ** -0.5
    return {'x': x, 'norm_w': norm_w, 'w_in': w_in, 'dn_conv_w': dn_conv_w, 'dn_a_log': dn_a_log,
            'dn_dt_bias': dn_dt_bias, 'dn_out_norm_w': dn_out_norm_w, 'swa_q_norm_w': swa_q_norm_w,
            'swa_k_norm_w': swa_k_norm_w, 'swa_sinks': swa_sinks, 'w_out': w_out}

def first_block(x, norm_w, w_in, dn_conv_w, dn_a_log, dn_dt_bias, dn_out_norm_w,
              swa_q_norm_w, swa_k_norm_w, swa_sinks, w_out):
    b, s, _ = x.shape
    cuts = []
    acc = 0
    for width in SPLITS[:-1]:
        acc += width
        cuts.append(acc)
    for l in range(DEPTH):
        h = rms_norm(x, norm_w[l])
        proj = h @ w_in[l].astype(h.dtype)
        (dn_q, dn_k, dn_v, dn_z, dn_beta, dn_decay,
         sw_q, sw_k, sw_v, sw_z) = jnp.split(proj, cuts, axis=-1)
        dn = gated_deltanet_bidir(dn_q, dn_k, dn_v, dn_beta, dn_decay,
                                  dn_conv_w[l], dn_a_log[l], dn_dt_bias[l])
        dn = rms_norm(dn, dn_out_norm_w[l]).reshape(b, s, DN_WIDTH)
        dn = dn * jax.nn.silu(dn_z.astype(jnp.float32))
        sw = windowed_gqa_with_sinks(sw_q, sw_k, sw_v, swa_q_norm_w[l], swa_k_norm_w[l], swa_sinks[l])
        sw = sw * jax.nn.silu(sw_z.astype(jnp.float32))
        mix = jnp.concatenate([dn, sw], axis=-1).astype(x.dtype)
        x = x + mix @ w_out[l].astype(x.dtype)
    return x


MIX_WIDTH_2 = D_MODEL
ATT_WIDTH = MIX_WIDTH_2 // 2
GMLP_WIDTH = MIX_WIDTH_2 - ATT_WIDTH
ATT_HEAD_DIM = 64
N_ATT_HEADS = ATT_WIDTH // ATT_HEAD_DIM
N_GMLP_GROUPS = 8
GMLP_GROUP_DIM = GMLP_WIDTH // N_GMLP_GROUPS
CHUNK = 128
Q_BLOCK = 128
D_FF = 2816
CONV_WIDTH = 3

Q_END = ATT_WIDTH
K_END = 2 * ATT_WIDTH
V_END = 3 * ATT_WIDTH
U_END = V_END + GMLP_WIDTH
G_END = U_END + GMLP_WIDTH
IN_COLS = G_END + N_ATT_HEADS


def rmsnorm(x, gain):
    xf = x.astype(jnp.float32)
    y = xf * lax.rsqrt(jnp.mean(xf * xf, axis=-1, keepdims=True) + EPS)
    return y.astype(x.dtype) * gain

def forgetting_attention(q, k, v, log_f):
    B, S, H, Dh = q.shape
    nb = S // Q_BLOCK
    c = jnp.cumsum(log_f, axis=1)
    c_k = c.transpose(0, 2, 1)[:, :, None, :]
    key_pos = jnp.arange(S)
    qb = q.reshape(B, nb, Q_BLOCK, H, Dh).transpose(1, 0, 2, 3, 4)
    cb = c.reshape(B, nb, Q_BLOCK, H).transpose(1, 0, 3, 2)
    pb = key_pos.reshape(nb, Q_BLOCK)
    scale = Dh ** -0.5

    def block(args):
        qi, ci, pi = args
        logits = jnp.einsum('bqhd,bkhd->bhqk', qi, k).astype(jnp.float32) * scale
        logits = logits + ci[..., None] - c_k
        causal = pi[:, None] >= key_pos[None, :]
        logits = jnp.where(causal, logits, -jnp.inf)
        p = jax.nn.softmax(logits, axis=-1).astype(v.dtype)
        return jnp.einsum('bhqk,bkhd->bqhd', p, v)

    out = lax.map(block, (qb, cb, pb))
    return out.transpose(1, 0, 2, 3, 4).reshape(B, S, H * Dh)

def chunked_spatial_gating(u, vg, v_gain, w_s, b_s):
    B, S, G, Dg = u.shape
    nc = S // CHUNK
    vg = rmsnorm(vg, v_gain.reshape(G, Dg))
    vc = vg.reshape(B, nc, CHUNK, G, Dg)
    w = w_s * jnp.tril(jnp.ones((CHUNK, CHUNK), dtype=w_s.dtype))
    mixed = jnp.einsum('gij,bnjgd->bnigd', w, vc) + b_s.T[None, None, :, :, None]
    return (u * mixed.reshape(B, S, G, Dg)).reshape(B, S, G * Dg)

def conv_ffn(x, w_up, conv_w, conv_b, w_down):
    h = x @ w_up
    h = lax.conv_general_dilated(
        h, conv_w[:, None, :], window_strides=(1,),
        padding=[(CONV_WIDTH - 1, 0)],
        dimension_numbers=('NWC', 'WIO', 'NWC'),
        feature_group_count=h.shape[-1]) + conv_b
    a, g = jnp.split(h, 2, axis=-1)
    return (jax.nn.silu(g) * a) @ w_down

def second_inputs(seed: int = 0) -> dict:
    key = jax.random.key(seed)
    ks = jax.random.split(key, 16)
    f32 = jnp.float32
    x = jax.random.normal(ks[0], (BATCH, SEQ, D_MODEL), f32)
    norm_mix_g = 1.0 + 0.02 * jax.random.normal(ks[1], (DEPTH, D_MODEL), f32)
    w_in = jax.random.normal(ks[2], (DEPTH, D_MODEL, IN_COLS), f32) * D_MODEL ** -0.5
    b_forget = 2.0 + 0.5 * jax.random.normal(ks[3], (DEPTH, N_ATT_HEADS), f32)
    gmlp_norm_g = 1.0 + 0.02 * jax.random.normal(ks[4], (DEPTH, GMLP_WIDTH), f32)
    w_spatial = jax.random.normal(ks[5], (DEPTH, N_GMLP_GROUPS, CHUNK, CHUNK), f32) * CHUNK ** -0.5
    b_spatial = 1.0 + 0.1 * jax.random.normal(ks[6], (DEPTH, N_GMLP_GROUPS, CHUNK), f32)
    w_out = jax.random.normal(ks[7], (DEPTH, MIX_WIDTH_2, D_MODEL), f32) * MIX_WIDTH_2 ** -0.5
    norm_ffn_g = 1.0 + 0.02 * jax.random.normal(ks[8], (DEPTH, D_MODEL), f32)
    w_up = jax.random.normal(ks[9], (DEPTH, D_MODEL, 2 * D_FF), f32) * D_MODEL ** -0.5
    conv_w = jax.random.normal(ks[10], (DEPTH, CONV_WIDTH, 2 * D_FF), f32) * CONV_WIDTH ** -0.5
    conv_b = 0.01 * jax.random.normal(ks[11], (DEPTH, 2 * D_FF), f32)
    w_down = jax.random.normal(ks[12], (DEPTH, D_FF, D_MODEL), f32) * D_FF ** -0.5
    norm_final_g = 1.0 + 0.02 * jax.random.normal(ks[13], (D_MODEL,), f32)
    return {"x": x, "norm_mix_g": norm_mix_g, "w_in": w_in, "b_forget": b_forget,
            "gmlp_norm_g": gmlp_norm_g, "w_spatial": w_spatial, "b_spatial": b_spatial,
            "w_out": w_out, "norm_ffn_g": norm_ffn_g, "w_up": w_up, "conv_w": conv_w,
            "conv_b": conv_b, "w_down": w_down, "norm_final_g": norm_final_g}

def second_block(x, norm_mix_g, w_in, b_forget, gmlp_norm_g, w_spatial, b_spatial,
              w_out, norm_ffn_g, w_up, conv_w, conv_b, w_down, norm_final_g):
    B, S, _ = x.shape
    h = x
    for layer in range(DEPTH):
        xn = rmsnorm(h, norm_mix_g[layer])
        proj = xn @ w_in[layer]
        q = proj[..., :Q_END].reshape(B, S, N_ATT_HEADS, ATT_HEAD_DIM)
        k = proj[..., Q_END:K_END].reshape(B, S, N_ATT_HEADS, ATT_HEAD_DIM)
        v = proj[..., K_END:V_END].reshape(B, S, N_ATT_HEADS, ATT_HEAD_DIM)
        log_f = jax.nn.log_sigmoid(
            (proj[..., G_END:] + b_forget[layer]).astype(jnp.float32))
        att = forgetting_attention(q, k, v, log_f)
        uv = jax.nn.gelu(proj[..., V_END:G_END])
        u = uv[..., :GMLP_WIDTH].reshape(B, S, N_GMLP_GROUPS, GMLP_GROUP_DIM)
        vg = uv[..., GMLP_WIDTH:].reshape(B, S, N_GMLP_GROUPS, GMLP_GROUP_DIM)
        sg = chunked_spatial_gating(u, vg, gmlp_norm_g[layer], w_spatial[layer], b_spatial[layer])
        mix = jnp.concatenate([att, sg], axis=-1)
        h = h + mix @ w_out[layer]
        h = h + conv_ffn(rmsnorm(h, norm_ffn_g[layer]), w_up[layer], conv_w[layer],
                         conv_b[layer], w_down[layer])
    return rmsnorm(h, norm_final_g)


def setup_inputs(seed=0):
    out = dict(first_inputs(seed))
    for name, value in second_inputs(seed + 1).items():
        if name != "x":
            out[name + "_2"] = value
    return out


def reference(
    x, norm_w, w_in, dn_conv_w, dn_a_log, dn_dt_bias, dn_out_norm_w, swa_q_norm_w, swa_k_norm_w,
    swa_sinks, w_out, norm_mix_g_2, w_in_2, b_forget_2, gmlp_norm_g_2, w_spatial_2, b_spatial_2,
    w_out_2, norm_ffn_g_2, w_up_2, conv_w_2, conv_b_2, w_down_2, norm_final_g_2,
):
    x = first_block(
        x, norm_w, w_in, dn_conv_w, dn_a_log, dn_dt_bias, dn_out_norm_w, swa_q_norm_w,
        swa_k_norm_w, swa_sinks, w_out,
    )
    return second_block(
        x, norm_mix_g_2, w_in_2, b_forget_2, gmlp_norm_g_2, w_spatial_2, b_spatial_2, w_out_2,
        norm_ffn_g_2, w_up_2, conv_w_2, conv_b_2, w_down_2, norm_final_g_2,
    )


_drawn_inputs = setup_inputs


def setup_inputs(seed=0):
    import zlib

    import numpy as np

    out = dict(_drawn_inputs(seed))
    spreads = {}
    factors = {'norm_w': 3.627,
     'dn_out_norm_w': 5.81,
     'swa_q_norm_w': 8.0,
     'swa_k_norm_w': 8.0,
     'swa_sinks': 8.0,
     'norm_mix_g_2': 3.922,
     'gmlp_norm_g_2': 31.745,
     'norm_ffn_g_2': 13.064,
     'conv_b_2': 27.709,
     'norm_final_g_2': 21.596,
     'b_spatial_2': 4.2,
     'b_forget_2': 3.957}
    for name, (base, spread) in spreads.items():
        noise = np.random.default_rng([zlib.crc32(name.encode()), seed]).standard_normal(out[name].shape)
        drawn = base * np.exp(spread * noise) if base else spread * noise
        out[name] = __import__('jax').numpy.asarray(drawn.astype(out[name].dtype))
    for name, factor in factors.items():
        out[name] = (out[name] * factor).astype(out[name].dtype)
    return out
```

```python
import math

import numpy as np

import concourse.bass as bass
from concourse import mybir

F32 = mybir.dt.float32
F32R = mybir.dt.float32r
BF16 = mybir.dt.bfloat16
ALU = mybir.AluOpType
ACT = mybir.ActivationFunctionType
AX = mybir.AxisListType

KB = 1024
BASE = 16512
EPS = 1e-6
NEG = -1e30
D = 1024
T = 512

P1_CH = [(j * 128, 128) for j in range(12)]
P1_TOK = [[(2048, 16), (2576, 256)], [(2064, 512)], [(2832, 512)], [(1536, 512)]]
P2_CH = [(j * 128, 128) for j in range(8)]
P2_TOK = [(1024, 512), (1536, 512), (2048, 512)]


def unit_plan():
    plan = []
    for c in P1_CH:
        plan.append(("w_in", range(8), [c], 128))
    for cols in P1_TOK:
        n = sum(w for _, w in cols)
        for k in range(0, 8, 2):
            plan.append(("w_in", range(k, k + 2), cols, n))
    for n in range(2):
        for k in range(0, 8, 2):
            plan.append(("w_out", range(k, k + 2), [(n * 512, 512)], 512))
    plan.append(("w_in_2", range(8), [(2560, 8)], 128))
    for c in P2_CH:
        plan.append(("w_in_2", range(8), [c], 128))
    for c in P2_TOK:
        for k in range(0, 8, 2):
            plan.append(("w_in_2", range(k, k + 2), [c], 512))
    for n in range(2):
        for k in range(0, 8, 2):
            plan.append(("w_out_2", range(k, k + 2), [(n * 512, 512)], 512))
    for j in range(22):
        for half in range(2):
            plan.append(("w_up_2", range(8), [(half * 2816 + j * 128, 128)], 128))
    for k in range(22):
        plan.append(("w_down_2", range(k, k + 1), [(0, 1024)], 1024))
    return plan


def pack_weights(mats):
    parts = []
    for name, ks, cols, width in unit_plan():
        m = mats[name]
        u = np.zeros((128, len(ks), width), np.float32)
        for i, k in enumerate(ks):
            at = 0
            for c, w in cols:
                u[:, i, at:at + w] = m[k * 128:(k + 1) * 128, c:c + w]
                at += w
        parts.append(u.reshape(-1))
    return np.concatenate(parts)


CF = {}
_at = 0
for _name, _w in (("ident", 128), ("triU", 128), ("triL", 128), ("SL", 128), ("SU", 128), ("ones", 128),
                  ("LM", 14 * 128), ("cos", 256), ("sin", 256)):
    CF[_name] = (_at, _w)
    _at += _w
NCF = _at


def const_tile():
    c = np.zeros((128, NCF), np.float32)
    i = np.arange(128)[:, None]
    j = np.arange(128)[None, :]
    put = lambda name, v: c.__setitem__((slice(None), slice(CF[name][0], CF[name][0] + CF[name][1])), v)
    put("ident", i == j)
    put("triU", i <= j)
    put("triL", i >= j)
    put("SL", i > j)
    put("SU", i < j)
    put("ones", 1.0)
    lm = []
    for d in range(2):
        for lvl in range(7):
            s = 1 << lvl
            a, b = (i, j) if d == 0 else (j, i)
            lm.append(((a // (2 * s) == b // (2 * s)) & ((a // s) % 2 == 0) & ((b // s) % 2 == 1)) | (i == j))
    put("LM", np.concatenate(lm, axis=1))
    inv = (np.float32(10000.0) ** (-np.arange(0, 64, 2, dtype=np.float32) / np.float32(64))).astype(np.float32)
    ang = np.arange(512, dtype=np.float32)[:, None] * inv[None, :]
    cos = np.cos(ang.astype(np.float64)).astype(np.float32)
    sin = np.sin(ang.astype(np.float64)).astype(np.float32)
    tok = lambda a: a.reshape(4, 128, 64).transpose(1, 0, 2).reshape(128, 256)
    put("cos", tok(np.concatenate([cos, cos], axis=1)))
    put("sin", tok(np.concatenate([-sin, sin], axis=1)))
    return c


def tri_big():
    j = np.arange(896)[None, :]
    return (j >= np.arange(128)[:, None] + 384).astype(np.float32)


def sel_tile():
    s = np.zeros((96, 8, 128), np.float32)
    for h in range(8):
        for part in range(3):
            s[32 * part + h, h, :] = -8.0
    return s.reshape(96, 1024)


PP = {"norm_w": (0, 8), "norm_mix_g_2": (8, 8), "norm_ffn_g_2": (16, 8), "dn_conv_w": (24, 60),
      "conv_w_2": (84, 132), "conv_b_2": (216, 44), "b_spatial_2": (260, 8), "b_forget_2": (268, 1)}
NPP = 272
PR = {"dn_a_log": (0, 8), "dn_dt_bias": (8, 8), "swa_sinks": (16, 8), "dn_out_norm_w": (24, 128),
      "swa_q_norm_w": (152, 64), "swa_k_norm_w": (216, 64), "gmlp_norm_g_2": (280, 512), "norm_final_g_2": (792, 1024)}
NPR = 1816


class Queues:

    def __init__(self, nc):
        self.q = {e: [] for e in ("pe", "act", "dve", "pool", "sp")}
        self.sem = {e: nc.alloc_semaphore("done_" + e) for e in self.q}
        self.n = dict.fromkeys(self.q, 0)
        self.waited = {e: {} for e in self.q}

    def put(self, eng, fn, waits=(), inc=True):
        for w in waits:
            if w is not None:
                sem, value = w
                if self.waited[eng].get(sem.name, 0) < value:
                    self.waited[eng][sem.name] = value
                    self.q[eng].append(lambda e, sem=sem, value=value: e.wait_ge(sem, value))
        if not inc:
            self.q[eng].append(fn)
            return None
        self.n[eng] += 1
        sem = self.sem[eng]
        self.q[eng].append(lambda e: fn(e).then_inc(sem, 1))
        return (sem, self.n[eng])

    def dma(self, eng, out, in_, sem, value, waits=()):
        self.put(eng, lambda e: e.dma_start(out, in_).then_inc(sem, 16), waits, inc=False)
        return (sem, value)


class BankFree(list):

    def __init__(self):
        super().__init__([None] * 8)
        self.held = set()

    def __setitem__(self, b, token):
        super().__setitem__(b, token)
        self.held.discard(b)


class Banks:

    def __init__(self, free, ids):
        self.free, self.ids, self.i = free, list(ids), 0

    def take(self):
        for _ in self.ids:
            b = self.ids[self.i % len(self.ids)]
            self.i += 1
            if b not in self.free.held:
                self.free.held.add(b)
                return b
        raise AssertionError("no bank is free")


def program(nc, x, wflat, cfd, ppd, prd, wsd, tbd, seld, out):
    Q = Queues(nc)
    psum = [nc.alloc_psum_tensor(f"bank{i}", [128, 512], F32) for i in range(8)]
    bfree = BankFree()

    def sb(name, shape, dt, kb):
        return nc.alloc_sbuf_tensor_at(name, shape, dt, offset=BASE + int(round(kb * KB)))

    def sem(name):
        return nc.alloc_semaphore(name)

    NS = 4
    RAW = [sb(f"raw{i}", [128, 1024], F32, 4 * i) for i in range(NS)]
    WH = [sb(f"wh{i}", [128, 1024], F32R, 16 + 4 * i) for i in range(NS)]
    WL = [sb(f"wl{i}", [128, 1024], F32R, 32 + 4 * i) for i in range(NS)]
    C0 = 48
    CT = sb("consts", [128, NCF], F32, C0)
    PT_ = sb("pparams", [128, NPP], F32, C0 + 12)
    RT = sb("rparams", [128, NPR], F32, C0 + 13.125)
    NUb = sb("nub", [128, 128], BF16, C0 + 20.25)
    NLb = sb("nlb", [128, 128], BF16, C0 + 20.5)
    IDb = sb("idb", [128, 128], BF16, C0 + 20.75)
    ID2 = sb("id2", [128, 512], BF16, C0 + 21)
    IDR = sb("idr", [128, 128], F32R, C0 + 22)
    CE = sb("ceps", [128, 2], F32, C0 + 22.5)
    small_at = [C0 + 22.625]

    def small(name, cols, shape=None):
        t = sb(name, shape or [128, cols], F32, small_at[0])
        small_at[0] += ((cols * 4 + 31) // 32 * 32) / KB
        assert small_at[0] <= C0 + 28
        return t

    Z0 = C0 + 28

    def zb(name, shape, dt, kb):
        n = 1
        for s in shape[1:]:
            n *= s
        assert kb + n * (2 if dt == BF16 else 4) / KB <= 131.8, name
        return sb(name, shape, dt, Z0 + kb)

    def cf(name, i=0, n=1):
        a, w = CF[name]
        if n == 1 and name != "LM":
            return CT[:, a:a + w]
        return CT[:, a + 128 * i:a + 128 * (i + n)]

    def pp(name, i=0, n=1, parts=128):
        a, _ = PP[name]
        return PT_[0:parts, a + i:a + i + n]

    def pr(name):
        a, w = PR[name]
        return RT[:, a:a + w]

    XH = zb("xh", [128, 8, 512], F32R, 0)
    XL = zb("xl", [128, 8, 512], F32R, 16)
    H = zb("h", [128, 4, 1024], F32, 32)

    s_c = sem("s_const")
    s_p = sem("s_params")
    s_x = [sem(f"s_x{i}") for i in range(4)]
    xv = x.rearrange("b (t p) d -> (b p) t d", p=128)
    for tb in range(4):
        Q.dma("act", H[:, tb, :], xv[:, tb, :], s_x[tb], 16)
    Q.dma("act", CT[:], cfd, s_c, 16)
    Q.dma("act", PT_[:], ppd, s_p, 16)
    Q.dma("act", RT[:], prd.partition_broadcast(128), s_p, 32)
    x_in = [(s_x[tb], 16) for tb in range(4)]
    c_in = (s_c, 16)
    p_in = (s_p, 32)

    plan = unit_plan()
    NU = len(plan)
    s_w = [sem(f"s_w{i}") for i in range(NS)]
    widths = [len(ks) * width for _, ks, _, width in plan]
    starts = [128 * sum(widths[:u]) for u in range(NU)]
    w_read = [None] * NU
    w_split = [None] * NU
    w_used = [None] * NU
    issued = [0, 0]

    def w_load(u):
        src = wflat[starts[u]:starts[u] + 128 * widths[u]].rearrange("(p n) -> p n", p=128)
        Q.dma("sp", RAW[u % NS][:, 0:widths[u]], src, s_w[u % NS], 16 * (u // NS + 1),
              [w_read[u - NS] if u >= NS else None])

    def w_prep(u):
        n = widths[u]
        raw, hi, lo = RAW[u % NS][:, 0:n], WH[u % NS][:, 0:n], WL[u % NS][:, 0:n]
        there = (s_w[u % NS], 16 * (u // NS + 1))
        free = w_used[u - NS] if u >= NS else None
        t = Q.put("act", lambda e: e.activation(hi, raw, ACT.Copy), [there, free])
        t = Q.put("pool", lambda e: e.tensor_tensor(lo, raw, hi.bitcast(F32), ALU.subtract), [there, t, free])
        w_read[u] = w_split[u] = t

    def w_ahead(u):
        while issued[1] <= min(u, NU - 1):
            while issued[0] < min(issued[1] + NS, NU):
                w_load(issued[0])
                issued[0] += 1
            w_prep(issued[1])
            issued[1] += 1
        while issued[0] < min(issued[1] + NS, NU):
            w_load(issued[0])
            issued[0] += 1

    unit = [0]

    def mm(out_, l, r, start, stop, waits=(), inc=False, part=False):
        return Q.put("pe", lambda e: e.matmul(out_, l, r, start=start, stop=stop, skip_group_check=part), waits, inc)

    def tr(out_, in_, waits=(), inc=False):
        idn = cf("ident")[0:in_.shape[0], 0:in_.shape[0]]
        return Q.put("pe", lambda e: e.transpose(out_, in_, idn), list(waits) + [c_in], inc)

    def mm3(o, lh, ll, rh, rl, start, stop, waits=(), inc=False):
        mm(o, lh, rh, start, False, waits)
        mm(o, lh, rl, False, False)
        return mm(o, ll, rh, False, stop, (), inc)

    def dense_ch(bank, x_ready):
        u = unit[0]
        unit[0] += 1
        w_ahead(u + 2)
        w = [w_split[u], bfree[bank]]
        for k in range(8):
            t = mm3(psum[bank][:, :], WH[u % NS][:, k * 128:(k + 1) * 128], WL[u % NS][:, k * 128:(k + 1) * 128],
                    XH[:, k, :], XL[:, k, :], k == 0, k == 7, w + [x_ready[k]], k == 7)
        w_used[u] = t
        return t

    def dense_tok(banks, n, x_ready, evac):
        for k0 in range(0, 8, 2):
            u = unit[0]
            unit[0] += 1
            w_ahead(u + 2)
            for tb in range(4):
                for k in range(2):
                    c = slice(k * n, (k + 1) * n)
                    ts = slice(tb * 128, (tb + 1) * 128)
                    w = [w_split[u], x_ready[k0 + k]] + ([bfree[banks[tb]]] if k0 + k == 0 else [])
                    t = mm3(psum[banks[tb]][:, 0:n], XH[:, k0 + k, ts], XL[:, k0 + k, ts], WH[u % NS][:, c],
                            WL[u % NS][:, c], k0 + k == 0, k0 + k == 7, w, k == 1)
                if k0 == 6:
                    evac(tb, t)
            w_used[u] = t
            yield

    t_ce = Q.put("dve", lambda e: e.memset(CE[:, 0:1], EPS))
    t_ce = Q.put("dve", lambda e: e.memset(CE[:, 1:2], -0.5 * math.log(128.0)))
    eps, lnq = CE[:, 0:1], CE[:, 1:2]
    w_ahead(0)

    SS = [small(f"ss{i}", 4) for i in range(3)]
    RS = [small(f"rs{i}", 4) for i in range(3)]

    def row_rstd(i, tb, src, junk, waits):
        t = Q.put("act", lambda e: e.activation(junk, src, ACT.Square, accum_out=SS[i][:, tb:tb + 1]), waits)
        t = Q.put("act", lambda e: e.activation(RS[i][:, tb:tb + 1], SS[i][:, tb:tb + 1], ACT.Ln, bias=eps,
                                                scale=1.0 / D), [t, t_ce])
        return Q.put("act", lambda e: e.activation(RS[i][:, tb:tb + 1], RS[i][:, tb:tb + 1], ACT.Exp, scale=-0.5), [t])

    def norm_xt(i, gain, XS, ready, free):
        xs = []
        for tb in range(4):
            t = row_rstd(i, tb, H[:, tb, :], XS[:, tb, :], [ready[tb], free])
            xs.append(Q.put("dve", lambda e, tb=tb: e.tensor_scalar(XS[:, tb, :], H[:, tb, :], RS[i][:, tb:tb + 1], None,
                                                                    ALU.mult), [t]))
        return split_t(XS, xs, gain)

    x_pe = [None]

    def split_t(src, ready, gain):
        done = []
        free = x_pe[0]
        for k in range(8):
            b = G.take()
            for tb in range(4):
                t = tr(psum[b][:, tb * 128:(tb + 1) * 128], src[:, tb, k * 128:(k + 1) * 128],
                       [ready[tb], bfree[b]], tb == 3)
            s = pp(gain, k) if gain else 1.0
            t1 = Q.put("act", lambda e, b=b, k=k, s=s: e.activation(XH[:, k, :], psum[b][:, :], ACT.Copy, scale=s),
                       [t, free, p_in])
            t2 = Q.put("dve", lambda e, b=b, k=k, s=s: e.scalar_tensor_tensor(
                XL[:, k, :], psum[b][:, :], s, XH[:, k, :].bitcast(F32), ALU.mult, ALU.subtract), [t, t1, free, p_in])
            bfree[b] = t2
            done.append(t2)
        return done

    G = Banks(bfree, range(8))

    XS1 = zb("xs1", [128, 4, 1024], F32, 88)
    QK = zb("qk", [128, 8, 512], F32, 48)
    VC = zb("vc", [128, 4, 512], F32, 64)
    KT = zb("kt", [128, 4, 512], F32, 72)
    VT = zb("vt", [128, 4, 512], F32, 80)
    MIX = zb("mix", [128, 4, 1024], F32, 88)
    SWR = zb("swr", [128, 4, 640], F32, 104)
    SV = zb("sv", [128, 4, 128], F32, 114)
    SQ = [zb(f"sq{i}", [128, 512], F32, 116 + 2 * i) for i in range(3)]
    R1 = zb("r1", [128, 640], F32, 122)
    R2 = zb("r2", [128, 640], F32, 124.5)
    SKT = zb("skt", [128, 512], F32, 127)
    SQT = zb("sqt", [128, 4, 512], F32, 64)
    BD = small("bd", 64, [128, 4, 16])

    x_ready = norm_xt(0, "norm_w", XS1, x_in, None)
    t_nu = Q.put("dve", lambda e: e.tensor_scalar(NUb[:], cf("SU"), NEG, None, ALU.mult), [c_in])
    t_nl = Q.put("dve", lambda e: e.tensor_scalar(NLb[:], cf("SL"), NEG, None, ALU.mult))
    t_id = Q.put("dve", lambda e: e.tensor_copy(IDb[:], cf("ident")))
    for h in range(4):
        t_id = Q.put("dve", lambda e, h=h: e.tensor_scalar(ID2[:, h * 128:(h + 1) * 128], cf("ident"), 2.0, None, ALU.mult))
    t_id = Q.put("dve", lambda e: e.tensor_copy(IDR[:], cf("ident")))

    def conv5(j, dst, bank, t):
        wc = lambda i: pp("dn_conv_w", j * 5 + i)
        t = Q.put("act", lambda e: e.activation(dst, psum[bank][:, :], ACT.Copy, scale=wc(2)), [t, p_in])
        for i in (0, 1, 3, 4):
            a, b = max(0, 2 - i), min(T, T + 2 - i)
            sh = i - 2
            t = Q.put("dve", lambda e, i=i, a=a, b=b, sh=sh: e.scalar_tensor_tensor(
                dst[:, a:b], psum[bank][:, a + sh:b + sh], wc(i), dst[:, a:b], ALU.mult, ALU.add), [t, p_in])
        bfree[bank] = t
        return Q.put("act", lambda e: e.activation(dst, dst, ACT.Silu), [t])

    t_conv = [None] * 12
    pend = None
    for j in range(12):
        b = G.take()
        t = dense_ch(b, x_ready)
        if pend:
            pj, pb, pt = pend
            t_conv[pj] = conv5(pj, QK[:, pj, :] if pj < 8 else VC[:, pj - 8, :], pb, pt)
        pend = (j, b, t)
    pj, pb, pt = pend
    t_conv[pj] = conv5(pj, VC[:, pj - 8, :], pb, pt)

    t_qk = [None] * 8
    sq_free = [None] * 3

    def qk_norm():
        for j in range(8):
            s = SQ[j % 3]
            t = Q.put("act", lambda e, j=j, s=s: e.activation(s[:], QK[:, j, :], ACT.Square), [t_conv[j], sq_free[j % 3]])
            b = G.take()
            t = mm(psum[b][:, :], cf("ones"), s[:], True, True, [t, bfree[b], c_in], True)
            yield
            t = Q.put("act", lambda e, b=b, s=s: e.activation(s[:], psum[b][:, :], ACT.Ln, bias=eps), [t, t_ce])
            bfree[b] = t
            bias = lnq if j < 4 else 0.0
            t = Q.put("act", lambda e, s=s, bias=bias: e.activation(s[:], s[:], ACT.Exp, scale=-0.5, bias=bias), [t])
            t_qk[j] = sq_free[j % 3] = Q.put(
                "dve", lambda e, j=j, s=s: e.tensor_tensor(QK[:, j, :], QK[:, j, :], s[:], ALU.mult), [t])
            yield

    t_kt = [None] * 4
    t_vt = [None] * 4

    def to_tokens():
        for dst, srcs, ready, done in ((VT, VC, t_conv[8:12], t_vt), (KT, QK, None, t_kt)):
            for cb in range(4):
                b = G.take()
                for h in range(4):
                    src = srcs[:, h, cb * 128:(cb + 1) * 128] if ready else srcs[:, 4 + h, cb * 128:(cb + 1) * 128]
                    r = ready[h] if ready else t_qk[4 + h]
                    t = tr(psum[b][:, h * 128:(h + 1) * 128], src, [r, bfree[b]], h == 3)
                done[cb] = bfree[b] = Q.put("act", lambda e, b=b, cb=cb, dst=dst: e.activation(
                    dst[:, cb, :], psum[b][:, :], ACT.Copy), [t])
                yield

    g4 = lambda name: small(name, 32, [128, 2, 4, 4])
    BETA, NBETA, GG, SPA, SPB, GC, GL, EG, EGL, EL, BEG = (g4(n) for n in (
        "beta", "nbeta", "gg", "spa", "spb", "gc", "gl", "eg", "egl", "el", "beg"))
    EA = small("ea", 8)
    NSINK = small("nsink", 8)
    t_gate = [None]

    def gates(t_bd):
        dch = lambda ap: ap.rearrange("p c (d h) -> p d c h", d=2)
        bl, dl = dch(BD[:, :, 0:8]), dch(BD[:, :, 8:16])
        row = lambda ap: ap.rearrange("p (d h) -> p d h", d=2).unsqueeze(2).broadcast_to([128, 2, 4, 4])
        t = Q.put("act", lambda e: e.activation(EA[:], pr("dn_a_log"), ACT.Exp), [p_in])
        for d in range(2):
            t = Q.put("act", lambda e, d=d: e.activation(BETA[:, d], bl[:, d], ACT.Exp, scale=-1.0), t_bd)
        t = Q.put("dve", lambda e: e.tensor_scalar(BETA[:], BETA[:], 1.0, None, ALU.add), [t])
        t = Q.put("dve", lambda e: e.reciprocal(BETA[:], BETA[:]), [t])
        t = Q.put("dve", lambda e: e.tensor_scalar(NBETA[:], BETA[:], -1.0, None, ALU.mult), [t])
        for d in range(2):
            rb = pr("dn_dt_bias")[:, 4 * d:4 * d + 4].unsqueeze(1).broadcast_to([128, 4, 4])
            t = Q.put("dve", lambda e, d=d, rb=rb: e.tensor_tensor(SPA[:, d], dl[:, d], rb, ALU.add), [p_in] + t_bd)
        t = Q.put("dve", lambda e: e.scalar_tensor_tensor(SPB[:], SPA[:], -1.0, SPA[:], ALU.mult, ALU.max), [t])
        t1 = Q.put("dve", lambda e: e.tensor_scalar(SPA[:], SPA[:], 0.0, None, ALU.max), [t])
        t = Q.put("act", lambda e: e.activation(SPB[:], SPB[:], ACT.Exp, scale=-1.0), [t])
        t = Q.put("act", lambda e: e.activation(SPB[:], SPB[:], ACT.Ln, bias=1.0), [t])
        t = Q.put("dve", lambda e: e.tensor_tensor(SPA[:], SPA[:], SPB[:], ALU.add), [t, t1])
        for d in range(2):
            ea = EA[:, 4 * d:4 * d + 4].unsqueeze(1).broadcast_to([128, 4, 4])
            t1 = Q.put("dve", lambda e, d=d, ea=ea: e.scalar_tensor_tensor(GG[:, d], SPA[:, d], -1.0, ea, ALU.mult, ALU.mult), [t])
        yield
        b = G.take()
        fl = lambda ap: ap.rearrange("p c h -> p (c h)")
        mm(psum[b][:, 0:16], cf("triU"), fl(GG[:, 0]), True, True, [t1, bfree[b], c_in])
        mm(psum[b][:, 16:32], cf("triL"), fl(GG[:, 1]), True, True)
        t = mm(psum[b][:, 32:64], cf("ones"), GG[:].rearrange("p d c h -> p (d c h)"), True, True, (), True)
        f3 = lambda t_: t_[:].rearrange("p d c h -> p (d c h)")
        t = Q.put("dve", lambda e: e.tensor_copy(f3(GC), psum[b][:, 0:32]), [t])
        t = Q.put("dve", lambda e: e.tensor_copy(f3(GL), psum[b][:, 32:64]), [t])
        bfree[b] = t
        t1 = Q.put("dve", lambda e: e.tensor_tensor(EGL[:], GL[:], GC[:], ALU.subtract), [t])
        t = Q.put("act", lambda e: e.activation(EG[:], GC[:], ACT.Exp), [t])
        t2 = Q.put("act", lambda e: e.activation(EL[:], GL[:], ACT.Exp), [t])
        t2 = Q.put("act", lambda e: e.activation(EGL[:], EGL[:], ACT.Exp), [t1])
        t = Q.put("dve", lambda e: e.tensor_tensor(BEG[:], BETA[:], EG[:], ALU.mult), [t])
        t_gate[0] = [t, t2]
        yield

    SSQ = small("ssq", 40, [128, 4, 10])
    t_swt = [None] * 4

    def swa_prep(t_swr):
        rows = SWR[:].rearrange("p t (h d) -> p t h d", d=64)
        r1 = R1[:].rearrange("p (h d) -> p h d", d=64)
        r2 = R2[:].rearrange("p (h d) -> p h d", d=64)
        tl = None
        tw = [None] * 4
        for tb in range(4):
            t = Q.put("pool", lambda e, tb=tb: e.tensor_tensor(R1[:], SWR[:, tb, :], SWR[:, tb, :], ALU.mult), t_swr[tb] + [tl])
            tl = Q.put("dve", lambda e, tb=tb: e.tensor_reduce(SSQ[:, tb, :], r1, AX.X, ALU.add), [t])
            yield
        t = Q.put("act", lambda e: e.activation(SSQ[:], SSQ[:], ACT.Ln, bias=eps, scale=1.0 / 64), [tl, t_ce])
        t_ss = Q.put("act", lambda e: e.activation(SSQ[:], SSQ[:], ACT.Exp, scale=-0.5), [t])
        t_r1 = tl
        t_r2 = None
        for tb in range(4):
            cs = cf("cos")[:, tb * 64:(tb + 1) * 64]
            sn = cf("sin")[:, tb * 64:(tb + 1) * 64]
            bc = lambda ap, n: ap.unsqueeze(1).broadcast_to([128, n, 64])
            rs = SSQ[:, tb, :].unsqueeze(2).broadcast_to([128, 10, 64])
            t = Q.put("dve", lambda e, tb=tb, rs=rs: e.tensor_tensor(rows[:, tb], rows[:, tb], rs, ALU.mult), [t_ss])
            tk = Q.put("pool", lambda e, tb=tb, bc=bc: e.tensor_tensor(
                rows[:, tb, 0:2], rows[:, tb, 0:2], bc(pr("swa_k_norm_w"), 2), ALU.mult), [t, p_in])
            t = Q.put("pool", lambda e, tb=tb, bc=bc: e.tensor_tensor(
                rows[:, tb, 2:10], rows[:, tb, 2:10], bc(pr("swa_q_norm_w"), 8), ALU.mult), [t, p_in])
            yield
            t1 = Q.put("dve", lambda e, tb=tb, bc=bc, cs=cs: e.tensor_tensor(r1, rows[:, tb], bc(cs, 10), ALU.mult),
                       [t, tk, t_r1, c_in])
            for o, i in ((0, 32), (32, 0)):
                s = sn[:, o:o + 32].unsqueeze(1).broadcast_to([128, 10, 32])
                t2 = Q.put("dve", lambda e, tb=tb, o=o, i=i, s=s: e.tensor_tensor(
                    r2[:, :, o:o + 32], rows[:, tb, :, i:i + 32], s, ALU.mult), [t, tk, t_r2, c_in])
            t3 = Q.put("dve", lambda e, tb=tb: e.tensor_tensor(rows[:, tb, 0:2], r1[:, 0:2], r2[:, 0:2], ALU.add), [t1, t2])
            qo = rows[:, tb, 2:10].rearrange("p (i g) d -> p g i d", g=2)
            qa = r1[:, 2:10].rearrange("p (g i) d -> p g i d", g=2)
            qb_ = r2[:, 2:10].rearrange("p (g i) d -> p g i d", g=2)
            t_r1 = t_r2 = tw[tb] = Q.put("dve", lambda e, qo=qo, qa=qa, qb_=qb_: e.tensor_tensor(qo, qa, qb_, ALU.add), [t1, t2])
            yield
        for i in range(5):
            b = G.take()
            for tb in range(4):
                src = SWR[:, tb, 0:128] if i == 4 else SWR[:, tb, 128 + i * 128:256 + i * 128]
                t = tr(psum[b][:, tb * 128:(tb + 1) * 128], src, [tw[tb], bfree[b]], tb == 3)
            dst = SKT[:] if i == 4 else SQT[:, i, :]
            t_swt[0] = bfree[b] = Q.put("act", lambda e, b=b, dst=dst: e.activation(dst, psum[b][:, :], ACT.Copy), [t] + t_vt)
            yield

    t_bd = [None] * 4
    t_k = [None] * 4
    t_swr = [None] * 4
    t_sv = [None] * 4
    t_z = [None] * 4
    t_sz = [None] * 4

    def evac_first(banks):
        def f(tb, t):
            b = banks[tb]
            t = Q.put("act", lambda e: e.activation(BD[:, tb, :], psum[b][:, 0:16], ACT.Copy), [t])
            t_bd[tb] = t
            t_k[tb] = Q.put("act", lambda e: e.activation(SWR[:, tb, 0:128], psum[b][:, 16:144], ACT.Copy))
            bfree[b] = t_sv[tb] = Q.put("act", lambda e: e.activation(SV[:, tb, :], psum[b][:, 144:272], ACT.Copy))
        return f

    def evac_to(banks, dst, func, done):
        def f(tb, t):
            b = banks[tb]
            done[tb] = bfree[b] = Q.put("act", lambda e: e.activation(dst(tb), psum[b][:, :], func), [t])
        return f

    def step(g, n=1):
        for _ in range(n):
            if next(g, "end") == "end":
                return False
        return True

    def four():
        return [G.take() for _ in range(4)]

    bk = [0, 1, 2, 3]
    G = Banks(bfree, (4, 5, 6, 7))
    g1 = qk_norm()
    step(g1, 1)
    for _ in dense_tok(bk, 272, x_ready, evac_first(bk)):
        step(g1, 4)
    g2 = gates(t_bd)
    for _ in dense_tok(bk, 512, x_ready, evac_to(bk, lambda tb: SWR[:, tb, 128:640], ACT.Copy, t_swr)):
        step(g1, 2)
        step(g2, 1)
    while step(g1):
        pass
    while step(g2):
        pass
    g1 = to_tokens()
    g2 = swa_prep([[a, b_] for a, b_ in zip(t_k, t_swr)])
    for _ in dense_tok(bk, 512, x_ready, evac_to(bk, lambda tb: MIX[:, tb, 512:1024], ACT.Silu, t_sz)):
        step(g1, 2)
        step(g2, 2)
    for _ in dense_tok(bk, 512, x_ready, evac_to(bk, lambda tb: MIX[:, tb, 0:512], ACT.Silu, t_z)):
        step(g1, 2)
        step(g2, 3)
    while step(g1):
        pass
    while step(g2):
        pass
    x_pe[0] = w_used[unit[0] - 1]

    DNB = []
    for i in range(2):
        o = 22 * i
        n = lambda s, i=i: f"{s}{i}"
        DNB.append(dict(
            MP=zb(n("mp"), [128, 512], F32, o), TT=zb(n("tt"), [128, 512], F32, o),
            MR=zb(n("mr"), [128, 512], F32R, o + 2), GN=zb(n("gn"), [128, 512], F32, o + 2),
            DD=zb(n("dd"), [128, 512], F32R, o + 4), TG=zb(n("tg"), [128, 512], F32, o + 4),
            DT=zb(n("dt"), [128, 512], F32R, o + 6), ER=zb(n("er"), [128, 512], F32, o + 6),
            XN=zb(n("xn"), [128, 512], F32R, o + 8), EE=zb(n("ee"), [128, 512], F32, o + 8),
            AT=zb(n("at"), [128, 512], F32, o + 10), QG=zb(n("qg"), [128, 4, 128], F32, o + 12),
            VB=zb(n("vb"), [128, 512], F32, o + 14), KB_=zb(n("kb"), [128, 512], F32, o + 16),
            VN=zb(n("vn"), [128, 512], F32, o + 16), KD=zb(n("kd"), [128, 512], F32, o + 18),
            NW=zb(n("nw"), [128, 512], F32, o + 20), S=zb(n("s"), [128, 512], F32, 44 + 2 * i)))
    O = zb("o", [128, 4, 512], F32, 104)
    PM = [zb(f"pm{i}", [128, 384], F32, 116 + 1.5 * i) for i in range(2)]
    PMT = [zb(f"pmt{i}", [128, 384], F32, 119 + 1.5 * i) for i in range(2)]
    SWO = zb("swo", [128, 512], F32, 122)
    OT = zb("ot", [128, 512], F32, 124)
    RO = small("ro", 16, [128, 4, 4])
    BI = BS = Banks(bfree, (0, 1, 2, 3, 4))
    BA = (5, 6, 7)
    hs = lambda t_, h: t_[:, h * 128:(h + 1) * 128]
    v3 = lambda t_: t_[:].rearrange("p (h n) -> p h n", h=4)
    bc4 = lambda ap: ap.unsqueeze(1).broadcast_to([128, 4, 128])
    b4r = lambda ap: ap.unsqueeze(2).broadcast_to([128, 4, 128])
    dn_free = [x_pe[0], x_pe[0]]
    s_tok = [None, None]
    o_tok = [None] * 4

    def dn_unit(d, r):
        cb = r if d == 0 else 3 - r
        W = DNB[d]
        fr = dn_free[d]
        cs = slice(cb * 128, (cb + 1) * 128)
        kT = lambda h: QK[:, 4 + h, cs]
        qT = lambda h: QK[:, h, cs]
        col = lambda t_, h: t_[:, d, cb, h:h + 1]
        gate = t_gate[0]
        tri = cf("triU" if d == 0 else "triL")
        for h in range(4):
            t = Q.put("dve", lambda e, h=h: e.tensor_scalar(hs(W["TG"], h), tri, col(GG, h), None, ALU.mult), [fr] + gate + [c_in])
        b = BI.take()
        t = mm(psum[b][:, :], cf("ones"), W["TG"][:], True, True, [t, bfree[b]], True)
        b2 = BI.take()
        for h in range(4):
            tk = mm(hs(psum[b2], h), kT(h), kT(h), True, True, [t_qk[4 + h], bfree[b2]], h == 3)
        yield
        t1 = Q.put("act", lambda e, b=b: e.activation(W["ER"][:], psum[b][:, :], ACT.Exp), [t, fr])
        for h in range(4):
            t2 = Q.put("dve", lambda e, h=h, b=b: e.tensor_scalar(hs(W["EE"], h), hs(psum[b], h), col(GC, h), 0.0,
                                                             ALU.subtract, ALU.max), [t1, fr])
        bfree[b] = t2
        te = Q.put("act", lambda e: e.activation(W["EE"][:], W["EE"][:], ACT.Exp, scale=-1.0), [t2])
        tq = Q.put("pool", lambda e: e.tensor_tensor(W["QG"][:], QK[:, 0:4, cs], v3(W["ER"]), ALU.mult), [t1] + t_qk[0:4])
        sl = cf("SL" if d == 0 else "SU")
        tk = Q.put("dve", lambda e, b2=b2: e.tensor_tensor(v3(W["MP"]), v3(psum[b2]), bc4(sl), ALU.mult), [tk, fr])
        bfree[b2] = tk
        yield
        for h in range(4):
            t = Q.put("dve", lambda e, h=h: e.scalar_tensor_tensor(hs(W["MP"], h), hs(W["MP"], h), col(NBETA, h),
                                                                   hs(W["EE"], h), ALU.mult, ALU.mult), [te, tk])
        tm = Q.put("pool", lambda e: e.tensor_tensor(v3(W["MP"]), v3(W["MP"]), bc4(cf("ident")), ALU.add), [t])
        tr_ = Q.put("act", lambda e: e.activation(W["MR"][:], W["MP"][:], ACT.Copy), [tm])
        b = BI.take()
        for h in range(4):
            ta = mm(hs(psum[b], h), kT(h), qT(h), True, True, [t_qk[4 + h], t_qk[h], bfree[b]], h == 3)
        b2 = BI.take()
        for h in range(4):
            tt = tr(hs(psum[b2], h), hs(W["EE"], h), [te, bfree[b2]], h == 3)
        tri_a = tri
        ta = Q.put("dve", lambda e, b=b: e.tensor_tensor(v3(W["AT"]), v3(psum[b]), bc4(tri_a), ALU.mult), [ta])
        bfree[b] = ta
        ta = Q.put("dve", lambda e, b2=b2: e.tensor_tensor(W["AT"][:], W["AT"][:], psum[b2][:, :], ALU.mult), [ta, tt])
        bfree[b2] = ta
        bt = b4r(BETA[:, d, cb, :])
        tvb = Q.put("pool", lambda e: e.tensor_tensor(v3(W["VB"]), VT[:, cb, :].rearrange("p (h n) -> p h n", h=4), bt, ALU.mult),
                    [t_vt[cb], fr] + gate)
        k3 = KT[:, cb, :].rearrange("p (h n) -> p h n", h=4)
        tkb = Q.put("pool", lambda e: e.tensor_tensor(v3(W["KB_"]), k3, b4r(BEG[:, d, cb, :]), ALU.mult), [t_kt[cb]])
        tkd = Q.put("pool", lambda e: e.tensor_tensor(v3(W["KD"]), k3, b4r(EGL[:, d, cb, :]), ALU.mult))
        yield
        td = tdt = None
        for lvl in range(7):
            b = BI.take()
            for h in range(4):
                t = mm(hs(psum[b], h), hs(W["MR"], h), hs(W["DT"], h) if lvl else IDR[:], True, True,
                       [tr_, tdt, bfree[b], t_id], h == 3)
            yield
            lm = cf("LM", 7 * d + lvl)
            t = Q.put("dve", lambda e, b=b, lm=lm: e.tensor_tensor(v3(W["XN"]), v3(psum[b]), bc4(lm), ALU.mult), [t, ta])
            bfree[b] = t
            b1, b2 = BI.take(), BI.take()
            for h in range(4):
                t1 = mm(hs(psum[b1], h), hs(W["DD"], h) if lvl else IDR[:], hs(W["XN"], h), True, True,
                        [t, td, bfree[b1]], h == 3)
            for h in range(4):
                t2 = mm(hs(psum[b2], h), hs(W["XN"], h), hs(W["DD"], h) if lvl else IDR[:], True, True,
                        [bfree[b2]], h == 3)
            tdt = bfree[b1] = Q.put("act", lambda e, b1=b1: e.activation(W["DT"][:], psum[b1][:, :], ACT.Copy), [t1, tq])
            td = bfree[b2] = Q.put("dve", lambda e, b2=b2: e.tensor_copy(W["DD"][:], psum[b2][:, :]), [t2])
            yield
        dt32, dd32 = W["DT"][:].bitcast(F32), W["DD"][:].bitcast(F32)
        b = BI.take()
        for h in range(4):
            t = mm(hs(psum[b], h), hs(W["MP"], h), hs(dt32, h), True, False, [tm, tdt, bfree[b]])
            t = mm(hs(psum[b], h), IDb[:], hs(ID2, h), False, True, [t_id], h == 3)
        yield
        t = Q.put("dve", lambda e, b=b: e.scalar_tensor_tensor(W["GN"][:], dt32, -2.0, psum[b][:, :], ALU.mult, ALU.add), [t, tdt])
        bfree[b] = t
        b = BI.take()
        for h in range(4):
            t1 = mm(hs(psum[b], h), hs(dd32, h), hs(W["GN"], h), True, True, [t, td, bfree[b]], h == 3)
        ti = bfree[b] = Q.put("act", lambda e, b=b: e.activation(W["TT"][:], psum[b][:, :], ACT.Copy), [t1])
        yield
        ts = s_tok[d]
        if r:
            b = BS.take()
            for h in range(4):
                t = mm(hs(psum[b], h), hs(W["KB_"], h), hs(W["TT"], h), True, True, [ti, tkb, bfree[b]], h == 3)
            tw = bfree[b] = Q.put("act", lambda e, b=b: e.activation(W["NW"][:], psum[b][:, :], ACT.Copy, scale=-1.0), [t])
        yield
        b = BS.take()
        for h in range(4):
            t = mm(hs(psum[b], h), hs(W["TT"], h), hs(W["VB"], h), True, r == 0, [ti, tvb, bfree[b]], h == 3)
            if r:
                t = mm(hs(psum[b], h), hs(W["NW"], h), hs(W["S"], h), False, True, [tw, ts], h == 3)
        tv = bfree[b] = Q.put("act", lambda e, b=b: e.activation(W["VN"][:], psum[b][:, :], ACT.Copy), [t, tkb])
        yield
        b = BS.take()
        for h in range(4):
            if r:
                mm(hs(psum[b], h), W["QG"][:, h, :], hs(W["S"], h), True, False, [tq, ts, bfree[b]])
            t = mm(hs(psum[b], h), hs(W["AT"], h), hs(W["VN"], h), r == 0, True, [ta, tv, bfree[b]], h == 3)
        last = t
        if o_tok[cb] is None:
            o_tok[cb] = bfree[b] = Q.put("act", lambda e, b=b: e.activation(O[:, cb, :], psum[b][:, :], ACT.Copy), [t])
        else:
            o_tok[cb] = bfree[b] = Q.put("dve", lambda e, b=b: e.tensor_tensor(O[:, cb, :], O[:, cb, :], psum[b][:, :], ALU.add),
                                         [t, o_tok[cb]])
        yield
        if r < 3:
            b = BS.take()
            for h in range(4):
                t = mm(hs(psum[b], h), hs(W["KD"], h), hs(W["VN"], h), True, True, [tkd, tv, bfree[b]], h == 3)
            last = t
            for h in range(4):
                if r:
                    t = Q.put("dve", lambda e, b=b, h=h: e.scalar_tensor_tensor(
                        hs(W["S"], h), hs(W["S"], h), col(EL, h), hs(psum[b], h), ALU.mult, ALU.add), [t, ts])
                else:
                    t = Q.put("dve", lambda e, b=b, h=h: e.tensor_copy(hs(W["S"], h), hs(psum[b], h)), [t, fr])
            s_tok[d] = bfree[b] = t
        dn_free[d] = last
        yield

    t_mix = [[None, None] for _ in range(4)]
    ot_free = [None]

    def dn_post(cb):
        o3 = O[:, cb, :].rearrange("p (h n) -> p h n", h=4)
        t = Q.put("pool", lambda e: e.tensor_tensor(OT[:], O[:, cb, :], O[:, cb, :], ALU.mult), [o_tok[cb], ot_free[0]])
        ot_free[0] = t = Q.put("dve", lambda e: e.tensor_reduce(RO[:, cb, :], v3(OT), AX.X, ALU.add), [t])
        t = Q.put("act", lambda e: e.activation(RO[:, cb, :], RO[:, cb, :], ACT.Ln, bias=eps, scale=1.0 / 128), [t])
        t = Q.put("act", lambda e: e.activation(RO[:, cb, :], RO[:, cb, :], ACT.Exp, scale=-0.5), [t])
        t = Q.put("dve", lambda e: e.tensor_tensor(o3, o3, b4r(RO[:, cb, :]), ALU.mult), [t])
        t = Q.put("pool", lambda e: e.tensor_tensor(o3, o3, bc4(pr("dn_out_norm_w")), ALU.mult), [t])
        t_mix[cb][0] = Q.put("dve", lambda e: e.tensor_tensor(MIX[:, cb, 0:512], MIX[:, cb, 0:512], O[:, cb, :], ALU.mult),
                             [t, t_z[cb]])

    MX = small("mx", 32, [128, 4, 8])
    DEN = small("den", 32, [128, 4, 8])
    ES = small("es", 32, [128, 4, 8])
    t_ns = Q.put("dve", lambda e: e.tensor_scalar(NSINK[:], pr("swa_sinks"), -1.0, None, ALU.mult), [p_in])

    def swa():
        bs, bt, bo = BA
        pieces = [(qb, h) for qb in range(4) for h in range(8)]
        st = [dict() for _ in pieces]
        pm_free, pmt_free = [None, None], [None, None]
        swo_free = [None]
        for n in range(len(pieces) + 2):
            if n < len(pieces):
                qb, h = pieces[n]
                g, i = h // 4, h % 4
                k0, k1 = max(qb - 1, 0), min(qb + 1, 3)
                nk = (k1 - k0 + 1) * 128
                ps = slice(64 * g, 64 * g + 64)
                masks = ([(0, NLb)] if qb > 0 else []) + ([(nk - 128, NUb)] if qb < 3 else [])
                mm(psum[bs][:, 0:nk], SQT[ps, i, qb * 128:(qb + 1) * 128], SKT[ps, k0 * 128:(k1 + 1) * 128], True, True,
                   [t_swt[0], bfree[bs]])
                for m, (at, mask) in enumerate(masks):
                    t = mm(psum[bs][:, at:at + 128], IDb[:], mask[:], False, True, [t_id, t_nl], m == len(masks) - 1, True)
                mx = MX[:, qb, h:h + 1]
                t = Q.put("dve", lambda e, nk=nk, mx=mx: e.tensor_reduce(mx, psum[bs][:, 0:nk], AX.X, ALU.max, negate=True), [t])
                t = Q.put("dve", lambda e, mx=mx, h=h: e.tensor_scalar(mx, mx, 0.125, NSINK[:, h:h + 1], ALU.mult, ALU.min), [t, t_ns])
                pm = PM[n % 2]
                t = bfree[bs] = Q.put("act", lambda e, nk=nk, mx=mx, pm=pm, qb=qb, h=h: e.activation(
                    pm[:, 0:nk], psum[bs][:, 0:nk], ACT.Exp, bias=mx, scale=0.125, accum_out=DEN[:, qb, h:h + 1]),
                    [t, pm_free[n % 2]])
                st[n].update(nk=nk, k0=k0, k1=k1, g=g, t=t)
                yield
            if 0 <= n - 1 < len(pieces):
                m = n - 1
                s = st[m]
                for k in range(s["nk"] // 128):
                    t = tr(psum[bt][:, k * 128:(k + 1) * 128], PM[m % 2][:, k * 128:(k + 1) * 128], [s["t"], bfree[bt]],
                           k == s["nk"] // 128 - 1)
                pm_free[m % 2] = t
                pt = PMT[m % 2]
                nk = s["nk"]
                if m % 2:
                    t = Q.put("act", lambda e, pt=pt, nk=nk: e.activation(pt[:, 0:nk], psum[bt][:, 0:nk], ACT.Copy), [t, pmt_free[m % 2]])
                else:
                    t = Q.put("dve", lambda e, pt=pt, nk=nk: e.tensor_copy(pt[:, 0:nk], psum[bt][:, 0:nk]), [t, pmt_free[m % 2]])
                s["tt"] = bfree[bt] = t
                yield
            if 0 <= n - 2 < len(pieces):
                m = n - 2
                s = st[m]
                qb, h = pieces[m]
                kn = s["k1"] - s["k0"] + 1
                for k in range(kn):
                    t = mm(psum[bo][:, h * 64:(h + 1) * 64], PMT[m % 2][:, k * 128:(k + 1) * 128],
                           SV[:, s["k0"] + k, s["g"] * 64:s["g"] * 64 + 64], k == 0, k == kn - 1,
                           [s["tt"], bfree[bo]] + t_sv, k == kn - 1)
                pmt_free[m % 2] = t
                if h == 7:
                    t1 = Q.put("dve", lambda e, qb=qb: e.tensor_tensor(ES[:, qb, :], pr("swa_sinks"), MX[:, qb, :], ALU.add), [t_ns])
                    t1 = Q.put("act", lambda e, qb=qb: e.activation(ES[:, qb, :], ES[:, qb, :], ACT.Exp), [t1])
                    t1 = Q.put("dve", lambda e, qb=qb: e.tensor_tensor(DEN[:, qb, :], DEN[:, qb, :], ES[:, qb, :], ALU.add), [t1])
                    t1 = Q.put("dve", lambda e, qb=qb: e.reciprocal(DEN[:, qb, :], DEN[:, qb, :]), [t1])
                    rd = DEN[:, qb, :].unsqueeze(2).broadcast_to([128, 8, 64])
                    o8 = lambda ap: ap.rearrange("p (h n) -> p h n", h=8)
                    t = bfree[bo] = Q.put("dve", lambda e, rd=rd: e.tensor_tensor(o8(SWO[:]), o8(psum[bo][:, :]), rd, ALU.mult),
                                          [t, t1, swo_free[0]])
                    swo_free[0] = t_mix[qb][1] = Q.put("pool", lambda e, qb=qb: e.tensor_tensor(
                        MIX[:, qb, 512:1024], MIX[:, qb, 512:1024], SWO[:], ALU.mult), [t, t_sz[qb]])
                yield

    gs = swa()
    for r in range(4):
        ga, gb = dn_unit(0, r), dn_unit(1, r)
        live = True
        while live:
            la = step(ga)
            step(gs)
            lb = step(gb)
            live = la or lb
        if r >= 2:
            dn_post(3 - r)
            dn_post(r)
    while step(gs):
        pass
    t_dn = [dn_free[0], dn_free[1]]
    x_pe[0] = t_dn[1] if t_dn[1][1] > t_dn[0][1] else t_dn[0]

    s_x2 = sem("s_xagain")
    t_h = Q.dma("act", H[:], xv, s_x2, 16, [x_pe[0], s_tok[0], s_tok[1]])
    s_b2 = sem("s_b2")
    WS = zb("ws", [128, 8, 128], F32, 104)
    TB = zb("tb", [128, 896], F32, 108)
    SELF = zb("self", [96, 1024], F32, 112)
    SEL = zb("sel", [96, 8, 128], BF16, 116)
    done1 = [t for m in t_mix for t in m]
    Q.dma("act", WS[:], wsd, s_b2, 16, done1)
    Q.dma("act", TB[:], tbd, s_b2, 32)
    b2_in = Q.dma("act", SELF[:], seld, s_b2, 48)

    def split_mix(src, ready):
        done = []
        for k in range(8):
            b = G.take()
            for tb in range(4):
                t = tr(psum[b][:, tb * 128:(tb + 1) * 128], src[:, tb, k * 128:(k + 1) * 128],
                       [ready[tb][0 if k < 4 else 1], bfree[b]], tb == 3)
            t1 = Q.put("act", lambda e, b=b, k=k: e.activation(XH[:, k, :], psum[b][:, :], ACT.Copy), [t, x_pe[0]])
            t2 = bfree[b] = Q.put("dve", lambda e, b=b, k=k: e.tensor_tensor(
                XL[:, k, :], psum[b][:, :], XH[:, k, :].bitcast(F32), ALU.subtract), [t, t1, x_pe[0]])
            done.append(t2)
        return done

    def add_h(banks, n, done, wait):
        def f(tb, t):
            b = banks[tb]
            hv = H[:, tb, n * 512:(n + 1) * 512]
            done[tb] = bfree[b] = Q.put("dve", lambda e: e.tensor_tensor(hv, hv, psum[b][:, :], ALU.add), [t, wait])
        return f

    def out_proj(ready, wait):
        done = [None] * 4
        for n in range(2):
            bk = four()
            for _ in dense_tok(bk, 512, ready, add_h(bk, n, done, wait)):
                pass
        x_pe[0] = w_used[unit[0] - 1]
        return done

    G = Banks(bfree, range(8))
    ready = split_mix(MIX, t_mix)
    h_tok = out_proj(ready, t_h)

    XS2 = zb("xs2", [128, 4, 1024], F32, 48)
    QK2 = zb("qk2", [128, 8, 512], F32, 48)
    V2 = zb("v2", [128, 4, 512], F32, 64)
    U2 = zb("u2", [128, 4, 512], F32, 72)
    VG = zb("vg", [128, 4, 512], F32, 80)
    MIX2 = zb("mix2", [128, 4, 1024], F32, 88)
    WST = WS
    LF = zb("lf", [8, 512], F32, 118)
    LG = zb("lg", [8, 512], F32, 120)
    VSQ = zb("vsq", [128, 512], F32, 118)
    C3 = zb("c3", [96, 512], BF16, 122)
    P2 = [zb(f"p2{i}", [128, 512], F32, 123 + 2 * i) for i in range(2)]
    P2T = [zb(f"p2t{i}", [128, 512], F32, 127 + 2 * i) for i in range(2)]
    LT = small("lt", 32, [128, 4, 8])

    x_ready = norm_xt(1, "norm_mix_g_2", XS2, h_tok, None)
    t_sel = Q.put("dve", lambda e: e.tensor_copy(SEL[:].rearrange("p h n -> p (h n)"), SELF[:]), [b2_in])
    t_c3 = Q.put("dve", lambda e: e.memset(C3[:], 0.0))
    b = G.take()
    t = dense_ch(b, x_ready)
    t = Q.put("dve", lambda e, b=b: e.tensor_scalar(LF[:], psum[b][0:8, :], pp("b_forget_2", 0, 1, 8), None, ALU.add), [t, p_in])
    bfree[b] = t
    t = Q.put("dve", lambda e: e.scalar_tensor_tensor(LG[:], LF[:], -1.0, LF[:], ALU.mult, ALU.max), [t])
    t1 = Q.put("dve", lambda e: e.tensor_scalar(LF[:], LF[:], 0.0, None, ALU.min), [t])
    t = Q.put("act", lambda e: e.activation(LG[:], LG[:], ACT.Exp, scale=-1.0), [t])
    t = Q.put("act", lambda e: e.activation(LG[:], LG[:], ACT.Ln, bias=1.0), [t])
    t_lf = Q.put("dve", lambda e: e.tensor_tensor(LF[:], LF[:], LG[:], ALU.subtract), [t, t1])
    t_q2 = [None] * 8
    t_cs = [None]

    def cum_a():
        b = G.take()
        for tb in range(4):
            t = tr(psum[b][:, tb * 8:(tb + 1) * 8], LF[:, tb * 128:(tb + 1) * 128], [t_lf, bfree[b]], tb == 3)
        return Q.put("act", lambda e: e.activation(LT[:].rearrange("p t h -> p (t h)"), psum[b][:, 0:32], ACT.Copy), [t]), b

    def cum_b(t):
        b = G.take()
        for tb in range(4):
            n0 = tb * 128
            t1 = mm(psum[b][0:8, n0:512], LT[:, tb, :], TB[:, 384:896 - n0], tb == 0, True, [t, b2_in, bfree[b]], tb == 3, tb > 0)
        hi, mid, lo = C3[0:8, :], C3[32:40, :], C3[64:72, :]
        t = Q.put("dve", lambda e: e.tensor_copy(LF[:], psum[b][0:8, :]), [t1])
        bfree[b] = t
        t = Q.put("dve", lambda e: e.tensor_copy(hi, LF[:]), [t, t_c3])
        t = Q.put("dve", lambda e: e.tensor_tensor(LG[:], LF[:], hi, ALU.subtract), [t])
        t = Q.put("dve", lambda e: e.tensor_copy(mid, LG[:]), [t])
        t = Q.put("dve", lambda e: e.tensor_copy(LF[:], mid), [t])
        t = Q.put("dve", lambda e: e.tensor_tensor(LG[:], LG[:], LF[:], ALU.subtract), [t])
        t_cs[0] = Q.put("dve", lambda e: e.tensor_copy(lo, LG[:]), [t])

    for j in range(8):
        b = G.take()
        t = dense_ch(b, x_ready)
        if j == 1:
            tl, bl_ = cum_a()
            bfree[bl_] = tl
        if j == 3:
            cum_b(tl)
        t_q2[j] = bfree[b] = Q.put("act", lambda e, b=b, j=j: e.activation(QK2[:, j, :], psum[b][:, :], ACT.Copy), [t])

    t_v2, t_u2, t_vg = [None] * 4, [None] * 4, [None] * 4
    VSS = small("vss", 32, [128, 4, 8])
    t_m2 = [[None, None] for _ in range(4)]
    t_wst = []

    def gmlp():
        for half in range(2):
            w4 = WST[:, 4 * half:4 * half + 4, :]
            t_wst.append(Q.put("pool", lambda e, w4=w4: e.tensor_tensor(w4, w4, bc4(cf("triU")), ALU.mult), [b2_in, c_in]))
        vt = None
        for tb in range(4):
            t = Q.put("pool", lambda e, tb=tb: e.tensor_tensor(VSQ[:], VG[:, tb, :], VG[:, tb, :], ALU.mult), [t_vg[tb], vt, t_cs[0]])
            vt = Q.put("dve", lambda e, tb=tb: e.tensor_reduce(VSS[:, tb, :], VSQ[:].rearrange("p (g n) -> p g n", g=8), AX.X, ALU.add), [t])
        t = Q.put("act", lambda e: e.activation(VSS[:], VSS[:], ACT.Ln, bias=eps, scale=1.0 / 64), [vt])
        t = Q.put("act", lambda e: e.activation(VSS[:], VSS[:], ACT.Exp, scale=-0.5), [t])
        ready = []
        yield
        for tb in range(4):
            v8 = VG[:, tb, :].rearrange("p (g n) -> p g n", g=8)
            rs = VSS[:, tb, :].unsqueeze(2).broadcast_to([128, 8, 64])
            t1 = Q.put("pool", lambda e, tb=tb: e.tensor_tensor(VG[:, tb, :], VG[:, tb, :], pr("gmlp_norm_g_2"), ALU.mult), [vt])
            ready.append(Q.put("dve", lambda e, v8=v8, rs=rs: e.tensor_tensor(v8, v8, rs, ALU.mult), [t, t1]))
        yield
        for g in range(8):
            if g % 2 == 0:
                b = G2.take()
            o = psum[b][:, (g % 2) * 256:(g % 2) * 256 + 256]
            t = mm(o, WST[:, g, :], VG[:, :, g * 64:(g + 1) * 64], True, True, [bfree[b], ready[3]] + t_wst, True)
            u = U2[:, :, g * 64:(g + 1) * 64]
            m = MIX2[:, :, 512 + g * 64:512 + (g + 1) * 64]
            t = bfree[b] = Q.put("dve", lambda e, o=o, g=g, u=u, m=m: e.scalar_tensor_tensor(
                m, o.rearrange("p (t n) -> p t n", t=4), pp("b_spatial_2", g), u, ALU.add, ALU.mult), [t] + t_u2)
            yield
        for tb in range(4):
            t_m2[tb][1] = t

    MX2 = small("mx2", 32, [128, 4, 8])
    DN2 = small("dn2", 32, [128, 4, 8])

    def forget_attention(banks):
        bs, bt, bo = banks
        pieces = [(qb, h) for qb in range(4) for h in range(8)]
        st = [dict() for _ in pieces]
        p_free, pt_free = [None, None], [None, None]
        for n in range(len(pieces) + 2):
            if n < len(pieces):
                qb, h = pieces[n]
                nk = (qb + 1) * 128
                ps = slice(64 * (h % 2), 64 * (h % 2) + 64)
                mm(psum[bs][:, 0:nk], QK2[ps, h // 2, qb * 128:(qb + 1) * 128], QK2[ps, 4 + h // 2, 0:nk], True, False,
                   [bfree[bs]] + t_q2)
                mm(psum[bs][:, 0:nk], SEL[:, h, :], C3[:, 0:nk], False, True, [t_cs[0], t_sel])
                t = mm(psum[bs][:, nk - 128:nk], IDb[:], NUb[:], False, True, [t_id, t_nu], True, True)
                mx = MX2[:, qb, h:h + 1]
                t = Q.put("dve", lambda e, nk=nk, mx=mx: e.tensor_reduce(mx, psum[bs][:, 0:nk], AX.X, ALU.max, negate=True), [t])
                t = Q.put("dve", lambda e, mx=mx: e.tensor_scalar(mx, mx, 0.125, None, ALU.mult), [t])
                pm = P2[n % 2]
                t = bfree[bs] = Q.put("act", lambda e, nk=nk, mx=mx, pm=pm, qb=qb, h=h: e.activation(
                    pm[:, 0:nk], psum[bs][:, 0:nk], ACT.Exp, bias=mx, scale=0.125, accum_out=DN2[:, qb, h:h + 1]),
                    [t, p_free[n % 2]])
                st[n].update(nk=nk, t=t)
                yield
            if 0 <= n - 1 < len(pieces):
                m = n - 1
                s = st[m]
                nk = s["nk"]
                for k in range(nk // 128):
                    t = tr(psum[bt][:, k * 128:(k + 1) * 128], P2[m % 2][:, k * 128:(k + 1) * 128], [s["t"], bfree[bt]],
                           k == nk // 128 - 1)
                p_free[m % 2] = t
                pt = P2T[m % 2]
                if m % 2:
                    t = Q.put("act", lambda e, pt=pt, nk=nk: e.activation(pt[:, 0:nk], psum[bt][:, 0:nk], ACT.Copy), [t, pt_free[m % 2]])
                else:
                    t = Q.put("dve", lambda e, pt=pt, nk=nk: e.tensor_copy(pt[:, 0:nk], psum[bt][:, 0:nk]), [t, pt_free[m % 2]])
                s["tt"] = bfree[bt] = t
                yield
            if 0 <= n - 2 < len(pieces):
                m = n - 2
                s = st[m]
                qb, h = pieces[m]
                for k in range(qb + 1):
                    t = mm(psum[bo][:, h * 64:(h + 1) * 64], P2T[m % 2][:, k * 128:(k + 1) * 128],
                           V2[:, k, h * 64:(h + 1) * 64], k == 0, k == qb, [s["tt"], bfree[bo]] + t_v2, k == qb)
                pt_free[m % 2] = t
                if h == 7:
                    t1 = Q.put("dve", lambda e, qb=qb: e.reciprocal(DN2[:, qb, :], DN2[:, qb, :]), [s["t"]])
                    rd = DN2[:, qb, :].unsqueeze(2).broadcast_to([128, 8, 64])
                    o8 = lambda ap: ap.rearrange("p (h n) -> p h n", h=8)
                    t_m2[qb][0] = bfree[bo] = Q.put("dve", lambda e, rd=rd, qb=qb: e.tensor_tensor(
                        o8(MIX2[:, qb, 0:512]), o8(psum[bo][:, :]), rd, ALU.mult), [t, t1])
                yield

    bk = four()
    for _ in dense_tok(bk, 512, x_ready, evac_to(bk, lambda tb: V2[:, tb, :], ACT.Copy, t_v2)):
        pass
    G2 = Banks(bfree, (3, 7))
    ga = forget_attention((4, 5, 6))
    bk = [0, 1, 2, 3]
    for _ in dense_tok(bk, 512, x_ready, evac_to(bk, lambda tb: U2[:, tb, :], ACT.Gelu_apprx_tanh, t_u2)):
        step(ga, 8)
    for _ in dense_tok(bk, 512, x_ready, evac_to(bk, lambda tb: VG[:, tb, :], ACT.Gelu_apprx_tanh, t_vg)):
        step(ga, 8)
    x_pe[0] = w_used[unit[0] - 1]
    gg = gmlp()
    live = True
    while live:
        la = step(ga, 3)
        lb = step(gg)
        live = la or lb

    ready = split_mix(MIX2, t_m2)
    h_tok = out_proj(ready, None)

    XS3 = zb("xs3", [128, 4, 1024], F32, 92)
    AC = zb("ac", [128, 22, 512], F32, 48)
    TA = [zb(f"ta{i}", [128, 512], F32, 92 + 2 * i) for i in range(2)]
    TGG = [zb(f"tgg{i}", [128, 512], F32, 96 + 2 * i) for i in range(2)]
    AH = [zb(f"ah{i}", [128, 512], F32R, 108 + 2 * i) for i in range(4)]
    AL = [zb(f"al{i}", [128, 512], F32R, 116 + 2 * i) for i in range(4)]

    x_ready = norm_xt(2, "norm_ffn_g_2", XS3, h_tok, None)
    ta_free = [x_ready[7], x_ready[7]]
    tg_free = [x_ready[7], x_ready[7]]

    def conv3(c, dst, bank, t, free):
        wc = lambda i: pp("conv_w_2", i * 44 + c)
        bias = pp("conv_b_2", c)
        t = Q.put("act", lambda e: e.activation(dst[:], psum[bank][:, :], ACT.Identity, scale=wc(2), bias=bias), [t, free, p_in])
        for i in (0, 1):
            sh = 2 - i
            t = Q.put("dve", lambda e, i=i, sh=sh: e.scalar_tensor_tensor(
                dst[:, sh:T], psum[bank][:, 0:T - sh], wc(i), dst[:, sh:T], ALU.mult, ALU.add), [t, p_in])
        bfree[bank] = t
        return t

    t_ac = [None] * 22

    def up_post(j, b1, t1, b2, t2):
        ta, tg = TA[j % 2], TGG[j % 2]
        t1 = conv3(j, ta, b1, t1, ta_free[j % 2])
        t2 = conv3(22 + j, tg, b2, t2, tg_free[j % 2])
        t2 = Q.put("act", lambda e: e.activation(tg[:], tg[:], ACT.Silu), [t2])
        t_ac[j] = ta_free[j % 2] = tg_free[j % 2] = Q.put(
            "dve", lambda e: e.tensor_tensor(AC[:, j, :], ta[:], tg[:], ALU.mult), [t1, t2])

    pend = None
    for j in range(22):
        b1 = G.take()
        t1 = dense_ch(b1, x_ready)
        if pend:
            up_post(*pend)
        b2 = G.take()
        t2 = dense_ch(b2, x_ready)
        pend = (j, b1, t1, b2, t2)
    up_post(*pend)

    a_used = [None] * 4
    a_split = [None] * 22

    def a_prep(k):
        ah, al = AH[k % 4], AL[k % 4]
        t = Q.put("act", lambda e: e.activation(ah[:], AC[:, k, :], ACT.Copy), [t_ac[k], a_used[k % 4], x_ready[7]])
        a_split[k] = Q.put("dve", lambda e: e.tensor_tensor(al[:], AC[:, k, :], ah[:].bitcast(F32), ALU.subtract),
                           [t, t_ac[k], a_used[k % 4]])

    a_prep(0)
    a_prep(1)
    hd = [None] * 4
    s_out = sem("s_out")
    ov = out.rearrange("b (t p) d -> (b p) t d", p=128)
    OUT = zb("outt", [128, 4, 1024], F32, 0)

    def finish(tb):
        t = row_rstd(0, tb, H[:, tb, :], OUT[:, tb, :], [hd[tb], w_used[unit[0] - 1]])
        t = Q.put("dve", lambda e: e.scalar_tensor_tensor(OUT[:, tb, :], H[:, tb, :], RS[0][:, tb:tb + 1], pr("norm_final_g_2"),
                                                          ALU.mult, ALU.mult), [t])
        Q.dma("sp", ov[:, tb, :], OUT[:, tb, :], s_out, 16 * (tb + 1), [t])

    order = [(tb, n) for tb in range(4) for n in range(2)]
    for k in range(22):
        u = unit[0]
        unit[0] += 1
        w_ahead(u + 2)
        if k + 2 < 22:
            a_prep(k + 2)
        for i, (tb, n) in enumerate(order):
            ts = slice(tb * 128, (tb + 1) * 128)
            c = slice(n * 512, (n + 1) * 512)
            t = mm3(psum[i][:, :], AH[k % 4][:, ts], AL[k % 4][:, ts], WH[u % NS][:, c], WL[u % NS][:, c], k == 0, k == 21,
                    [w_split[u], a_split[k]] + ([bfree[i]] if k == 0 else []), k == 21 or i == 7)
            if k == 21:
                hv = H[:, tb, c]
                hd[tb] = Q.put("dve", lambda e, hv=hv, i=i: e.tensor_tensor(hv, hv, psum[i][:, :], ALU.add), [t])
        w_used[u] = a_used[k % 4] = t
    for tb in range(4):
        finish(tb)
    Q.put("sp", lambda e: e.wait_ge(s_out, 64), (), inc=False)

    with nc.Block() as block:
        @block.sync
        def _(e):
            for f in Q.q["sp"]:
                f(e)

        @block.scalar
        def _(e):
            for f in Q.q["act"]:
                f(e)

        @block.vector
        def _(e):
            for f in Q.q["dve"]:
                f(e)

        @block.gpsimd
        def _(e):
            for f in Q.q["pool"]:
                f(e)

        @block.tensor
        def _(e):
            for f in Q.q["pe"]:
                f(e)


def lay_out(a):
    mats = {k: a[k][0] for k in ("w_in", "w_out", "w_in_2", "w_out_2", "w_up_2", "w_down_2")}
    pp = np.zeros((128, NPP), np.float32)

    def put(name, v):
        at, w = PP[name]
        pp[:v.shape[0], at:at + w] = v

    for n in ("norm_w", "norm_mix_g_2", "norm_ffn_g_2"):
        put(n, a[n].reshape(8, 128).T)
    put("dn_conv_w", a["dn_conv_w"][0].reshape(5, 12, 128).transpose(2, 1, 0).reshape(128, 60))
    put("conv_w_2", a["conv_w_2"][0].reshape(3, 44, 128).transpose(2, 0, 1).reshape(128, 132))
    put("conv_b_2", a["conv_b_2"][0].reshape(44, 128).T)
    put("b_spatial_2", a["b_spatial_2"][0].T)
    put("b_forget_2", a["b_forget_2"][0].reshape(8, 1))
    pr = np.concatenate([a[n].reshape(-1) for n in PR])
    ws = np.ascontiguousarray(a["w_spatial_2"][0].transpose(2, 0, 1))
    return dict(x=np.ascontiguousarray(a["x"]), wflat=pack_weights(mats), cf=const_tile(), pp=pp, pr=pr, ws=ws,
                tb=tri_big(), sel=sel_tile())


def kernel(**inputs):
    import concourse.bacc as bacc
    from concourse.bass_utils import run_bass_kernel_spmd

    arrays = lay_out({k: np.asarray(v) for k, v in inputs.items()})
    nc = bacc.Bacc("TRN2", target_bir_lowering=False, num_devices=1)
    maps, args = {}, {}
    for name, v in arrays.items():
        maps["in_" + name] = v
        args[name] = nc.dram_tensor("in_" + name, v.shape, mybir.dt.from_np(v.dtype), kind="ExternalInput").ap()
    o = nc.dram_tensor("out_0", (1, T, D), F32, kind="ExternalOutput").ap()
    program(nc, args["x"], args["wflat"], args["cf"], args["pp"], args["pr"], args["ws"], args["tb"], args["sel"], o)
    r = run_bass_kernel_spmd(nc, [maps], core_ids=[0])
    return r.results[0]["out_0"]
```

```python
import math

import numpy as np

import concourse.bass as bass
from concourse import mybir

F32 = mybir.dt.float32
F32R = mybir.dt.float32r
BF16 = mybir.dt.bfloat16
ALU = mybir.AluOpType
ACT = mybir.ActivationFunctionType
AX = mybir.AxisListType

KB = 1024
BASE = 16512
EPS = 1e-6
NEG = -1e30
D = 1024
T = 512

P1_CH = [(j * 128, 128) for j in range(12)]
P1_TOK = [[(2048, 16), (2576, 256)], [(2064, 512)], [(2832, 512)], [(1536, 512)]]
P2_CH = [(j * 128, 128) for j in range(8)]
P2_TOK = [(1024, 512), (1536, 512), (2048, 512)]


def unit_plan():
    plan = []
    for c in P1_CH:
        plan.append(("w_in", range(8), [c], 128))
    for cols in P1_TOK:
        n = sum(w for _, w in cols)
        for k in range(0, 8, 2):
            plan.append(("w_in", range(k, k + 2), cols, n))
    for n in range(2):
        for k in range(0, 8, 2):
            plan.append(("w_out", range(k, k + 2), [(n * 512, 512)], 512))
    plan.append(("w_in_2", range(8), [(2560, 8)], 128))
    for c in P2_CH:
        plan.append(("w_in_2", range(8), [c], 128))
    for c in P2_TOK:
        for k in range(0, 8, 2):
            plan.append(("w_in_2", range(k, k + 2), [c], 512))
    for n in range(2):
        for k in range(0, 8, 2):
            plan.append(("w_out_2", range(k, k + 2), [(n * 512, 512)], 512))
    for j in range(22):
        for half in range(2):
            plan.append(("w_up_2", range(8), [(half * 2816 + j * 128, 128)], 128))
    for k in range(22):
        plan.append(("w_down_2", range(k, k + 1), [(0, 1024)], 1024))
    return plan


def pack_weights(mats):
    parts = []
    for name, ks, cols, width in unit_plan():
        m = mats[name]
        u = np.zeros((128, len(ks), width), np.float32)
        for i, k in enumerate(ks):
            at = 0
            for c, w in cols:
                u[:, i, at:at + w] = m[k * 128:(k + 1) * 128, c:c + w]
                at += w
        parts.append(u.reshape(-1))
    return np.concatenate(parts)


CF = {}
_at = 0
for _name, _w in (("ident", 128), ("triU", 128), ("triL", 128), ("SL", 128), ("SU", 128), ("ones", 128),
                  ("LM", 14 * 128), ("cos", 256), ("sin", 256)):
    CF[_name] = (_at, _w)
    _at += _w
NCF = _at


def const_tile():
    c = np.zeros((128, NCF), np.float32)
    i = np.arange(128)[:, None]
    j = np.arange(128)[None, :]
    put = lambda name, v: c.__setitem__((slice(None), slice(CF[name][0], CF[name][0] + CF[name][1])), v)
    put("ident", i == j)
    put("triU", i <= j)
    put("triL", i >= j)
    put("SL", i > j)
    put("SU", i < j)
    put("ones", 1.0)
    lm = []
    for d in range(2):
        for lvl in range(7):
            s = 1 << lvl
            a, b = (i, j) if d == 0 else (j, i)
            lm.append(((a // (2 * s) == b // (2 * s)) & ((a // s) % 2 == 0) & ((b // s) % 2 == 1)) | (i == j))
    put("LM", np.concatenate(lm, axis=1))
    inv = (np.float32(10000.0) ** (-np.arange(0, 64, 2, dtype=np.float32) / np.float32(64))).astype(np.float32)
    ang = np.arange(512, dtype=np.float32)[:, None] * inv[None, :]
    cos = np.cos(ang.astype(np.float64)).astype(np.float32)
    sin = np.sin(ang.astype(np.float64)).astype(np.float32)
    tok = lambda a: a.reshape(4, 128, 64).transpose(1, 0, 2).reshape(128, 256)
    put("cos", tok(np.concatenate([cos, cos], axis=1)))
    put("sin", tok(np.concatenate([-sin, sin], axis=1)))
    return c


def tri_big():
    j = np.arange(896)[None, :]
    return (j >= np.arange(128)[:, None] + 384).astype(np.float32)


def sel_tile():
    s = np.zeros((96, 8, 128), np.float32)
    for h in range(8):
        for part in range(3):
            s[32 * part + h, h, :] = -8.0
    return s.reshape(96, 1024)


PP = {"norm_w": (0, 8), "norm_mix_g_2": (8, 8), "norm_ffn_g_2": (16, 8), "dn_conv_w": (24, 60),
      "conv_w_2": (84, 132), "conv_b_2": (216, 44), "b_spatial_2": (260, 8), "b_forget_2": (268, 1)}
NPP = 272
PR = {"dn_a_log": (0, 8), "dn_dt_bias": (8, 8), "swa_sinks": (16, 8), "dn_out_norm_w": (24, 128),
      "swa_q_norm_w": (152, 64), "swa_k_norm_w": (216, 64), "gmlp_norm_g_2": (280, 512), "norm_final_g_2": (792, 1024)}
NPR = 792


class Queues:

    def __init__(self, nc):
        self.q = {e: [] for e in ("pe", "act", "dve", "pool", "sp")}
        self.sem = {e: nc.alloc_semaphore("done_" + e) for e in self.q}
        self.n = dict.fromkeys(self.q, 0)
        self.waited = {e: {} for e in self.q}

    def put(self, eng, fn, waits=(), inc=True):
        for w in waits:
            if w is not None:
                sem, value = w
                if self.waited[eng].get(sem.name, 0) < value:
                    self.waited[eng][sem.name] = value
                    self.q[eng].append(lambda e, sem=sem, value=value: e.wait_ge(sem, value))
        if not inc:
            self.q[eng].append(fn)
            return None
        self.n[eng] += 1
        sem = self.sem[eng]
        self.q[eng].append(lambda e: fn(e).then_inc(sem, 1))
        return (sem, self.n[eng])

    def dma(self, eng, out, in_, sem, value, waits=()):
        self.put(eng, lambda e: e.dma_start(out, in_).then_inc(sem, 16), waits, inc=False)
        return (sem, value)


class BankFree(list):

    def __init__(self):
        super().__init__([None] * 8)
        self.held = set()

    def __setitem__(self, b, token):
        super().__setitem__(b, token)
        self.held.discard(b)


class Banks:

    def __init__(self, free, ids):
        self.free, self.ids, self.i = free, list(ids), 0

    def take(self):
        for _ in self.ids:
            b = self.ids[self.i % len(self.ids)]
            self.i += 1
            if b not in self.free.held:
                self.free.held.add(b)
                return b
        raise AssertionError("no bank is free")


def program(nc, x, wflat, cfd, ppd, prd, wsd, tbd, seld, out):
    Q = Queues(nc)
    psum = [nc.alloc_psum_tensor(f"bank{i}", [128, 512], F32) for i in range(8)]
    bfree = BankFree()

    def sb(name, shape, dt, kb):
        return nc.alloc_sbuf_tensor_at(name, shape, dt, offset=BASE + int(round(kb * KB)))

    def sem(name):
        return nc.alloc_semaphore(name)

    NS = 4
    RAW = [sb(f"raw{i}", [128, 1024], F32, 4 * i) for i in range(NS)]
    WH = [sb(f"wh{i}", [128, 1024], F32R, 16 + 4 * i) for i in range(NS)]
    WL = [sb(f"wl{i}", [128, 1024], F32R, 32 + 4 * i) for i in range(NS)]
    C0 = 48
    CT = sb("consts", [128, NCF], F32, C0)
    PT_ = sb("pparams", [128, NPP], F32, C0 + 12)
    RT = sb("rparams", [128, NPR], F32, C0 + 13.125)
    NUb = sb("nub", [128, 128], BF16, C0 + 20.25)
    NLb = sb("nlb", [128, 128], BF16, C0 + 20.5)
    IDb = sb("idb", [128, 128], BF16, C0 + 20.75)
    ID2 = sb("id2", [128, 512], BF16, C0 + 21)
    IDR = sb("idr", [128, 128], F32R, C0 + 22)
    CE = sb("ceps", [128, 2], F32, C0 + 22.5)
    small_at = [C0 + 22.625]

    def small(name, cols, shape=None):
        t = sb(name, shape or [128, cols], F32, small_at[0])
        small_at[0] += ((cols * 4 + 31) // 32 * 32) / KB
        assert small_at[0] <= C0 + 28
        return t

    Z0 = C0 + 28

    def zb(name, shape, dt, kb):
        n = 1
        for s in shape[1:]:
            n *= s
        assert kb + n * (2 if dt == BF16 else 4) / KB <= 131.8, name
        return sb(name, shape, dt, Z0 + kb)

    def cf(name, i=0):
        a, w = CF[name]
        return CT[:, a + 128 * i:a + 128 * (i + 1)] if name == "LM" else CT[:, a:a + w]

    def pp(name, i=0, n=1, parts=128):
        a, _ = PP[name]
        return PT_[0:parts, a + i:a + i + n]

    def pr(name):
        a, w = PR[name]
        return RT[:, a:a + w]

    XH = zb("xh", [128, 8, 512], F32R, 0)
    XL = zb("xl", [128, 8, 512], F32R, 16)
    H = zb("h", [128, 4, 1024], F32, 32)

    s_c = sem("s_const")
    s_p = sem("s_params")
    s_x = [sem(f"s_x{i}") for i in range(4)]
    xv = x.rearrange("b (t p) d -> (b p) t d", p=128)
    for tb in range(4):
        Q.dma("act", H[:, tb, :], xv[:, tb, :], s_x[tb], 16)
    Q.dma("act", CT[:], cfd, s_c, 16)
    Q.dma("act", PT_[:], ppd, s_p, 16)
    Q.dma("act", RT[:], prd[0:NPR].partition_broadcast(128), s_p, 32)
    x_in = [(s_x[tb], 16) for tb in range(4)]
    c_in = (s_c, 16)
    p_in = (s_p, 32)

    plan = unit_plan()
    NU = len(plan)
    s_w = [sem(f"s_w{i}") for i in range(NS)]
    widths = [len(ks) * width for _, ks, _, width in plan]
    starts = [128 * sum(widths[:u]) for u in range(NU)]
    w_read = [None] * NU
    w_split = [None] * NU
    w_used = [None] * NU
    issued = [0, 0]
    last_split = [27]
    ring_busy = []

    def w_load(u):
        src = wflat[starts[u]:starts[u] + 128 * widths[u]].rearrange("(p n) -> p n", p=128)
        Q.dma("sp", RAW[u % NS][:, 0:widths[u]], src, s_w[u % NS], 16 * (u // NS + 1),
              [w_read[u - NS] if u >= NS else None])

    def w_prep(u):
        n = widths[u]
        raw, hi, lo = RAW[u % NS][:, 0:n], WH[u % NS][:, 0:n], WL[u % NS][:, 0:n]
        there = (s_w[u % NS], 16 * (u // NS + 1))
        free = w_used[u - NS] if u >= NS else None
        t = Q.put("act", lambda e: e.activation(hi, raw, ACT.Copy), [there, free] + ring_busy)
        t = Q.put("pool", lambda e: e.tensor_tensor(lo, raw, hi.bitcast(F32), ALU.subtract), [there, t, free])
        w_read[u] = w_split[u] = t

    def w_ahead(u):
        u = min(u, last_split[0], NU - 1)
        while issued[1] <= u:
            while issued[0] < min(issued[1] + NS, NU):
                w_load(issued[0])
                issued[0] += 1
            w_prep(issued[1])
            issued[1] += 1
        while issued[0] < min(issued[1] + NS, NU):
            w_load(issued[0])
            issued[0] += 1

    unit = [0]

    def mm(out_, l, r, start, stop, waits=(), inc=False, part=False):
        return Q.put("pe", lambda e: e.matmul(out_, l, r, start=start, stop=stop, skip_group_check=part), waits, inc)

    def tr(out_, in_, waits=(), inc=False):
        idn = cf("ident")[0:in_.shape[0], 0:in_.shape[0]]
        return Q.put("pe", lambda e: e.transpose(out_, in_, idn), list(waits) + [c_in], inc)

    def mm3(o, lh, ll, rh, rl, start, stop, waits=(), inc=False):
        mm(o, lh, rh, start, False, waits)
        mm(o, lh, rl, False, False)
        return mm(o, ll, rh, False, stop, (), inc)

    def dense_ch(bank, x_ready):
        u = unit[0]
        unit[0] += 1
        w_ahead(u + 2)
        w = [w_split[u], bfree[bank]]
        for k in range(8):
            t = mm3(psum[bank][:, :], WH[u % NS][:, k * 128:(k + 1) * 128], WL[u % NS][:, k * 128:(k + 1) * 128],
                    XH[:, k, :], XL[:, k, :], k == 0, k == 7, w + [x_ready[k]], k == 7)
        w_used[u] = t
        return t

    def dense_tok(banks, n, x_ready, evac):
        for k0 in range(0, 8, 2):
            u = unit[0]
            unit[0] += 1
            w_ahead(u + 2)
            for tb in range(4):
                for k in range(2):
                    c = slice(k * n, (k + 1) * n)
                    ts = slice(tb * 128, (tb + 1) * 128)
                    w = [w_split[u], x_ready[k0 + k]] + ([bfree[banks[tb]]] if k0 + k == 0 else [])
                    t = mm3(psum[banks[tb]][:, 0:n], XH[:, k0 + k, ts], XL[:, k0 + k, ts], WH[u % NS][:, c],
                            WL[u % NS][:, c], k0 + k == 0, k0 + k == 7, w, k == 1)
                if k0 == 6:
                    evac(tb, t)
            w_used[u] = t
            yield

    t_ce = Q.put("dve", lambda e: e.memset(CE[:, 0:1], EPS))
    t_ce = Q.put("dve", lambda e: e.memset(CE[:, 1:2], -0.5 * math.log(128.0)))
    eps, lnq = CE[:, 0:1], CE[:, 1:2]
    w_ahead(0)

    SS = [small(f"ss{i}", 4) for i in range(3)]
    RS = [small(f"rs{i}", 4) for i in range(3)]

    def row_rstd(i, tb, src, junk, waits):
        t = Q.put("act", lambda e: e.activation(junk, src, ACT.Square, accum_out=SS[i][:, tb:tb + 1]), waits)
        t = Q.put("act", lambda e: e.activation(RS[i][:, tb:tb + 1], SS[i][:, tb:tb + 1], ACT.Ln, bias=eps,
                                                scale=1.0 / D), [t, t_ce])
        return Q.put("act", lambda e: e.activation(RS[i][:, tb:tb + 1], RS[i][:, tb:tb + 1], ACT.Exp, scale=-0.5), [t])

    def norm_xt(i, gain, XS, ready, free):
        xs = []
        for tb in range(4):
            t = row_rstd(i, tb, H[:, tb, :], XS[:, tb, :], [ready[tb], free])
            xs.append(Q.put("dve", lambda e, tb=tb: e.tensor_scalar(XS[:, tb, :], H[:, tb, :], RS[i][:, tb:tb + 1], None,
                                                                    ALU.mult), [t]))
        return split_t(XS, xs, gain)

    x_pe = [None]

    def split_t(src, ready, gain):
        done = []
        free = x_pe[0]
        for k in range(8):
            b = G.take()
            for tb in range(4):
                t = tr(psum[b][:, tb * 128:(tb + 1) * 128], src[:, tb, k * 128:(k + 1) * 128],
                       [ready[tb], bfree[b]], tb == 3)
            s = pp(gain, k) if gain else 1.0
            t1 = Q.put("act", lambda e, b=b, k=k, s=s: e.activation(XH[:, k, :], psum[b][:, :], ACT.Copy, scale=s),
                       [t, free, p_in])
            t2 = Q.put("dve", lambda e, b=b, k=k, s=s: e.scalar_tensor_tensor(
                XL[:, k, :], psum[b][:, :], s, XH[:, k, :].bitcast(F32), ALU.mult, ALU.subtract), [t, t1, free, p_in])
            bfree[b] = t2
            done.append(t2)
        return done

    G = Banks(bfree, range(8))

    XS1 = zb("xs1", [128, 4, 1024], F32, 88)
    QK = zb("qk", [128, 8, 512], F32, 48)
    VC = zb("vc", [128, 4, 512], F32, 64)
    KT = zb("kt", [128, 4, 512], F32, 72)
    VT = zb("vt", [128, 4, 512], F32, 80)
    MIX = zb("mix", [128, 4, 1024], F32, 88)
    SWR = zb("swr", [128, 4, 640], F32, 104)
    SV = zb("sv", [128, 4, 128], F32, 114)
    SQ = [zb(f"sq{i}", [128, 512], F32, 116 + 2 * i) for i in range(3)]
    R1 = zb("r1", [128, 640], F32, 122)
    R2 = zb("r2", [128, 640], F32, 124.5)
    SKT = zb("skt", [128, 512], F32, 127)
    SQT = zb("sqt", [128, 4, 512], F32, 64)
    BD = small("bd", 64, [128, 4, 16])

    x_ready = norm_xt(0, "norm_w", XS1, x_in, None)
    t_nu = Q.put("dve", lambda e: e.tensor_scalar(NUb[:], cf("SU"), NEG, None, ALU.mult), [c_in])
    t_nl = Q.put("dve", lambda e: e.tensor_scalar(NLb[:], cf("SL"), NEG, None, ALU.mult))
    t_id = Q.put("dve", lambda e: e.tensor_copy(IDb[:], cf("ident")))
    for h in range(4):
        t_id = Q.put("dve", lambda e, h=h: e.tensor_scalar(ID2[:, h * 128:(h + 1) * 128], cf("ident"), 2.0, None, ALU.mult))
    t_id = Q.put("dve", lambda e: e.tensor_copy(IDR[:], cf("ident")))

    def conv5(j, dst, bank, t):
        wc = lambda i: pp("dn_conv_w", j * 5 + i)
        t = Q.put("act", lambda e: e.activation(dst, psum[bank][:, :], ACT.Copy, scale=wc(2)), [t, p_in])
        for i in (0, 1, 3, 4):
            a, b = max(0, 2 - i), min(T, T + 2 - i)
            sh = i - 2
            t = Q.put("dve", lambda e, i=i, a=a, b=b, sh=sh: e.scalar_tensor_tensor(
                dst[:, a:b], psum[bank][:, a + sh:b + sh], wc(i), dst[:, a:b], ALU.mult, ALU.add), [t, p_in])
        bfree[bank] = t
        return Q.put("act", lambda e: e.activation(dst, dst, ACT.Silu), [t])

    t_conv = [None] * 12
    pend = None
    for j in range(12):
        b = G.take()
        t = dense_ch(b, x_ready)
        if pend:
            pj, pb, pt = pend
            t_conv[pj] = conv5(pj, QK[:, pj, :] if pj < 8 else VC[:, pj - 8, :], pb, pt)
        pend = (j, b, t)
    pj, pb, pt = pend
    t_conv[pj] = conv5(pj, VC[:, pj - 8, :], pb, pt)

    t_qk = [None] * 8
    sq_free = [None] * 3

    def qk_norm():
        for j in range(8):
            s = SQ[j % 3]
            t = Q.put("act", lambda e, j=j, s=s: e.activation(s[:], QK[:, j, :], ACT.Square), [t_conv[j], sq_free[j % 3]])
            b = G.take()
            t = mm(psum[b][:, :], cf("ones"), s[:], True, True, [t, bfree[b], c_in], True)
            yield
            t = Q.put("act", lambda e, b=b, s=s: e.activation(s[:], psum[b][:, :], ACT.Ln, bias=eps), [t, t_ce])
            bfree[b] = t
            bias = lnq if j < 4 else 0.0
            t = Q.put("act", lambda e, s=s, bias=bias: e.activation(s[:], s[:], ACT.Exp, scale=-0.5, bias=bias), [t])
            t_qk[j] = sq_free[j % 3] = Q.put(
                "dve", lambda e, j=j, s=s: e.tensor_tensor(QK[:, j, :], QK[:, j, :], s[:], ALU.mult), [t])
            yield

    t_kt = [None] * 4
    t_vt = [None] * 4

    def to_tokens():
        for dst, srcs, ready, done in ((VT, VC, t_conv[8:12], t_vt), (KT, QK, None, t_kt)):
            for cb in range(4):
                b = G.take()
                for h in range(4):
                    src = srcs[:, h, cb * 128:(cb + 1) * 128] if ready else srcs[:, 4 + h, cb * 128:(cb + 1) * 128]
                    r = ready[h] if ready else t_qk[4 + h]
                    t = tr(psum[b][:, h * 128:(h + 1) * 128], src, [r, bfree[b]], h == 3)
                done[cb] = bfree[b] = Q.put("act", lambda e, b=b, cb=cb, dst=dst: e.activation(
                    dst[:, cb, :], psum[b][:, :], ACT.Copy), [t])
                yield

    g4 = lambda name: small(name, 32, [128, 2, 4, 4])
    BETA, NBETA, GG, SPA, SPB, GC, GL, EG, EGL, EL, BEG = (g4(n) for n in (
        "beta", "nbeta", "gg", "spa", "spb", "gc", "gl", "eg", "egl", "el", "beg"))
    EA = small("ea", 8)
    NSINK = small("nsink", 8)
    t_gate = [None]

    def gates(t_bd):
        dch = lambda ap: ap.rearrange("p c (d h) -> p d c h", d=2)
        bl, dl = dch(BD[:, :, 0:8]), dch(BD[:, :, 8:16])
        row = lambda ap: ap.rearrange("p (d h) -> p d h", d=2).unsqueeze(2).broadcast_to([128, 2, 4, 4])
        t = Q.put("act", lambda e: e.activation(EA[:], pr("dn_a_log"), ACT.Exp), [p_in])
        for d in range(2):
            t = Q.put("act", lambda e, d=d: e.activation(BETA[:, d], bl[:, d], ACT.Exp, scale=-1.0), t_bd)
        t = Q.put("dve", lambda e: e.tensor_scalar(BETA[:], BETA[:], 1.0, None, ALU.add), [t])
        t = Q.put("dve", lambda e: e.reciprocal(BETA[:], BETA[:]), [t])
        t = Q.put("dve", lambda e: e.tensor_scalar(NBETA[:], BETA[:], -1.0, None, ALU.mult), [t])
        for d in range(2):
            rb = pr("dn_dt_bias")[:, 4 * d:4 * d + 4].unsqueeze(1).broadcast_to([128, 4, 4])
            t = Q.put("dve", lambda e, d=d, rb=rb: e.tensor_tensor(SPA[:, d], dl[:, d], rb, ALU.add), [p_in] + t_bd)
        t = Q.put("dve", lambda e: e.scalar_tensor_tensor(SPB[:], SPA[:], -1.0, SPA[:], ALU.mult, ALU.max), [t])
        t1 = Q.put("dve", lambda e: e.tensor_scalar(SPA[:], SPA[:], 0.0, None, ALU.max), [t])
        t = Q.put("act", lambda e: e.activation(SPB[:], SPB[:], ACT.Exp, scale=-1.0), [t])
        t = Q.put("act", lambda e: e.activation(SPB[:], SPB[:], ACT.Ln, bias=1.0), [t])
        t = Q.put("dve", lambda e: e.tensor_tensor(SPA[:], SPA[:], SPB[:], ALU.add), [t, t1])
        for d in range(2):
            ea = EA[:, 4 * d:4 * d + 4].unsqueeze(1).broadcast_to([128, 4, 4])
            t1 = Q.put("dve", lambda e, d=d, ea=ea: e.scalar_tensor_tensor(GG[:, d], SPA[:, d], -1.0, ea, ALU.mult, ALU.mult), [t])
        yield
        b = G.take()
        fl = lambda ap: ap.rearrange("p c h -> p (c h)")
        mm(psum[b][:, 0:16], cf("triU"), fl(GG[:, 0]), True, True, [t1, bfree[b], c_in])
        mm(psum[b][:, 16:32], cf("triL"), fl(GG[:, 1]), True, True)
        t = mm(psum[b][:, 32:64], cf("ones"), GG[:].rearrange("p d c h -> p (d c h)"), True, True, (), True)
        f3 = lambda t_: t_[:].rearrange("p d c h -> p (d c h)")
        t = Q.put("dve", lambda e: e.tensor_copy(f3(GC), psum[b][:, 0:32]), [t])
        t = Q.put("dve", lambda e: e.tensor_copy(f3(GL), psum[b][:, 32:64]), [t])
        bfree[b] = t
        t1 = Q.put("dve", lambda e: e.tensor_tensor(EGL[:], GL[:], GC[:], ALU.subtract), [t])
        t = Q.put("act", lambda e: e.activation(EG[:], GC[:], ACT.Exp), [t])
        t2 = Q.put("act", lambda e: e.activation(EL[:], GL[:], ACT.Exp), [t])
        t2 = Q.put("act", lambda e: e.activation(EGL[:], EGL[:], ACT.Exp), [t1])
        t = Q.put("dve", lambda e: e.tensor_tensor(BEG[:], BETA[:], EG[:], ALU.mult), [t])
        t_gate[0] = [t, t2]
        yield

    SSQ = small("ssq", 40, [128, 4, 10])
    t_swt = [None] * 4

    def swa_prep(t_swr):
        rows = SWR[:].rearrange("p t (h d) -> p t h d", d=64)
        r1 = R1[:].rearrange("p (h d) -> p h d", d=64)
        r2 = R2[:].rearrange("p (h d) -> p h d", d=64)
        tl = None
        tw = [None] * 4
        for tb in range(4):
            t = Q.put("pool", lambda e, tb=tb: e.tensor_tensor(R1[:], SWR[:, tb, :], SWR[:, tb, :], ALU.mult), t_swr[tb] + [tl])
            tl = Q.put("dve", lambda e, tb=tb: e.tensor_reduce(SSQ[:, tb, :], r1, AX.X, ALU.add), [t])
            yield
        t = Q.put("act", lambda e: e.activation(SSQ[:], SSQ[:], ACT.Ln, bias=eps, scale=1.0 / 64), [tl, t_ce])
        t_ss = Q.put("act", lambda e: e.activation(SSQ[:], SSQ[:], ACT.Exp, scale=-0.5), [t])
        t_r1 = tl
        t_r2 = None
        for tb in range(4):
            cs = cf("cos")[:, tb * 64:(tb + 1) * 64]
            sn = cf("sin")[:, tb * 64:(tb + 1) * 64]
            bc = lambda ap, n: ap.unsqueeze(1).broadcast_to([128, n, 64])
            rs = SSQ[:, tb, :].unsqueeze(2).broadcast_to([128, 10, 64])
            t = Q.put("dve", lambda e, tb=tb, rs=rs: e.tensor_tensor(rows[:, tb], rows[:, tb], rs, ALU.mult), [t_ss])
            tk = Q.put("pool", lambda e, tb=tb, bc=bc: e.tensor_tensor(
                rows[:, tb, 0:2], rows[:, tb, 0:2], bc(pr("swa_k_norm_w"), 2), ALU.mult), [t, p_in])
            t = Q.put("pool", lambda e, tb=tb, bc=bc: e.tensor_tensor(
                rows[:, tb, 2:10], rows[:, tb, 2:10], bc(pr("swa_q_norm_w"), 8), ALU.mult), [t, p_in])
            yield
            t1 = Q.put("dve", lambda e, tb=tb, bc=bc, cs=cs: e.tensor_tensor(r1, rows[:, tb], bc(cs, 10), ALU.mult),
                       [t, tk, t_r1, c_in])
            for o, i in ((0, 32), (32, 0)):
                s = sn[:, o:o + 32].unsqueeze(1).broadcast_to([128, 10, 32])
                t2 = Q.put("dve", lambda e, tb=tb, o=o, i=i, s=s: e.tensor_tensor(
                    r2[:, :, o:o + 32], rows[:, tb, :, i:i + 32], s, ALU.mult), [t, tk, t_r2, c_in])
            t3 = Q.put("dve", lambda e, tb=tb: e.tensor_tensor(rows[:, tb, 0:2], r1[:, 0:2], r2[:, 0:2], ALU.add), [t1, t2])
            qo = rows[:, tb, 2:10].rearrange("p (i g) d -> p g i d", g=2)
            qa = r1[:, 2:10].rearrange("p (g i) d -> p g i d", g=2)
            qb_ = r2[:, 2:10].rearrange("p (g i) d -> p g i d", g=2)
            t_r1 = t_r2 = tw[tb] = Q.put("dve", lambda e, qo=qo, qa=qa, qb_=qb_: e.tensor_tensor(qo, qa, qb_, ALU.add), [t1, t2])
            yield
        for i in range(5):
            b = G.take()
            for tb in range(4):
                src = SWR[:, tb, 0:128] if i == 4 else SWR[:, tb, 128 + i * 128:256 + i * 128]
                t = tr(psum[b][:, tb * 128:(tb + 1) * 128], src, [tw[tb], bfree[b]], tb == 3)
            dst = SKT[:] if i == 4 else SQT[:, i, :]
            t_swt[0] = bfree[b] = Q.put("act", lambda e, b=b, dst=dst: e.activation(dst, psum[b][:, :], ACT.Copy), [t] + t_vt)
            yield

    t_bd = [None] * 4
    t_k = [None] * 4
    t_swr = [None] * 4
    t_sv = [None] * 4
    t_z = [None] * 4
    t_sz = [None] * 4

    def evac_first(banks):
        def f(tb, t):
            b = banks[tb]
            t = Q.put("act", lambda e: e.activation(BD[:, tb, :], psum[b][:, 0:16], ACT.Copy), [t])
            t_bd[tb] = t
            t_k[tb] = Q.put("act", lambda e: e.activation(SWR[:, tb, 0:128], psum[b][:, 16:144], ACT.Copy))
            bfree[b] = t_sv[tb] = Q.put("act", lambda e: e.activation(SV[:, tb, :], psum[b][:, 144:272], ACT.Copy))
        return f

    def evac_to(banks, dst, func, done):
        def f(tb, t):
            b = banks[tb]
            done[tb] = bfree[b] = Q.put("act", lambda e: e.activation(dst(tb), psum[b][:, :], func), [t])
        return f

    def step(g, n=1):
        for _ in range(n):
            if next(g, "end") == "end":
                return False
        return True

    def four():
        return [G.take() for _ in range(4)]

    bk = [0, 1, 2, 3]
    G = Banks(bfree, (4, 5, 6, 7))
    g1 = qk_norm()
    step(g1, 1)
    for _ in dense_tok(bk, 272, x_ready, evac_first(bk)):
        step(g1, 4)
    g2 = gates(t_bd)
    for _ in dense_tok(bk, 512, x_ready, evac_to(bk, lambda tb: SWR[:, tb, 128:640], ACT.Copy, t_swr)):
        step(g1, 2)
        step(g2, 1)
    while step(g1):
        pass
    while step(g2):
        pass
    g1 = to_tokens()
    g2 = swa_prep([[a, b_] for a, b_ in zip(t_k, t_swr)])
    for _ in dense_tok(bk, 512, x_ready, evac_to(bk, lambda tb: MIX[:, tb, 512:1024], ACT.Silu, t_sz)):
        step(g1, 2)
        step(g2, 2)
    for _ in dense_tok(bk, 512, x_ready, evac_to(bk, lambda tb: MIX[:, tb, 0:512], ACT.Silu, t_z)):
        step(g1, 2)
        step(g2, 3)
    while step(g1):
        pass
    while step(g2):
        pass
    x_pe[0] = w_used[unit[0] - 1]

    MP = [zb(f"mp{c}", [128, 2, 512], F32, 4 * c) for c in range(4)]
    TT = MP
    AT = [zb(f"at{c}", [128, 2, 512], F32, 16 + 4 * c) for c in range(4)]

    def work(i, *at):
        return {n: f(f"{n.lower()}{i}", [128, 2, 512], F32, o) for n, (f, o) in zip(("XF", "DD", "DT"), at)}

    WORK = [work(0, (zb, 32), (zb, 36), (zb, 40)), work(1, (sb, 16), (sb, 20), (sb, 24)), work(2, (sb, 28), (sb, 32), (sb, 36)),
            work(3, (sb, 40), (sb, 44), (zb, 44))]
    O = zb("o", [128, 4, 512], F32, 104)
    PM = [zb(f"pm{i}", [128, 384], F32, 116 + 1.5 * i) for i in range(2)]
    PMT = [zb(f"pmt{i}", [128, 384], F32, 119 + 1.5 * i) for i in range(2)]
    SWO = zb("swo", [128, 512], F32, 122)
    OT = zb("ot", [128, 512], F32, 129)
    SCAN = [dict(VB=zb("vb0", [128, 512], F32, 32), KB_=zb("kb0", [128, 512], F32, 34), KD=zb("kd0", [128, 512], F32, 36),
                 NW=zb("nw0", [128, 512], F32, 38), VN=zb("vn0", [128, 512], F32, 40), S=zb("s0", [128, 512], F32, 112)),
            dict(VB=zb("vb1", [128, 512], F32, 42), KB_=zb("kb1", [128, 512], F32, 44), KD=zb("kd1", [128, 512], F32, 46),
                 NW=zb("nw1", [128, 512], F32, 64), VN=zb("vn1", [128, 512], F32, 66), S=zb("s1", [128, 512], F32, 124))]
    RO = small("ro", 16, [128, 4, 4])
    BI = Banks(bfree, (0, 1, 2, 3, 4))
    BA = (5, 6, 7)
    hs = lambda t_, h: t_[:, h * 128:(h + 1) * 128]
    v3 = lambda t_: t_[:].rearrange("p (h n) -> p h n", h=4)
    h3 = lambda ap: ap.rearrange("p (h n) -> p h n", h=4)
    bc4 = lambda ap: ap.unsqueeze(1).broadcast_to([128, 4, 128])
    b4r = lambda ap: ap.unsqueeze(2).broadcast_to([128, 4, 128])
    work_end = [None] * 4
    ti = [[None, None] for _ in range(4)]
    t_at = [[None, None] for _ in range(4)]

    def invert(cb):
        W = WORK[cb]
        fr = x_pe[0]
        cs = slice(cb * 128, (cb + 1) * 128)
        kT = lambda h: QK[:, 4 + h, cs]
        qT = lambda h: QK[:, h, cs]
        col = lambda t_, d, h: t_[:, d, cb, h:h + 1]
        gate = t_gate[0]
        XF, DD, DT = W["XF"], W["DD"], W["DT"]
        TG, EE, MB = DD, XF, DT
        mp, at = MP[cb], AT[cb]
        tri = (cf("triU"), cf("triL"))
        strict = (cf("SL"), cf("SU"))
        sub = lambda t_, d, h: t_[:, d, h * 128:(h + 1) * 128]
        two = range(2)
        br = [BI.take(), BI.take()]
        t = [None, None]
        for d in two:
            for h in range(4):
                tg = Q.put("dve", lambda e, d=d, h=h: e.tensor_scalar(sub(TG, d, h), tri[d], col(GG, d, h), None, ALU.mult),
                           [fr, c_in] + gate)
            t[d] = mm(psum[br[d]][:, :], cf("ones"), TG[:, d, :], True, True, [tg, bfree[br[d]]], True)
        yield
        te = [None, None]
        for d in two:
            for h in range(4):
                tg = Q.put("dve", lambda e, d=d, h=h: e.tensor_scalar(
                    sub(EE, d, h), hs(psum[br[d]], h), col(GC, d, h), 0.0, ALU.subtract, ALU.max), [t[d], fr])
            bfree[br[d]] = tg
            te[d] = Q.put("act", lambda e, d=d: e.activation(EE[:, d, :], EE[:, d, :], ACT.Exp, scale=-1.0), [tg])
        r_read = t
        bk_, bq = BI.take(), BI.take()
        for h in range(4):
            tk = mm(hs(psum[bk_], h), kT(h), kT(h), True, True, [t_qk[4 + h], bfree[bk_]], h == 3)
        for h in range(4):
            tq = mm(hs(psum[bq], h), kT(h), qT(h), True, True, [t_qk[h], bfree[bq]], h == 3)
        for d in two:
            ta = Q.put("dve", lambda e, d=d: e.tensor_tensor(h3(at[:, d, :]), h3(psum[bq][:, :]), bc4(tri[d]), ALU.mult), [tq, fr])
        bfree[bq] = ta
        yield
        tm = [None, None]
        for d in two:
            tb_ = Q.put("pool", lambda e, d=d: e.tensor_tensor(h3(MB[:, d, :]), h3(EE[:, d, :]), bc4(strict[d]), ALU.mult), [te[d], fr])
            for h in range(4):
                tm[d] = Q.put("dve", lambda e, d=d, h=h: e.scalar_tensor_tensor(
                    sub(mp, d, h), hs(psum[bk_], h), col(NBETA, d, h), sub(MB, d, h), ALU.mult, ALU.mult), [tb_, tk, fr])
        bfree[bk_] = tm[1]
        for d in two:
            be = BI.take()
            for h in range(4):
                tt = tr(hs(psum[be], h), sub(EE, d, h), [te[d], bfree[be]], h == 3)
            t_at[cb][d] = bfree[be] = Q.put("dve", lambda e, d=d, be=be: e.tensor_tensor(
                at[:, d, :], at[:, d, :], psum[be][:, :], ALU.mult), [ta, tt])
        tdd = [None, None]
        for d in two:
            tm[d] = Q.put("pool", lambda e, d=d: e.tensor_tensor(h3(mp[:, d, :]), h3(mp[:, d, :]), bc4(cf("ident")), ALU.add), [tm[d]])
        for d in two:
            tdd[d] = Q.put("pool", lambda e, d=d: e.tensor_tensor(h3(DD[:, d, :]), h3(mp[:, d, :]), bc4(cf("LM", 7 * (1 - d))), ALU.mult),
                           [r_read[d], tm[d]])
        yield
        tdt = [None, None]
        for d in two:
            b = BI.take()
            for h in range(4):
                t = tr(hs(psum[b], h), sub(mp, d, h), [tm[d], bfree[b]], h == 3)
            tdt[d] = bfree[b] = Q.put("dve", lambda e, d=d, b=b: e.tensor_tensor(
                h3(DT[:, d, :]), h3(psum[b][:, :]), bc4(cf("LM", 7 * d)), ALU.mult), [t])
        yield
        for lvl in range(1, 7):
            tx = [None, None]
            for d in two:
                b = BI.take()
                for h in range(4):
                    t = mm(hs(psum[b], h), sub(mp, d, h), sub(DT, d, h), True, True, [tdt[d], bfree[b]], h == 3)
                tx[d] = bfree[b] = Q.put("dve", lambda e, d=d, b=b, lvl=lvl: e.tensor_tensor(
                    h3(XF[:, d, :]), h3(psum[b][:, :]), bc4(cf("LM", 7 * d + lvl)), ALU.mult), [t, tt])
            yield
            dst = DT if lvl < 6 else TT[cb]
            for d in two:
                b = BI.take()
                for h in range(4):
                    t1 = mm(hs(psum[b], h), sub(DD, d, h), sub(XF, d, h), True, True, [tx[d], tdd[d], bfree[b]], h == 3)
                tdt[d] = bfree[b] = Q.put("act", lambda e, d=d, b=b, dst=dst: e.activation(dst[:, d, :], psum[b][:, :], ACT.Copy), [t1])
            if lvl < 6:
                for d in two:
                    b = BI.take()
                    for h in range(4):
                        t2 = mm(hs(psum[b], h), sub(XF, d, h), sub(DD, d, h), True, True, [bfree[b]], h == 3)
                    if d:
                        tdd[d] = bfree[b] = Q.put("act", lambda e, d=d, b=b: e.activation(DD[:, d, :], psum[b][:, :], ACT.Copy), [t2])
                    else:
                        tdd[d] = bfree[b] = Q.put("dve", lambda e, d=d, b=b: e.tensor_copy(DD[:, d, :], psum[b][:, :]), [t2])
            yield
        ti[cb][:] = tdt
        work_end[cb] = t1

    o_tok = [None] * 4
    s_tok = [None, None]
    kb_tok = [None, None]
    nw_tok = [None, None]
    scan_free = [[], []]

    def scan_keys(d, r, waits):
        cb = r if d == 0 else 3 - r
        W = SCAN[d]
        k3 = h3(KT[:, cb, :])
        gate = t_gate[0]
        w = waits + gate + [t_vt[cb], t_kt[cb]]
        if r:
            t = Q.put("pool", lambda e: e.tensor_tensor(v3(W["KB_"]), k3, b4r(BEG[:, d, cb, :]), ALU.mult), w)
        tv = Q.put("pool", lambda e: e.tensor_tensor(v3(W["VB"]), h3(VT[:, cb, :]), b4r(BETA[:, d, cb, :]), ALU.mult), w)
        td = Q.put("pool", lambda e: e.tensor_tensor(v3(W["KD"]), k3, b4r(EGL[:, d, cb, :]), ALU.mult), w) if r < 3 else None
        kb_tok[d] = (tv, td)
        if r:
            b = BI.take()
            for h in range(4):
                t = mm(hs(psum[b], h), hs(W["KB_"], h), TT[cb][:, d, h * 128:(h + 1) * 128], True, True, [t, ti[cb][d], bfree[b]], h == 3)
            nw_tok[d] = bfree[b] = Q.put("act", lambda e, b=b: e.activation(W["NW"][:], psum[b][:, :], ACT.Copy, scale=-1.0), [t] + waits)

    def scan_step(d, r):
        cb = r if d == 0 else 3 - r
        W = SCAN[d]
        cs = slice(cb * 128, (cb + 1) * 128)
        col = lambda t_, h: t_[:, d, cb, h:h + 1]
        th = lambda t_, h: t_[cb][:, d, h * 128:(h + 1) * 128]
        if r == 0:
            scan_keys(d, 0, scan_free[d])
        tvb, tkd = kb_tok[d]
        tw, ts = nw_tok[d], s_tok[d]
        b = BI.take()
        for h in range(4):
            t = mm(hs(psum[b], h), th(TT, h), hs(W["VB"], h), True, r == 0, [ti[cb][d], tvb, bfree[b]], h == 3 and r == 0)
            if r:
                t = mm(hs(psum[b], h), hs(W["NW"], h), hs(W["S"], h), False, True, [tw, ts], h == 3)
        tv = bfree[b] = Q.put("act", lambda e, b=b: e.activation(W["VN"][:], psum[b][:, :], ACT.Copy), [t] + scan_free[d])
        yield
        if r:
            bs = BI.take()
            for h in range(4):
                tqs = mm(hs(psum[bs], h), QK[:, h, cs], hs(W["S"], h), True, True, [ts, bfree[bs]] + t_qk[0:4], h == 3)
        if r < 3:
            b = BI.take()
            for h in range(4):
                t = mm(hs(psum[b], h), hs(W["KD"], h), hs(W["VN"], h), True, True, [tkd, tv, bfree[b]], h == 3)
            for h in range(4):
                if r:
                    t = Q.put("dve", lambda e, b=b, h=h: e.scalar_tensor_tensor(
                        hs(W["S"], h), hs(W["S"], h), col(EL, h), hs(psum[b], h), ALU.mult, ALU.add), [t, ts, tqs])
                else:
                    t = Q.put("dve", lambda e, b=b, h=h: e.tensor_copy(hs(W["S"], h), hs(psum[b], h)), [t] + scan_free[d])
            s_tok[d] = bfree[b] = t
        b = BI.take()
        for h in range(4):
            t = mm(hs(psum[b], h), th(AT, h), hs(W["VN"], h), True, True, [t_at[cb][d], tv, bfree[b]], h == 3)
        last = t
        ov_ = O[:, cb, :]
        if o_tok[cb] is None:
            t = bfree[b] = Q.put("act", lambda e, b=b: e.activation(ov_, psum[b][:, :], ACT.Copy), [t] + scan_free[d])
        else:
            t = bfree[b] = Q.put("dve", lambda e, b=b: e.tensor_tensor(ov_, ov_, psum[b][:, :], ALU.add), [t, o_tok[cb]])
        if r:
            for h in range(4):
                t = Q.put("dve", lambda e, h=h, bs=bs: e.scalar_tensor_tensor(
                    O[:, cb, h * 128:(h + 1) * 128], hs(psum[bs], h), col(EG, h), O[:, cb, h * 128:(h + 1) * 128],
                    ALU.mult, ALU.add), [t, tqs])
            bfree[bs] = t
        o_tok[cb] = t
        yield
        if r < 3:
            scan_keys(d, r + 1, [last])
        dn_free[d] = last
        yield

    dn_free = [None, None]

    t_mix = [[None, None] for _ in range(4)]
    ot_free = [None]

    def dn_post(cb):
        o3 = O[:, cb, :].rearrange("p (h n) -> p h n", h=4)
        t = Q.put("pool", lambda e: e.tensor_tensor(OT[:], O[:, cb, :], O[:, cb, :], ALU.mult), [o_tok[cb], ot_free[0]])
        ot_free[0] = t = Q.put("dve", lambda e: e.tensor_reduce(RO[:, cb, :], v3(OT), AX.X, ALU.add), [t])
        t = Q.put("act", lambda e: e.activation(RO[:, cb, :], RO[:, cb, :], ACT.Ln, bias=eps, scale=1.0 / 128), [t])
        t = Q.put("act", lambda e: e.activation(RO[:, cb, :], RO[:, cb, :], ACT.Exp, scale=-0.5), [t])
        t = Q.put("dve", lambda e: e.tensor_tensor(o3, o3, b4r(RO[:, cb, :]), ALU.mult), [t])
        t = Q.put("pool", lambda e: e.tensor_tensor(o3, o3, bc4(pr("dn_out_norm_w")), ALU.mult), [t])
        t_mix[cb][0] = Q.put("dve", lambda e: e.tensor_tensor(MIX[:, cb, 0:512], MIX[:, cb, 0:512], O[:, cb, :], ALU.mult),
                             [t, t_z[cb]])

    MX = small("mx", 32, [128, 4, 8])
    DEN = small("den", 32, [128, 4, 8])
    ES = small("es", 32, [128, 4, 8])
    t_ns = Q.put("dve", lambda e: e.tensor_scalar(NSINK[:], pr("swa_sinks"), -1.0, None, ALU.mult), [p_in])

    def swa():
        bs, bt, bo = BA
        pieces = [(qb, h) for qb in range(4) for h in range(8)]
        st = [dict() for _ in pieces]
        pm_free, pmt_free = [None, None], [None, None]
        swo_free = [None]
        for n in range(len(pieces) + 2):
            if n < len(pieces):
                qb, h = pieces[n]
                g, i = h // 4, h % 4
                k0, k1 = max(qb - 1, 0), min(qb + 1, 3)
                nk = (k1 - k0 + 1) * 128
                ps = slice(64 * g, 64 * g + 64)
                masks = ([(0, NLb)] if qb > 0 else []) + ([(nk - 128, NUb)] if qb < 3 else [])
                mm(psum[bs][:, 0:nk], SQT[ps, i, qb * 128:(qb + 1) * 128], SKT[ps, k0 * 128:(k1 + 1) * 128], True, True,
                   [t_swt[0], bfree[bs]])
                for m, (at, mask) in enumerate(masks):
                    t = mm(psum[bs][:, at:at + 128], IDb[:], mask[:], False, True, [t_id, t_nl], m == len(masks) - 1, True)
                mx = MX[:, qb, h:h + 1]
                t = Q.put("dve", lambda e, nk=nk, mx=mx: e.tensor_reduce(mx, psum[bs][:, 0:nk], AX.X, ALU.max, negate=True), [t])
                t = t_mx = Q.put("dve", lambda e, mx=mx, h=h: e.tensor_scalar(mx, mx, 0.125, NSINK[:, h:h + 1], ALU.mult, ALU.min), [t, t_ns])
                pm = PM[n % 2]
                t = bfree[bs] = Q.put("act", lambda e, nk=nk, mx=mx, pm=pm, qb=qb, h=h: e.activation(
                    pm[:, 0:nk], psum[bs][:, 0:nk], ACT.Exp, bias=mx, scale=0.125, accum_out=DEN[:, qb, h:h + 1]),
                    [t, pm_free[n % 2]])
                st[n].update(nk=nk, k0=k0, k1=k1, g=g, t=t, mx=t_mx)
                yield
            if 0 <= n - 1 < len(pieces):
                m = n - 1
                s = st[m]
                for k in range(s["nk"] // 128):
                    t = tr(psum[bt][:, k * 128:(k + 1) * 128], PM[m % 2][:, k * 128:(k + 1) * 128], [s["t"], bfree[bt]],
                           k == s["nk"] // 128 - 1)
                pm_free[m % 2] = t
                pt = PMT[m % 2]
                nk = s["nk"]
                if m % 2:
                    t = Q.put("act", lambda e, pt=pt, nk=nk: e.activation(pt[:, 0:nk], psum[bt][:, 0:nk], ACT.Copy), [t, pmt_free[m % 2]])
                else:
                    t = Q.put("dve", lambda e, pt=pt, nk=nk: e.tensor_copy(pt[:, 0:nk], psum[bt][:, 0:nk]), [t, pmt_free[m % 2]])
                s["tt"] = bfree[bt] = t
                yield
            if 0 <= n - 2 < len(pieces):
                m = n - 2
                s = st[m]
                qb, h = pieces[m]
                kn = s["k1"] - s["k0"] + 1
                for k in range(kn):
                    t = mm(psum[bo][:, h * 64:(h + 1) * 64], PMT[m % 2][:, k * 128:(k + 1) * 128],
                           SV[:, s["k0"] + k, s["g"] * 64:s["g"] * 64 + 64], k == 0, k == kn - 1,
                           [s["tt"], bfree[bo]] + t_sv, k == kn - 1)
                pmt_free[m % 2] = t
                if h == 7:
                    t1 = Q.put("dve", lambda e, qb=qb: e.tensor_tensor(ES[:, qb, :], pr("swa_sinks"), MX[:, qb, :], ALU.add), [t_ns, s["mx"]])
                    t1 = Q.put("act", lambda e, qb=qb: e.activation(ES[:, qb, :], ES[:, qb, :], ACT.Exp), [t1])
                    t1 = Q.put("dve", lambda e, qb=qb: e.tensor_tensor(DEN[:, qb, :], DEN[:, qb, :], ES[:, qb, :], ALU.add), [t1])
                    t1 = Q.put("dve", lambda e, qb=qb: e.reciprocal(DEN[:, qb, :], DEN[:, qb, :]), [t1])
                    rd = DEN[:, qb, :].unsqueeze(2).broadcast_to([128, 8, 64])
                    o8 = lambda ap: ap.rearrange("p (h n) -> p h n", h=8)
                    t = bfree[bo] = Q.put("dve", lambda e, rd=rd: e.tensor_tensor(o8(SWO[:]), o8(psum[bo][:, :]), rd, ALU.mult),
                                          [t, t1, swo_free[0]])
                    swo_free[0] = t_mix[qb][1] = Q.put("pool", lambda e, qb=qb: e.tensor_tensor(
                        MIX[:, qb, 512:1024], MIX[:, qb, 512:1024], SWO[:], ALU.mult), [t, t_sz[qb]])
                yield

    def both(cbs, i):
        for cb in cbs:
            yield from invert(cb, i)

    gs = swa()
    gi = [invert(cb) for cb in (0, 3, 1, 2)]
    for n in range(3):
        for m in range(n, 3):
            step(gi[n])
    live = True
    while live:
        live = False
        for g in gi:
            live = step(g) or live
            step(gs, 2)
    while step(gs):
        pass
    BI = Banks(bfree, range(8))
    swa_end = [t for m in t_mix for t in m if t]
    for d in range(2):
        scan_free[d] += work_end + [swa_end[-1]]
    for r in range(4):
        if r == 3:
            last_split[0] = NU
            ring_busy.extend(work_end)
            w_ahead(30)
        ga, gb = scan_step(0, r), scan_step(1, r)
        live = True
        while live:
            la = step(ga)
            lb = step(gb)
            live = la or lb
        if r >= 2:
            dn_post(3 - r)
            dn_post(r)
    t_dn = [dn_free[0], dn_free[1]]
    x_pe[0] = t_dn[1] if t_dn[1][1] > t_dn[0][1] else t_dn[0]

    s_x2 = sem("s_xagain")
    t_h = Q.dma("act", H[:], xv, s_x2, 16, [x_pe[0], s_tok[0], s_tok[1]])
    s_b2 = sem("s_b2")
    WS = zb("ws", [128, 8, 128], F32, 104)
    TB = zb("tb", [128, 896], F32, 108)
    SELF = zb("self", [96, 1024], F32, 112)
    SEL = zb("sel", [96, 8, 128], BF16, 116)
    done1 = [t for m in t_mix for t in m]
    Q.dma("act", WS[:], wsd, s_b2, 16, done1)
    Q.dma("act", TB[:], tbd, s_b2, 32)
    b2_in = Q.dma("act", SELF[:], seld, s_b2, 48)

    def split_mix(src, ready):
        done = []
        for k in range(8):
            b = G.take()
            for tb in range(4):
                t = tr(psum[b][:, tb * 128:(tb + 1) * 128], src[:, tb, k * 128:(k + 1) * 128],
                       [ready[tb][0 if k < 4 else 1], bfree[b]], tb == 3)
            t1 = Q.put("act", lambda e, b=b, k=k: e.activation(XH[:, k, :], psum[b][:, :], ACT.Copy), [t, x_pe[0]])
            t2 = bfree[b] = Q.put("dve", lambda e, b=b, k=k: e.tensor_tensor(
                XL[:, k, :], psum[b][:, :], XH[:, k, :].bitcast(F32), ALU.subtract), [t, t1, x_pe[0]])
            done.append(t2)
        return done

    def add_h(banks, n, done, wait):
        def f(tb, t):
            b = banks[tb]
            hv = H[:, tb, n * 512:(n + 1) * 512]
            done[tb] = bfree[b] = Q.put("dve", lambda e: e.tensor_tensor(hv, hv, psum[b][:, :], ALU.add), [t, wait])
        return f

    def out_proj(ready, wait):
        done = [None] * 4
        for n in range(2):
            bk = four()
            for _ in dense_tok(bk, 512, ready, add_h(bk, n, done, wait)):
                pass
        x_pe[0] = w_used[unit[0] - 1]
        return done

    G = Banks(bfree, range(8))
    ready = split_mix(MIX, t_mix)
    h_tok = out_proj(ready, t_h)

    XS2 = zb("xs2", [128, 4, 1024], F32, 48)
    QK2 = zb("qk2", [128, 8, 512], F32, 48)
    V2 = zb("v2", [128, 4, 512], F32, 64)
    U2 = zb("u2", [128, 4, 512], F32, 72)
    VG = zb("vg", [128, 4, 512], F32, 80)
    MIX2 = zb("mix2", [128, 4, 1024], F32, 88)
    WST = WS
    LF = zb("lf", [8, 512], F32, 118)
    LG = zb("lg", [8, 512], F32, 120)
    VSQ = zb("vsq", [128, 512], F32, 118)
    C3 = zb("c3", [96, 512], BF16, 122)
    P2 = [zb(f"p2{i}", [128, 512], F32, 123 + 2 * i) for i in range(2)]
    P2T = [zb(f"p2t{i}", [128, 512], F32, 127 + 2 * i) for i in range(2)]
    LT = small("lt", 32, [128, 4, 8])

    x_ready = norm_xt(1, "norm_mix_g_2", XS2, h_tok, None)
    t_sel = Q.put("dve", lambda e: e.tensor_copy(SEL[:].rearrange("p h n -> p (h n)"), SELF[:]), [b2_in])
    t_c3 = Q.put("dve", lambda e: e.memset(C3[:], 0.0))
    b = G.take()
    t = dense_ch(b, x_ready)
    t = Q.put("dve", lambda e, b=b: e.tensor_scalar(LF[:], psum[b][0:8, :], pp("b_forget_2", 0, 1, 8), None, ALU.add), [t, p_in])
    bfree[b] = t
    t = Q.put("dve", lambda e: e.scalar_tensor_tensor(LG[:], LF[:], -1.0, LF[:], ALU.mult, ALU.max), [t])
    t1 = Q.put("dve", lambda e: e.tensor_scalar(LF[:], LF[:], 0.0, None, ALU.min), [t])
    t = Q.put("act", lambda e: e.activation(LG[:], LG[:], ACT.Exp, scale=-1.0), [t])
    t = Q.put("act", lambda e: e.activation(LG[:], LG[:], ACT.Ln, bias=1.0), [t])
    t_lf = Q.put("dve", lambda e: e.tensor_tensor(LF[:], LF[:], LG[:], ALU.subtract), [t, t1])
    t_q2 = [None] * 8
    t_cs = [None]

    def cum_a():
        b = G.take()
        for tb in range(4):
            t = tr(psum[b][:, tb * 8:(tb + 1) * 8], LF[:, tb * 128:(tb + 1) * 128], [t_lf, bfree[b]], tb == 3)
        return Q.put("act", lambda e: e.activation(LT[:].rearrange("p t h -> p (t h)"), psum[b][:, 0:32], ACT.Copy), [t]), b

    def cum_b(t):
        b = G.take()
        for tb in range(4):
            n0 = tb * 128
            t1 = mm(psum[b][0:8, n0:512], LT[:, tb, :], TB[:, 384:896 - n0], tb == 0, True, [t, b2_in, bfree[b]], tb == 3, tb > 0)
        hi, mid, lo = C3[0:8, :], C3[32:40, :], C3[64:72, :]
        t = Q.put("dve", lambda e: e.tensor_copy(LF[:], psum[b][0:8, :]), [t1])
        bfree[b] = t
        t = Q.put("dve", lambda e: e.tensor_copy(hi, LF[:]), [t, t_c3])
        t = Q.put("dve", lambda e: e.tensor_tensor(LG[:], LF[:], hi, ALU.subtract), [t])
        t = Q.put("dve", lambda e: e.tensor_copy(mid, LG[:]), [t])
        t = Q.put("dve", lambda e: e.tensor_copy(LF[:], mid), [t])
        t = Q.put("dve", lambda e: e.tensor_tensor(LG[:], LG[:], LF[:], ALU.subtract), [t])
        t_cs[0] = Q.put("dve", lambda e: e.tensor_copy(lo, LG[:]), [t])

    for j in range(8):
        b = G.take()
        t = dense_ch(b, x_ready)
        if j == 1:
            tl, bl_ = cum_a()
            bfree[bl_] = tl
        if j == 3:
            cum_b(tl)
        t_q2[j] = bfree[b] = Q.put("act", lambda e, b=b, j=j: e.activation(QK2[:, j, :], psum[b][:, :], ACT.Copy), [t])

    t_v2, t_u2, t_vg = [None] * 4, [None] * 4, [None] * 4
    VSS = small("vss", 32, [128, 4, 8])
    t_m2 = [[None, None] for _ in range(4)]
    t_wst = []

    def gmlp():
        for half in range(2):
            w4 = WST[:, 4 * half:4 * half + 4, :]
            t_wst.append(Q.put("pool", lambda e, w4=w4: e.tensor_tensor(w4, w4, bc4(cf("triU")), ALU.mult), [b2_in, c_in]))
        vt = None
        for tb in range(4):
            t = Q.put("pool", lambda e, tb=tb: e.tensor_tensor(VSQ[:], VG[:, tb, :], VG[:, tb, :], ALU.mult), [t_vg[tb], vt, t_cs[0]])
            vt = Q.put("dve", lambda e, tb=tb: e.tensor_reduce(VSS[:, tb, :], VSQ[:].rearrange("p (g n) -> p g n", g=8), AX.X, ALU.add), [t])
        t = Q.put("act", lambda e: e.activation(VSS[:], VSS[:], ACT.Ln, bias=eps, scale=1.0 / 64), [vt])
        t = Q.put("act", lambda e: e.activation(VSS[:], VSS[:], ACT.Exp, scale=-0.5), [t])
        ready = []
        yield
        for tb in range(4):
            v8 = VG[:, tb, :].rearrange("p (g n) -> p g n", g=8)
            rs = VSS[:, tb, :].unsqueeze(2).broadcast_to([128, 8, 64])
            t1 = Q.put("pool", lambda e, tb=tb: e.tensor_tensor(VG[:, tb, :], VG[:, tb, :], pr("gmlp_norm_g_2"), ALU.mult), [vt])
            ready.append(Q.put("dve", lambda e, v8=v8, rs=rs: e.tensor_tensor(v8, v8, rs, ALU.mult), [t, t1]))
        yield
        for g in range(8):
            if g % 2 == 0:
                b = G2.take()
            o = psum[b][:, (g % 2) * 256:(g % 2) * 256 + 256]
            t = mm(o, WST[:, g, :], VG[:, :, g * 64:(g + 1) * 64], True, True, [bfree[b], ready[3]] + t_wst, True)
            u = U2[:, :, g * 64:(g + 1) * 64]
            m = MIX2[:, :, 512 + g * 64:512 + (g + 1) * 64]
            t = bfree[b] = Q.put("dve", lambda e, o=o, g=g, u=u, m=m: e.scalar_tensor_tensor(
                m, o.rearrange("p (t n) -> p t n", t=4), pp("b_spatial_2", g), u, ALU.add, ALU.mult), [t] + t_u2)
            yield
        for tb in range(4):
            t_m2[tb][1] = t

    MX2 = small("mx2", 32, [128, 4, 8])
    DN2 = small("dn2", 32, [128, 4, 8])

    def forget_attention(banks):
        bs, bt, bo = banks
        pieces = [(qb, h) for qb in range(4) for h in range(8)]
        st = [dict() for _ in pieces]
        p_free, pt_free = [None, None], [None, None]
        for n in range(len(pieces) + 2):
            if n < len(pieces):
                qb, h = pieces[n]
                nk = (qb + 1) * 128
                ps = slice(64 * (h % 2), 64 * (h % 2) + 64)
                mm(psum[bs][:, 0:nk], QK2[ps, h // 2, qb * 128:(qb + 1) * 128], QK2[ps, 4 + h // 2, 0:nk], True, False,
                   [bfree[bs]] + t_q2)
                mm(psum[bs][:, 0:nk], SEL[:, h, :], C3[:, 0:nk], False, True, [t_cs[0], t_sel])
                t = mm(psum[bs][:, nk - 128:nk], IDb[:], NUb[:], False, True, [t_id, t_nu], True, True)
                mx = MX2[:, qb, h:h + 1]
                t = Q.put("dve", lambda e, nk=nk, mx=mx: e.tensor_reduce(mx, psum[bs][:, 0:nk], AX.X, ALU.max, negate=True), [t])
                t = Q.put("dve", lambda e, mx=mx: e.tensor_scalar(mx, mx, 0.125, None, ALU.mult), [t])
                pm = P2[n % 2]
                t = bfree[bs] = Q.put("act", lambda e, nk=nk, mx=mx, pm=pm, qb=qb, h=h: e.activation(
                    pm[:, 0:nk], psum[bs][:, 0:nk], ACT.Exp, bias=mx, scale=0.125, accum_out=DN2[:, qb, h:h + 1]),
                    [t, p_free[n % 2]])
                st[n].update(nk=nk, t=t)
                yield
            if 0 <= n - 1 < len(pieces):
                m = n - 1
                s = st[m]
                nk = s["nk"]
                for k in range(nk // 128):
                    t = tr(psum[bt][:, k * 128:(k + 1) * 128], P2[m % 2][:, k * 128:(k + 1) * 128], [s["t"], bfree[bt]],
                           k == nk // 128 - 1)
                p_free[m % 2] = t
                pt = P2T[m % 2]
                if m % 2:
                    t = Q.put("act", lambda e, pt=pt, nk=nk: e.activation(pt[:, 0:nk], psum[bt][:, 0:nk], ACT.Copy), [t, pt_free[m % 2]])
                else:
                    t = Q.put("dve", lambda e, pt=pt, nk=nk: e.tensor_copy(pt[:, 0:nk], psum[bt][:, 0:nk]), [t, pt_free[m % 2]])
                s["tt"] = bfree[bt] = t
                yield
            if 0 <= n - 2 < len(pieces):
                m = n - 2
                s = st[m]
                qb, h = pieces[m]
                for k in range(qb + 1):
                    t = mm(psum[bo][:, h * 64:(h + 1) * 64], P2T[m % 2][:, k * 128:(k + 1) * 128],
                           V2[:, k, h * 64:(h + 1) * 64], k == 0, k == qb, [s["tt"], bfree[bo]] + t_v2, k == qb)
                pt_free[m % 2] = t
                if h == 7:
                    t1 = Q.put("dve", lambda e, qb=qb: e.reciprocal(DN2[:, qb, :], DN2[:, qb, :]), [s["t"]])
                    rd = DN2[:, qb, :].unsqueeze(2).broadcast_to([128, 8, 64])
                    o8 = lambda ap: ap.rearrange("p (h n) -> p h n", h=8)
                    t_m2[qb][0] = bfree[bo] = Q.put("dve", lambda e, rd=rd, qb=qb: e.tensor_tensor(
                        o8(MIX2[:, qb, 0:512]), o8(psum[bo][:, :]), rd, ALU.mult), [t, t1])
                yield

    bk = four()
    for _ in dense_tok(bk, 512, x_ready, evac_to(bk, lambda tb: V2[:, tb, :], ACT.Copy, t_v2)):
        pass
    G2 = Banks(bfree, (3, 7))
    ga = forget_attention((4, 5, 6))
    bk = [0, 1, 2, 3]
    for _ in dense_tok(bk, 512, x_ready, evac_to(bk, lambda tb: U2[:, tb, :], ACT.Gelu_apprx_tanh, t_u2)):
        step(ga, 8)
    for _ in dense_tok(bk, 512, x_ready, evac_to(bk, lambda tb: VG[:, tb, :], ACT.Gelu_apprx_tanh, t_vg)):
        step(ga, 8)
    x_pe[0] = w_used[unit[0] - 1]
    gg = gmlp()
    live = True
    while live:
        la = step(ga, 3)
        lb = step(gg)
        live = la or lb

    ready = split_mix(MIX2, t_m2)
    h_tok = out_proj(ready, None)

    XS3 = zb("xs3", [128, 4, 1024], F32, 92)
    AC = zb("ac", [128, 22, 512], F32, 48)
    TA = [zb(f"ta{i}", [128, 512], F32, 92 + 2 * i) for i in range(2)]
    TGG = [zb(f"tgg{i}", [128, 512], F32, 96 + 2 * i) for i in range(2)]
    AH = [zb(f"ah{i}", [128, 512], F32R, 108 + 2 * i) for i in range(4)]
    AL = [zb(f"al{i}", [128, 512], F32R, 116 + 2 * i) for i in range(4)]

    x_ready = norm_xt(2, "norm_ffn_g_2", XS3, h_tok, None)
    FG = zb("fg", [128, 1024], F32, 124)
    a, w = PR["norm_final_g_2"]
    s_fg = sem("s_fg")
    t_fg = Q.dma("sp", FG[:], prd[a:a + w].partition_broadcast(128), s_fg, 16, [x_ready[7]])
    ta_free = [x_ready[7], x_ready[7]]
    tg_free = [x_ready[7], x_ready[7]]

    def conv3(c, dst, bank, t, free):
        wc = lambda i: pp("conv_w_2", i * 44 + c)
        bias = pp("conv_b_2", c)
        t = Q.put("act", lambda e: e.activation(dst[:], psum[bank][:, :], ACT.Identity, scale=wc(2), bias=bias), [t, free, p_in])
        for i in (0, 1):
            sh = 2 - i
            t = Q.put("dve", lambda e, i=i, sh=sh: e.scalar_tensor_tensor(
                dst[:, sh:T], psum[bank][:, 0:T - sh], wc(i), dst[:, sh:T], ALU.mult, ALU.add), [t, p_in])
        bfree[bank] = t
        return t

    t_ac = [None] * 22

    def up_post(j, b1, t1, b2, t2):
        ta, tg = TA[j % 2], TGG[j % 2]
        t1 = conv3(j, ta, b1, t1, ta_free[j % 2])
        t2 = conv3(22 + j, tg, b2, t2, tg_free[j % 2])
        t2 = Q.put("act", lambda e: e.activation(tg[:], tg[:], ACT.Silu), [t2])
        t_ac[j] = ta_free[j % 2] = tg_free[j % 2] = Q.put(
            "dve", lambda e: e.tensor_tensor(AC[:, j, :], ta[:], tg[:], ALU.mult), [t1, t2])

    pend = None
    for j in range(22):
        b1 = G.take()
        t1 = dense_ch(b1, x_ready)
        if pend:
            up_post(*pend)
        b2 = G.take()
        t2 = dense_ch(b2, x_ready)
        pend = (j, b1, t1, b2, t2)
    up_post(*pend)

    a_used = [None] * 4
    a_split = [None] * 22

    def a_prep(k):
        ah, al = AH[k % 4], AL[k % 4]
        t = Q.put("act", lambda e: e.activation(ah[:], AC[:, k, :], ACT.Copy), [t_ac[k], a_used[k % 4], x_ready[7]])
        a_split[k] = Q.put("dve", lambda e: e.tensor_tensor(al[:], AC[:, k, :], ah[:].bitcast(F32), ALU.subtract),
                           [t, t_ac[k], a_used[k % 4]])

    a_prep(0)
    a_prep(1)
    hd = [None] * 4
    s_out = sem("s_out")
    ov = out.rearrange("b (t p) d -> (b p) t d", p=128)
    OUT = zb("outt", [128, 4, 1024], F32, 0)

    def finish(tb):
        t = row_rstd(0, tb, H[:, tb, :], OUT[:, tb, :], [hd[tb], w_used[unit[0] - 1]])
        t = Q.put("dve", lambda e: e.scalar_tensor_tensor(OUT[:, tb, :], H[:, tb, :], RS[0][:, tb:tb + 1], FG[:],
                                                          ALU.mult, ALU.mult), [t, t_fg])
        Q.dma("sp", ov[:, tb, :], OUT[:, tb, :], s_out, 16 * (tb + 1), [t])

    order = [(tb, n) for tb in range(4) for n in range(2)]
    for k in range(22):
        u = unit[0]
        unit[0] += 1
        w_ahead(u + 2)
        if k + 2 < 22:
            a_prep(k + 2)
        for i, (tb, n) in enumerate(order):
            ts = slice(tb * 128, (tb + 1) * 128)
            c = slice(n * 512, (n + 1) * 512)
            t = mm3(psum[i][:, :], AH[k % 4][:, ts], AL[k % 4][:, ts], WH[u % NS][:, c], WL[u % NS][:, c], k == 0, k == 21,
                    [w_split[u], a_split[k]] + ([bfree[i]] if k == 0 else []), k == 21 or i == 7)
            if k == 21:
                hv = H[:, tb, c]
                hd[tb] = Q.put("dve", lambda e, hv=hv, i=i: e.tensor_tensor(hv, hv, psum[i][:, :], ALU.add), [t])
        w_used[u] = a_used[k % 4] = t
    for tb in range(4):
        finish(tb)
    Q.put("sp", lambda e: e.wait_ge(s_out, 64), (), inc=False)

    with nc.Block() as block:
        @block.sync
        def _(e):
            for f in Q.q["sp"]:
                f(e)

        @block.scalar
        def _(e):
            for f in Q.q["act"]:
                f(e)

        @block.vector
        def _(e):
            for f in Q.q["dve"]:
                f(e)

        @block.gpsimd
        def _(e):
            for f in Q.q["pool"]:
                f(e)

        @block.tensor
        def _(e):
            for f in Q.q["pe"]:
                f(e)


def lay_out(a):
    mats = {k: a[k][0] for k in ("w_in", "w_out", "w_in_2", "w_out_2", "w_up_2", "w_down_2")}
    pp = np.zeros((128, NPP), np.float32)

    def put(name, v):
        at, w = PP[name]
        pp[:v.shape[0], at:at + w] = v

    for n in ("norm_w", "norm_mix_g_2", "norm_ffn_g_2"):
        put(n, a[n].reshape(8, 128).T)
    put("dn_conv_w", a["dn_conv_w"][0].reshape(5, 12, 128).transpose(2, 1, 0).reshape(128, 60))
    put("conv_w_2", a["conv_w_2"][0].reshape(3, 44, 128).transpose(2, 0, 1).reshape(128, 132))
    put("conv_b_2", a["conv_b_2"][0].reshape(44, 128).T)
    put("b_spatial_2", a["b_spatial_2"][0].T)
    put("b_forget_2", a["b_forget_2"][0].reshape(8, 1))
    pr = np.concatenate([a[n].reshape(-1) for n in PR])
    ws = np.ascontiguousarray(a["w_spatial_2"][0].transpose(2, 0, 1))
    return dict(x=np.ascontiguousarray(a["x"]), wflat=pack_weights(mats), cf=const_tile(), pp=pp, pr=pr, ws=ws,
                tb=tri_big(), sel=sel_tile())


def kernel(**inputs):
    import concourse.bacc as bacc
    from concourse.bass_utils import run_bass_kernel_spmd

    arrays = lay_out({k: np.asarray(v) for k, v in inputs.items()})
    nc = bacc.Bacc("TRN2", target_bir_lowering=False, num_devices=1)
    maps, args = {}, {}
    for name, v in arrays.items():
        maps["in_" + name] = v
        args[name] = nc.dram_tensor("in_" + name, v.shape, mybir.dt.from_np(v.dtype), kind="ExternalInput").ap()
    o = nc.dram_tensor("out_0", (1, T, D), F32, kind="ExternalOutput").ap()
    program(nc, args["x"], args["wflat"], args["cf"], args["pp"], args["pr"], args["ws"], args["tb"], args["sel"], o)
    r = run_bass_kernel_spmd(nc, [maps], core_ids=[0])
    return r.results[0]["out_0"]
```

```python
import math

import numpy as np

import concourse.bass as bass
from concourse import mybir

F32 = mybir.dt.float32
F32R = mybir.dt.float32r
BF16 = mybir.dt.bfloat16
ALU = mybir.AluOpType
ACT = mybir.ActivationFunctionType
AX = mybir.AxisListType

KB = 1024
BASE = 16512
EPS = 1e-6
NEG = -1e30
D = 1024
T = 512

P1_CH = [(j * 128, 128) for j in range(12)]
P1_TOK = [[(2048, 16), (2576, 256)], [(2064, 512)], [(2832, 512)], [(1536, 512)]]
P2_CH = [(j * 128, 128) for j in range(8)]
P2_TOK = [(1024, 512), (1536, 512), (2048, 512)]

MIX_K = (4, 6, 0, 2)


def unit_plan():
    plan = []
    for c in P1_CH:
        plan.append(("w_in", range(8), [c], 128))
    for cols in P1_TOK:
        n = sum(w for _, w in cols)
        for k in range(0, 8, 2):
            plan.append(("w_in", range(k, k + 2), cols, n))
    for n in range(2):
        for k in MIX_K:
            plan.append(("w_out", range(k, k + 2), [(n * 512, 512)], 512))
    tok2 = [("w_in_2", range(k, k + 2), [c], 512) for c in P2_TOK for k in range(0, 8, 2)]
    plan += tok2[:4]
    plan.append(("w_in_2", range(8), [(2560, 8)], 128))
    for c in P2_CH:
        plan.append(("w_in_2", range(8), [c], 128))
    plan += tok2[4:]
    for n in range(2):
        for k in range(0, 8, 2):
            plan.append(("w_out_2", range(k, k + 2), [(n * 512, 512)], 512))
    for j in range(22):
        for half in range(2):
            plan.append(("w_up_2", range(8), [(half * 2816 + j * 128, 128)], 128))
    for k in range(22):
        plan.append(("w_down_2", range(k, k + 1), [(0, 1024)], 1024))
    return plan


def pack_weights(mats):
    parts = []
    for name, ks, cols, width in unit_plan():
        m = mats[name]
        u = np.zeros((128, len(ks), width), np.float32)
        for i, k in enumerate(ks):
            at = 0
            for c, w in cols:
                u[:, i, at:at + w] = m[k * 128:(k + 1) * 128, c:c + w]
                at += w
        parts.append(u.reshape(-1))
    return np.concatenate(parts)


CF = {}
_at = 0
for _name, _w in (("ident", 128), ("triU", 128), ("triL", 128), ("SL", 128), ("SU", 128), ("ones", 128),
                  ("LM", 14 * 128), ("cos", 256), ("sin", 256)):
    CF[_name] = (_at, _w)
    _at += _w
NCF = _at


def const_tile():
    c = np.zeros((128, NCF), np.float32)
    i = np.arange(128)[:, None]
    j = np.arange(128)[None, :]
    put = lambda name, v: c.__setitem__((slice(None), slice(CF[name][0], CF[name][0] + CF[name][1])), v)
    put("ident", i == j)
    put("triU", i <= j)
    put("triL", i >= j)
    put("SL", i > j)
    put("SU", i < j)
    put("ones", 1.0)
    lm = []
    for d in range(2):
        for lvl in range(7):
            s = 1 << lvl
            a, b = (i, j) if d == 0 else (j, i)
            lm.append(((a // (2 * s) == b // (2 * s)) & ((a // s) % 2 == 0) & ((b // s) % 2 == 1)) | (i == j))
    put("LM", np.concatenate(lm, axis=1))
    inv = (np.float32(10000.0) ** (-np.arange(0, 64, 2, dtype=np.float32) / np.float32(64))).astype(np.float32)
    ang = np.arange(512, dtype=np.float32)[:, None] * inv[None, :]
    cos = np.cos(ang.astype(np.float64)).astype(np.float32)
    sin = np.sin(ang.astype(np.float64)).astype(np.float32)
    tok = lambda a: a.reshape(4, 128, 64).transpose(1, 0, 2).reshape(128, 256)
    put("cos", tok(np.concatenate([cos, cos], axis=1)))
    put("sin", tok(np.concatenate([-sin, sin], axis=1)))
    return c


def tri_big():
    j = np.arange(896)[None, :]
    return (j >= np.arange(128)[:, None] + 384).astype(np.float32)


def sel_tile():
    s = np.zeros((96, 8, 128), np.float32)
    for h in range(8):
        for part in range(3):
            s[32 * part + h, h, :] = -8.0
    return s.reshape(96, 1024)


PP = {"dn_conv_w": (24, 60),
      "conv_w_2": (84, 132), "conv_b_2": (216, 44), "b_spatial_2": (260, 8), "b_forget_2": (268, 1)}
NPP = 272
PR = {"dn_a_log": (0, 8), "dn_dt_bias": (8, 8), "swa_sinks": (16, 8), "dn_out_norm_w": (24, 128),
      "swa_q_norm_w": (152, 64), "swa_k_norm_w": (216, 64), "gmlp_norm_g_2": (280, 512), "norm_final_g_2": (792, 1024),
      "norm_w": (1816, 1024), "norm_mix_g_2": (2840, 1024), "norm_ffn_g_2": (3864, 1024)}
NPR = 792


class Queues:

    def __init__(self, nc):
        self.q = {e: [] for e in ("pe", "act", "dve", "pool", "sp")}
        self.sem = {e: nc.alloc_semaphore("done_" + e) for e in self.q}
        self.n = dict.fromkeys(self.q, 0)
        self.waited = {e: {} for e in self.q}

    def put(self, eng, fn, waits=(), inc=True):
        for w in waits:
            if w is not None:
                sem, value = w
                if self.waited[eng].get(sem.name, 0) < value:
                    self.waited[eng][sem.name] = value
                    self.q[eng].append(lambda e, sem=sem, value=value: e.wait_ge(sem, value))
        if not inc:
            self.q[eng].append(fn)
            return None
        self.n[eng] += 1
        sem = self.sem[eng]
        self.q[eng].append(lambda e: fn(e).then_inc(sem, 1))
        return (sem, self.n[eng])

    def dma(self, eng, out, in_, sem, value, waits=()):
        self.put(eng, lambda e: e.dma_start(out, in_).then_inc(sem, 16), waits, inc=False)
        return (sem, value)


class BankFree(list):

    def __init__(self):
        super().__init__([None] * 8)
        self.held = set()

    def __setitem__(self, b, token):
        super().__setitem__(b, token)
        self.held.discard(b)


class Banks:

    def __init__(self, free, ids):
        self.free, self.ids, self.i = free, list(ids), 0

    def take(self):
        for _ in self.ids:
            b = self.ids[self.i % len(self.ids)]
            self.i += 1
            if b not in self.free.held:
                self.free.held.add(b)
                return b
        raise AssertionError("no bank is free")


def program(nc, x, wflat, cfd, ppd, prd, wsd, tbd, seld, out):
    Q = Queues(nc)
    psum = [nc.alloc_psum_tensor(f"bank{i}", [128, 512], F32) for i in range(8)]
    bfree = BankFree()

    def sb(name, shape, dt, kb):
        return nc.alloc_sbuf_tensor_at(name, shape, dt, offset=BASE + int(round(kb * KB)))

    def sem(name):
        return nc.alloc_semaphore(name)

    NS = 4
    RAW = [sb(f"raw{i}", [128, 1024], F32, 4 * i) for i in range(NS)]
    WH = [sb(f"wh{i}", [128, 1024], F32R, 16 + 4 * i) for i in range(NS)]
    WL = [sb(f"wl{i}", [128, 1024], F32R, 32 + 4 * i) for i in range(NS)]
    C0 = 48
    CT = sb("consts", [128, NCF], F32, C0)
    PT_ = sb("pparams", [128, NPP], F32, C0 + 12)
    RT = sb("rparams", [128, NPR], F32, C0 + 13.125)
    NUb = sb("nub", [128, 128], BF16, C0 + 20.25)
    NLb = sb("nlb", [128, 128], BF16, C0 + 20.5)
    IDb = sb("idb", [128, 128], BF16, C0 + 20.75)
    CE = sb("ceps", [128, 2], F32, C0 + 22.5)
    small_at = [C0 + 22.625]

    def small(name, cols, shape=None):
        t = sb(name, shape or [128, cols], F32, small_at[0])
        small_at[0] += ((cols * 4 + 31) // 32 * 32) / KB
        assert small_at[0] <= C0 + 28
        return t

    Z0 = C0 + 28

    def zb(name, shape, dt, kb):
        n = 1
        for s in shape[1:]:
            n *= s
        assert kb + n * (2 if dt == BF16 else 4) / KB <= 131.8, name
        return sb(name, shape, dt, Z0 + kb)

    def cf(name, i=0):
        a, w = CF[name]
        return CT[:, a + 128 * i:a + 128 * (i + 1)] if name == "LM" else CT[:, a:a + w]

    def pp(name, i=0, n=1, parts=128):
        a, _ = PP[name]
        return PT_[0:parts, a + i:a + i + n]

    def pr(name):
        a, w = PR[name]
        return RT[:, a:a + w]

    XH = zb("xh", [128, 8, 512], F32R, 0)
    XL = zb("xl", [128, 8, 512], F32R, 16)
    H = zb("h", [128, 4, 1024], F32, 32)

    s_c = sem("s_const")
    s_p = sem("s_params")
    s_x = [sem(f"s_x{i}") for i in range(4)]
    xv = x.rearrange("b (t p) d -> (b p) t d", p=128)
    s_id = sem("s_ident")
    s_g = sem("s_gain")
    c_id = Q.dma("act", CT[:, 0:128], cfd[:, 0:128], s_id, 16)
    def x_load(tb, waits=()):
        Q.dma("sp", H[:, tb, :], xv[:, tb, :], s_x[tb], 16, waits)

    x_load(0)
    x_load(1)
    GAIN = sb("gain", [128, 1024], F32, C0 + 16.25)
    gains = [0]

    def load_gain(name, waits, eng="sp"):
        a, w = PR[name]
        gains[0] += 16
        return Q.dma(eng, GAIN[:], prd[a:a + w].partition_broadcast(128), s_g, gains[0], waits)

    x_in = [(s_x[tb], 16) for tb in range(4)]
    t_gain = load_gain("norm_w", [x_in[0]], "act")
    c_in = (s_c, 16)
    p_in = (s_p, 32)

    plan = unit_plan()
    NU = len(plan)
    s_w = [sem(f"s_w{i}") for i in range(NS)]
    widths = [len(ks) * width for _, ks, _, width in plan]
    starts = [128 * sum(widths[:u]) for u in range(NU)]
    w_read = [None] * NU
    w_split = [None] * NU
    w_used = [None] * NU
    issued = [0, 0]
    last_split = [27]
    ring_busy = []

    def w_load(u):
        src = wflat[starts[u]:starts[u] + 128 * widths[u]].rearrange("(p n) -> p n", p=128)
        Q.dma("sp", RAW[u % NS][:, 0:widths[u]], src, s_w[u % NS], 16 * (u // NS + 1),
              [w_read[u - NS] if u >= NS else None])

    def w_prep(u):
        n = widths[u]
        raw, hi, lo = RAW[u % NS][:, 0:n], WH[u % NS][:, 0:n], WL[u % NS][:, 0:n]
        there = (s_w[u % NS], 16 * (u // NS + 1))
        free = w_used[u - NS] if u >= NS else None
        t = Q.put("act", lambda e: e.activation(hi, raw, ACT.Copy), [there, free] + ring_busy)
        t = Q.put("pool", lambda e: e.tensor_tensor(lo, raw, hi.bitcast(F32), ALU.subtract), [there, t, free])
        w_read[u] = w_split[u] = t

    def w_ahead(u):
        u = min(u, last_split[0], NU - 1)
        while issued[1] <= u:
            while issued[0] < min(issued[1] + NS, NU):
                w_load(issued[0])
                issued[0] += 1
            w_prep(issued[1])
            issued[1] += 1
        while issued[0] < min(issued[1] + NS, NU):
            w_load(issued[0])
            issued[0] += 1

    unit = [0]

    def mm(out_, l, r, start, stop, waits=(), inc=False, part=False):
        return Q.put("pe", lambda e: e.matmul(out_, l, r, start=start, stop=stop, skip_group_check=part), waits, inc)

    def tr(out_, in_, waits=(), inc=False):
        idn = cf("ident")[0:in_.shape[0], 0:in_.shape[0]]
        return Q.put("pe", lambda e: e.transpose(out_, in_, idn), list(waits) + [c_id], inc)

    def mm3(o, lh, ll, rh, rl, start, stop, waits=(), inc=False):
        mm(o, lh, rh, start, False, waits)
        mm(o, lh, rl, False, False)
        return mm(o, ll, rh, False, stop, (), inc)

    def dense_ch(bank, x_ready, halves=1):
        u = unit[0]
        unit[0] += 1
        w_ahead(u + 2)
        w = [w_split[u], bfree[bank]]
        n = T // halves
        for half in range(halves):
            ts = slice(half * n, (half + 1) * n)
            for k in range(8):
                c = slice(k * 128, (k + 1) * 128)
                t = mm3(psum[bank][:, ts], WH[u % NS][:, c], WL[u % NS][:, c], XH[:, k, ts], XL[:, k, ts], k == 0, k == 7,
                        w + x_ready[k][half * 4 // halves:(half + 1) * 4 // halves], k == 7)
        w_used[u] = t
        return t

    def dense_tok(banks, n, x_ready, evac, slot=range(8), ks=range(0, 8, 2), late=None):
        for k0 in ks:
            u = unit[0]
            unit[0] += 1
            w_ahead(u + 2)
            for tb in range(4):
                if late and k0 == ks[0] and tb > 1:
                    late(tb)
                for k in range(2):
                    c = slice(k * n, (k + 1) * n)
                    ts = slice(tb * 128, (tb + 1) * 128)
                    x = slot[k0 + k]
                    w = [w_split[u], x_ready[x][tb]] + ([bfree[banks[tb]]] if k0 + k == ks[0] else [])
                    t = mm3(psum[banks[tb]][:, 0:n], XH[:, x, ts], XL[:, x, ts], WH[u % NS][:, c],
                            WL[u % NS][:, c], k0 + k == ks[0], k0 + k == ks[-1] + 1, w, k == 1)
                if k0 == ks[-1]:
                    evac(tb, t)
            w_used[u] = t
            yield

    def dense_last(n, x_ready, slot, ks, evac, between):
        u0 = unit[0]
        unit[0] += 4
        banks = [G.take() for _ in range(4)]

        def go(i, tb):
            ts = slice(tb * 128, (tb + 1) * 128)
            for k in range(2):
                c = slice(k * n, (k + 1) * n)
                x = slot[ks[i] + k]
                t = mm3(psum[banks[tb]][:, 0:n], XH[:, x, ts], XL[:, x, ts], WH[(u0 + i) % NS][:, c], WL[(u0 + i) % NS][:, c],
                        i + k == 0, i + k == 4, [w_split[u0 + i], x_ready[x][tb], bfree[banks[tb]] if i + k == 0 else None], k == 1)
            return t

        w_ahead(u0 + 2)
        for tb in range(4):
            w_used[u0] = go(0, tb)
        w_ahead(u0 + 3)
        for tb in range(4):
            for i in (1, 2, 3):
                w_used[u0 + i] = t = go(i, tb)
            evac(banks[tb], tb, t)
            between(tb)
            if tb == 1:
                w_ahead(u0 + 4)

    t_ce = Q.put("dve", lambda e: e.memset(CE[:, 0:1], EPS))
    eps = CE[:, 0:1]
    Q.put("act", lambda e: e.activation(CE[:, 1:2], eps, ACT.Sqrt), [t_ce])
    Q.put("sp", lambda e: e.wait_ge(s_x[0], 16), (), inc=False)
    w_load(0)
    x_load(2)
    x_load(3, [x_in[1]])
    issued[0] = 1
    Q.put("sp", lambda e: e.wait_ge(s_x[2], 16), (), inc=False)
    while issued[0] < NS:
        w_load(issued[0])
        issued[0] += 1
    Q.dma("sp", PT_[:], ppd, s_p, 16)
    Q.dma("sp", CT[:, 128:NCF], cfd[:, 128:NCF], s_c, 16)
    Q.dma("sp", RT[:], prd[0:NPR].partition_broadcast(128), s_p, 32)

    SS = [small(f"ss{i}", 4) for i in range(3)]
    RS = [small(f"rs{i}", 4) for i in range(3)]

    def root(dst, src, scale, waits):
        return Q.put("act", lambda e: e.activation(dst, src, ACT.Sqrt, bias=eps, scale=scale), list(waits) + [t_ce])

    def norm_stats(i, tb, XS, waits):
        t = Q.put("act", lambda e: e.activation(XS[:, tb, :], H[:, tb, :], ACT.Square, accum_out=SS[i][:, tb:tb + 1]), waits)
        return root(RS[i][:, tb:tb + 1], SS[i][:, tb:tb + 1], 1.0 / D, [t])

    def norm_scale(i, tb, XS, t):
        t = Q.put("dve", lambda e: e.reciprocal(RS[i][:, tb:tb + 1], RS[i][:, tb:tb + 1]), [t])
        return Q.put("dve", lambda e: e.scalar_tensor_tensor(XS[:, tb, :], H[:, tb, :], RS[i][:, tb:tb + 1], GAIN[:],
                                                             ALU.mult, ALU.mult), [t, t_gain])

    x_pe = [None] * 4

    def split_t(src, tb, half, ready, slot, x_ready):
        b = G.take()
        for i in range(4):
            k = half * 4 + i
            t = tr(psum[b][:, i * 128:(i + 1) * 128], src[:, tb, k * 128:(k + 1) * 128], [ready, bfree[b]], i == 3)
        places = [slot[half * 4 + i] for i in range(4)]
        ts = slice(tb * 128, (tb + 1) * 128)

        def at(X):
            if places[3] == places[0] + 3:
                return X[:, places[0]:places[0] + 4, ts]
            return X[:].rearrange("p (a b) n -> p a b n", b=2)[:, places[0] // 2:places[2] // 2 + 1:(places[2] - places[0]) // 2, :, ts]

        p4 = psum[b][:, :].rearrange("p (k n) -> p k n", k=4)
        if places[3] != places[0] + 3:
            p4 = psum[b][:, :].rearrange("p (a b n) -> p a b n", a=2, b=2)
        t1 = Q.put("act", lambda e: e.activation(at(XH), p4, ACT.Copy), [t, x_pe[tb]])
        t2 = bfree[b] = Q.put("dve", lambda e: e.tensor_tensor(at(XL), p4, at(XH).bitcast(F32), ALU.subtract), [t, t1, x_pe[tb]])
        for x in places:
            x_ready[x][tb] = t2

    def no_tiles():
        return [[None] * 4 for _ in range(8)]

    def norm_b(tb, XS, t, x_ready):
        for half in range(2):
            split_t(XS, tb, half, t, range(8), x_ready)

    G = Banks(bfree, range(8))

    XS1 = zb("xs1", [128, 4, 1024], F32, 88)
    QK = zb("qk", [128, 8, 512], F32, 48)
    VC = zb("vc", [128, 4, 512], F32, 64)
    KT = zb("kt", [128, 4, 512], F32, 72)
    VT = zb("vt", [128, 4, 512], F32, 80)
    MIX = zb("mix", [128, 4, 1024], F32, 88)
    SWR = zb("swr", [128, 4, 640], F32, 104)
    SV = zb("sv", [128, 4, 128], F32, 114)
    R1 = zb("r1", [128, 640], F32, 122)
    R2 = zb("r2", [128, 640], F32, 124.5)
    SKT = zb("skt", [128, 512], F32, 127)
    SQT = zb("sqt", [128, 4, 512], F32, 64)
    BD = small("bd", 64, [128, 4, 16])

    x_ready = no_tiles()
    ts = [None] * 4
    for tb in range(5):
        if tb < 4:
            ts[tb] = norm_scale(0, tb, XS1, norm_stats(0, tb, XS1, [x_in[tb]]))
        if tb == 1:
            w_ahead(0)
        if tb:
            norm_b(tb - 1, XS1, ts[tb - 1], x_ready)
    t_nu = Q.put("dve", lambda e: e.tensor_scalar(NUb[:], cf("SU"), NEG, None, ALU.mult), [c_in])
    t_nl = Q.put("dve", lambda e: e.tensor_scalar(NLb[:], cf("SL"), NEG, None, ALU.mult))
    t_id = Q.put("dve", lambda e: e.tensor_copy(IDb[:], cf("ident")))

    def conv5(j, dst, bank, t):
        wc = lambda i: pp("dn_conv_w", j * 5 + i)
        t = Q.put("act", lambda e: e.activation(dst, psum[bank][:, :], ACT.Copy, scale=wc(2)), [t, p_in])
        for i in (0, 1, 3, 4):
            a, b = max(0, 2 - i), min(T, T + 2 - i)
            sh = i - 2
            t = Q.put("dve", lambda e, i=i, a=a, b=b, sh=sh: e.scalar_tensor_tensor(
                dst[:, a:b], psum[bank][:, a + sh:b + sh], wc(i), dst[:, a:b], ALU.mult, ALU.add), [t, p_in])
        bfree[bank] = t
        return Q.put("act", lambda e: e.activation(dst, dst, ACT.Silu), [t])

    t_qk = [None] * 8
    sq_free = [None] * 8
    LNQ = small("lnq", 1)
    t_lnq = Q.put("dve", lambda e: e.memset(LNQ[:], -0.5 * math.log(128.0)))

    SL8 = [zb(f"sl{j}", [128, 512], F32, 72 + 2 * j) for j in range(8)]

    def qk_square(j):
        sq_free[j] = Q.put("act", lambda e: e.activation(SL8[j][:], QK[:, j, :], ACT.Square), [t_conv[j]])

    def qk_norm():
        t_ln = [None] * 8
        for j in range(8):
            b = G.take()
            t = mm(psum[b][:, :], cf("ones"), SL8[j][:], True, True, [sq_free[j], bfree[b], c_in], True)
            t_ln[j] = bfree[b] = Q.put("act", lambda e, b=b, j=j: e.activation(SL8[j][:], psum[b][:, :], ACT.Ln, bias=eps), [t, t_ce])
            yield
        for j in range(8):
            bias = LNQ[:] if j < 4 else 0.0
            t = Q.put("act", lambda e, j=j, bias=bias: e.activation(SL8[j][:], SL8[j][:], ACT.Exp, scale=-0.5, bias=bias), [t_ln[j], t_lnq])
            t_qk[j] = Q.put("dve" if j % 2 else "pool", lambda e, j=j: e.tensor_tensor(QK[:, j, :], QK[:, j, :], SL8[j][:], ALU.mult), [t])
            if j % 2:
                yield

    t_conv = [None] * 12
    pend = None
    for j in range(12):
        b = G.take()
        t = dense_ch(b, x_ready, 2 if j == 0 else 1)
        if pend:
            pj, pb, pt = pend
            t_conv[pj] = conv5(pj, QK[:, pj, :] if pj < 8 else VC[:, pj - 8, :], pb, pt)
            if 1 <= pj <= 8:
                qk_square(pj - 1)
        pend = (j, b, t)
    pj, pb, pt = pend
    t_conv[pj] = conv5(pj, VC[:, pj - 8, :], pb, pt)

    t_kt = [None] * 4
    t_vt = [None] * 4

    def to_tokens():
        for dst, srcs, ready, done in ((VT, VC, t_conv[8:12], t_vt), (KT, QK, None, t_kt)):
            for cb in range(4):
                b = G.take()
                for h in range(4):
                    src = srcs[:, h, cb * 128:(cb + 1) * 128] if ready else srcs[:, 4 + h, cb * 128:(cb + 1) * 128]
                    r = ready[h] if ready else t_qk[4 + h]
                    t = tr(psum[b][:, h * 128:(h + 1) * 128], src, [r, bfree[b]], h == 3)
                done[cb] = bfree[b] = Q.put("act", lambda e, b=b, cb=cb, dst=dst: e.activation(
                    dst[:, cb, :], psum[b][:, :], ACT.Copy), [t] + t_qk)
                yield

    g4 = lambda name: small(name, 32, [128, 2, 4, 4])
    BETA, NBETA, NGC, GG, SPA, SPB, GC, GL, EG, EGL, EL, BEG = (g4(n) for n in (
        "beta", "nbeta", "ngc", "gg", "spa", "spb", "gc", "gl", "eg", "egl", "el", "beg"))
    EA = small("ea", 8)
    NSINK = small("nsink", 8)
    t_gate = [None]

    def gates(t_bd):
        dch = lambda ap: ap.rearrange("p c (d h) -> p d c h", d=2)
        bl, dl = dch(BD[:, :, 0:8]), dch(BD[:, :, 8:16])
        row = lambda ap: ap.rearrange("p (d h) -> p d h", d=2).unsqueeze(2).broadcast_to([128, 2, 4, 4])
        t = Q.put("act", lambda e: e.activation(EA[:], pr("dn_a_log"), ACT.Exp), [p_in])
        for d in range(2):
            t = Q.put("act", lambda e, d=d: e.activation(BETA[:, d], bl[:, d], ACT.Exp, scale=-1.0), t_bd)
        t = Q.put("dve", lambda e: e.tensor_scalar(BETA[:], BETA[:], 1.0, None, ALU.add), [t])
        t = Q.put("dve", lambda e: e.reciprocal(BETA[:], BETA[:]), [t])
        t = Q.put("dve", lambda e: e.tensor_scalar(NBETA[:], BETA[:], -1.0, None, ALU.mult), [t])
        for d in range(2):
            rb = pr("dn_dt_bias")[:, 4 * d:4 * d + 4].unsqueeze(1).broadcast_to([128, 4, 4])
            t = Q.put("dve", lambda e, d=d, rb=rb: e.tensor_tensor(SPA[:, d], dl[:, d], rb, ALU.add), [p_in] + t_bd)
        t = Q.put("dve", lambda e: e.scalar_tensor_tensor(SPB[:], SPA[:], -1.0, SPA[:], ALU.mult, ALU.max), [t])
        t1 = Q.put("dve", lambda e: e.tensor_scalar(SPA[:], SPA[:], 0.0, None, ALU.max), [t])
        t = Q.put("act", lambda e: e.activation(SPB[:], SPB[:], ACT.Exp, scale=-1.0), [t])
        t = Q.put("act", lambda e: e.activation(SPB[:], SPB[:], ACT.Ln, bias=1.0), [t])
        t = Q.put("dve", lambda e: e.tensor_tensor(SPA[:], SPA[:], SPB[:], ALU.add), [t, t1])
        for d in range(2):
            ea = EA[:, 4 * d:4 * d + 4].unsqueeze(1).broadcast_to([128, 4, 4])
            t1 = Q.put("dve", lambda e, d=d, ea=ea: e.scalar_tensor_tensor(GG[:, d], SPA[:, d], -1.0, ea, ALU.mult, ALU.mult), [t])
        yield
        b = G.take()
        fl = lambda ap: ap.rearrange("p c h -> p (c h)")
        mm(psum[b][:, 0:16], cf("triU"), fl(GG[:, 0]), True, True, [t1, bfree[b], c_in])
        mm(psum[b][:, 16:32], cf("triL"), fl(GG[:, 1]), True, True)
        t = mm(psum[b][:, 32:64], cf("ones"), GG[:].rearrange("p d c h -> p (d c h)"), True, True, (), True)
        f3 = lambda t_: t_[:].rearrange("p d c h -> p (d c h)")
        t = Q.put("dve", lambda e: e.tensor_copy(f3(GC), psum[b][:, 0:32]), [t])
        t = Q.put("dve", lambda e: e.tensor_copy(f3(GL), psum[b][:, 32:64]), [t])
        bfree[b] = t
        t1 = Q.put("dve", lambda e: e.tensor_scalar(NGC[:], GC[:], -1.0, None, ALU.mult), [t])
        t1 = Q.put("dve", lambda e: e.tensor_tensor(EGL[:], GL[:], GC[:], ALU.subtract), [t])
        t = Q.put("act", lambda e: e.activation(EG[:], GC[:], ACT.Exp), [t])
        t2 = Q.put("act", lambda e: e.activation(EL[:], GL[:], ACT.Exp), [t])
        t2 = Q.put("act", lambda e: e.activation(EGL[:], EGL[:], ACT.Exp), [t1])
        t = Q.put("dve", lambda e: e.tensor_tensor(BEG[:], BETA[:], EG[:], ALU.mult), [t])
        t_gate[0] = [t, t2]
        yield

    SSQ = small("ssq", 40, [128, 4, 10])
    t_swt = [None] * 4

    def swa_prep(t_swr):
        rows = SWR[:].rearrange("p t (h d) -> p t h d", d=64)
        r1 = R1[:].rearrange("p (h d) -> p h d", d=64)
        r2 = R2[:].rearrange("p (h d) -> p h d", d=64)
        tls, tg = [], []
        bc = lambda ap, n: ap.unsqueeze(1).broadcast_to([128, n, 64])
        tw = [None] * 4
        for tb in range(4):
            R = (R1, R2)[tb % 2]
            t = Q.put("pool", lambda e, tb=tb, R=R: e.tensor_tensor(R[:], SWR[:, tb, :], SWR[:, tb, :], ALU.mult),
                      t_swr[tb] + [tls[tb - 2] if tb > 1 else None])
            tls.append(Q.put("dve", lambda e, tb=tb, R=R: e.tensor_reduce(
                SSQ[:, tb, :], R[:].rearrange("p (h d) -> p h d", d=64), AX.X, ALU.add), [t]))
            Q.put("pool", lambda e, tb=tb: e.tensor_tensor(
                rows[:, tb, 0:2], rows[:, tb, 0:2], bc(pr("swa_k_norm_w"), 2), ALU.mult), [t, p_in])
            tg.append(Q.put("pool", lambda e, tb=tb: e.tensor_tensor(
                rows[:, tb, 2:10], rows[:, tb, 2:10], bc(pr("swa_q_norm_w"), 8), ALU.mult), [t, p_in]))
            yield
        t = root(SSQ[:], SSQ[:], 1.0 / 64, tls)
        t_ss = Q.put("dve", lambda e: e.reciprocal(SSQ[:], SSQ[:]), [t])
        t_r1 = t_r2 = tls[3]
        yield
        for tb in range(4):
            cs = cf("cos")[:, tb * 64:(tb + 1) * 64]
            sn = cf("sin")[:, tb * 64:(tb + 1) * 64]
            rs = SSQ[:, tb, :].unsqueeze(2).broadcast_to([128, 10, 64])
            t = tk = Q.put("dve", lambda e, tb=tb, rs=rs: e.tensor_tensor(rows[:, tb], rows[:, tb], rs, ALU.mult), [t_ss, tg[tb]])
            yield
            t1 = Q.put("dve", lambda e, tb=tb, bc=bc, cs=cs: e.tensor_tensor(r1, rows[:, tb], bc(cs, 10), ALU.mult),
                       [t, tk, t_r1, c_in])
            for o, i in ((0, 32), (32, 0)):
                s = sn[:, o:o + 32].unsqueeze(1).broadcast_to([128, 10, 32])
                t2 = Q.put("dve", lambda e, tb=tb, o=o, i=i, s=s: e.tensor_tensor(
                    r2[:, :, o:o + 32], rows[:, tb, :, i:i + 32], s, ALU.mult), [t, tk, t_r2, c_in])
            t3 = Q.put("dve", lambda e, tb=tb: e.tensor_tensor(rows[:, tb, 0:2], r1[:, 0:2], r2[:, 0:2], ALU.add), [t1, t2])
            qo = rows[:, tb, 2:10].rearrange("p (i g) d -> p g i d", g=2)
            qa = r1[:, 2:10].rearrange("p (g i) d -> p g i d", g=2)
            qb_ = r2[:, 2:10].rearrange("p (g i) d -> p g i d", g=2)
            t_r1 = t_r2 = tw[tb] = Q.put("dve", lambda e, qo=qo, qa=qa, qb_=qb_: e.tensor_tensor(qo, qa, qb_, ALU.add), [t1, t2])
            yield
        for i in range(5):
            b = G.take()
            for tb in range(4):
                src = SWR[:, tb, 0:128] if i == 4 else SWR[:, tb, 128 + i * 128:256 + i * 128]
                t = tr(psum[b][:, tb * 128:(tb + 1) * 128], src, [tw[tb], bfree[b]], tb == 3)
            dst = SKT[:] if i == 4 else SQT[:, i, :]
            t_swt[0] = bfree[b] = Q.put("act", lambda e, b=b, dst=dst: e.activation(dst, psum[b][:, :], ACT.Copy), [t] + t_vt)
            yield

    t_bd = [None] * 4
    t_k = [None] * 4
    t_swr = [None] * 4
    t_sv = [None] * 4
    t_z = [None] * 4
    t_sz = [None] * 4

    def evac_first(banks):
        def f(tb, t):
            b = banks[tb]
            t = Q.put("act", lambda e: e.activation(BD[:, tb, :], psum[b][:, 0:16], ACT.Copy), [t])
            t_bd[tb] = t
            t_k[tb] = Q.put("act", lambda e: e.activation(SWR[:, tb, 0:128], psum[b][:, 16:144], ACT.Copy))
            bfree[b] = t_sv[tb] = Q.put("act", lambda e: e.activation(SV[:, tb, :], psum[b][:, 144:272], ACT.Copy))
        return f

    def evac_to(banks, dst, func, done):
        def f(tb, t):
            b = banks[tb]
            done[tb] = bfree[b] = Q.put("act", lambda e: e.activation(dst(tb), psum[b][:, :], func), [t])
        return f

    def step(g, n=1):
        for _ in range(n):
            if next(g, "end") == "end":
                return False
        return True

    def four():
        return [G.take() for _ in range(4)]

    bk = [0, 1, 2, 3]
    G = Banks(bfree, (4, 5, 6, 7))

    def in_turn(*gs):
        for g in gs:
            yield from g

    g1 = in_turn(qk_norm(), to_tokens())
    for _ in dense_tok(bk, 272, x_ready, evac_first(bk)):
        step(g1, 2)
    g2 = gates(t_bd)
    for _ in dense_tok(bk, 512, x_ready, evac_to(bk, lambda tb: SWR[:, tb, 128:640], ACT.Copy, t_swr)):
        step(g1, 1)
        step(g2, 1)
    g3 = swa_prep([[a, b_] for a, b_ in zip(t_k, t_swr)])
    for _ in dense_tok(bk, 512, x_ready, evac_to(bk, lambda tb: MIX[:, tb, 512:1024], ACT.Silu, t_sz)):
        step(g1, 3)
        step(g2, 1)
        step(g3, 3)
    z_proj = dense_tok(bk, 512, x_ready, evac_to(bk, lambda tb: MIX[:, tb, 0:512], ACT.Silu, t_z))

    MP = [zb(f"mp{c}", [128, 2, 512], F32, 4 * c) for c in range(4)]
    TT = MP
    AT = [zb(f"at{c}", [128, 2, 512], F32, 16 + 4 * c) for c in range(4)]

    def work(i, *at):
        at = dict(zip(("XF", "DD", "MR", "DT"), at))
        put = lambda n, m, dt: [at[m][0](f"{n.lower()}{i}{d}", [128, 512], dt, at[m][1][d]) for d in range(2)]
        W = {n: put(n, n, F32R) for n in at}
        W.update({n: put(n, m, F32) for n, m in (("EE", "XF"), ("MB", "DT"))})
        return W

    two_at = lambda f, o: (f, (o, o + 2))
    four_at = lambda f, o: [two_at(f, o + 4 * n) for n in range(4)]
    WORK = [work(0, *four_at(zb, 32)), work(1, *four_at(sb, 16)), work(2, *four_at(sb, 32)),
            work(3, two_at(zb, 104), two_at(zb, 108), two_at(sb, C0 + 16.25), (zb, (112, 124)))]
    O = zb("o", [128, 4, 512], F32, 104)
    PM = [zb(f"pm{i}", [128, 384], F32, 116 + 1.5 * i) for i in range(2)]
    PMT = [zb(f"pmt{i}", [128, 384], F32, 119 + 1.5 * i) for i in range(2)]
    SWO = zb("swo", [128, 512], F32, 122)
    OT = zb("ot", [128, 512], F32, 129)
    SCAN = [dict(VB=zb("vb0", [128, 512], F32, 32), KB_=zb("kb0", [128, 512], F32, 34), KD=zb("kd0", [128, 512], F32, 36),
                 NW=zb("nw0", [128, 512], F32, 38), VN=zb("vn0", [128, 512], F32, 40), S=zb("s0", [128, 512], F32, 112)),
            dict(VB=zb("vb1", [128, 512], F32, 42), KB_=zb("kb1", [128, 512], F32, 44), KD=zb("kd1", [128, 512], F32, 46),
                 NW=zb("nw1", [128, 512], F32, 64), VN=zb("vn1", [128, 512], F32, 66), S=zb("s1", [128, 512], F32, 124))]
    s_x2 = sem("s_xagain")
    RO = small("ro", 16, [128, 4, 4])
    BI = Banks(bfree, (0, 1, 2, 3, 4))
    BA = (5, 6, 7)
    hs = lambda t_, h: t_[:, h * 128:(h + 1) * 128]
    v3 = lambda t_: t_[:].rearrange("p (h n) -> p h n", h=4)
    h3 = lambda ap: ap.rearrange("p (h n) -> p h n", h=4)
    bc4 = lambda ap: ap.unsqueeze(1).broadcast_to([128, 4, 128])
    b4r = lambda ap: ap.unsqueeze(2).broadcast_to([128, 4, 128])
    work_end = [None] * 4
    ti = [[None, None] for _ in range(4)]
    t_at = [[None, None] for _ in range(4)]

    def invert(cb):
        W = WORK[cb]
        fr = None if cb in (0, 3) else x_pe[0]
        cs = slice(cb * 128, (cb + 1) * 128)
        kT = lambda h: QK[:, 4 + h, cs]
        qT = lambda h: QK[:, h, cs]
        col = lambda t_, d, h: t_[:, d, cb, h:h + 1]
        gate = t_gate[0]
        XF, DD, DT, MR = W["XF"], W["DD"], W["DT"], W["MR"]
        f32 = lambda ts: [t_[:].bitcast(F32) for t_ in ts]
        EE, MB = ([t_[:] for t_ in W[n]] for n in ("EE", "MB"))
        mp, at = [MP[cb][:, d, :] for d in range(2)], [AT[cb][:, d, :] for d in range(2)]
        tri = (cf("triU"), cf("triL"))
        strict = (cf("SL"), cf("SU"))
        sub = lambda t_, d, h: t_[d][:, h * 128:(h + 1) * 128]
        two = range(2)
        te, tb_ = [None, None], [None, None]
        for d in two:
            b = BI.take()
            for h in range(4):
                t = tr(hs(psum[b], h), col(GC, d, h).broadcast_to([128, 128]), [bfree[b]] + gate, h == 3)
            for h in range(4):
                if d:
                    t2 = Q.put("dve", lambda e, d=d, h=h, b=b: e.tensor_scalar(
                        sub(EE, d, h), hs(psum[b], h), col(GC, d, h), 0.0, ALU.subtract, ALU.max), [t, fr])
                else:
                    t2 = Q.put("act", lambda e, d=d, h=h, b=b: e.activation(
                        sub(EE, d, h), hs(psum[b], h), ACT.Relu, bias=col(NGC, d, h)), [t, fr])
            bfree[b] = t2
            te[d] = Q.put("act", lambda e, d=d: e.activation(EE[d], EE[d], ACT.Exp, scale=-1.0), [t2])
            tb_[d] = Q.put("pool", lambda e, d=d: e.tensor_tensor(h3(MB[d]), h3(EE[d]), bc4(strict[d]), ALU.mult), [te[d], fr])
            tb_[d] = Q.put("pool", lambda e, d=d: e.tensor_tensor(h3(MB[d]), h3(MB[d]), b4r(NBETA[:, d, cb, :]), ALU.mult), [tb_[d]])
            yield
        fr = x_pe[0]
        bk_, bq = BI.take(), BI.take()
        for h in range(4):
            tk = mm(hs(psum[bk_], h), kT(h), kT(h), True, True, [t_qk[4 + h], bfree[bk_]], h == 3)
        for h in range(4):
            tq = mm(hs(psum[bq], h), kT(h), qT(h), True, True, [t_qk[h], bfree[bq]], h == 3)
        for d in two:
            ta = Q.put("dve", lambda e, d=d: e.tensor_tensor(h3(at[d]), h3(psum[bq][:, :]), bc4(tri[d]), ALU.mult), [tq, fr])
        bfree[bq] = ta
        yield
        tm = [None, None]
        for d in two:
            tm[d] = Q.put("dve", lambda e, d=d: e.tensor_tensor(mp[d], psum[bk_][:, :], MB[d], ALU.mult), [tb_[d], tk, fr])
        bfree[bk_] = tm[1]
        for d in two:
            be = BI.take()
            for h in range(4):
                tt = tr(hs(psum[be], h), sub(EE, d, h), [te[d], bfree[be]], h == 3)
            t_at[cb][d] = bfree[be] = Q.put("dve", lambda e, d=d, be=be: e.tensor_tensor(
                at[d], at[d], psum[be][:, :], ALU.mult), [ta, tt])
        tdd, tmr = [None, None], [None, None]
        for d in two:
            tm[d] = Q.put("pool", lambda e, d=d: e.tensor_tensor(h3(mp[d]), h3(mp[d]), bc4(cf("ident")), ALU.add), [tm[d]])
        for d in two:
            tdd[d] = Q.put("dve", lambda e, d=d: e.tensor_tensor(h3(DD[d][:]), h3(mp[d]), bc4(cf("LM", 7 * (1 - d))), ALU.mult),
                           [fr, tm[d]])
            tmr[d] = Q.put("act", lambda e, d=d: e.activation(MR[d][:], mp[d], ACT.Copy), [tm[d], fr])
        yield
        tdt = [None, None]
        for d in two:
            b = BI.take()
            for h in range(4):
                t = tr(hs(psum[b], h), sub(mp, d, h), [tm[d], bfree[b]], h == 3)
            tdt[d] = bfree[b] = Q.put("dve", lambda e, d=d, b=b: e.tensor_tensor(
                h3(DT[d][:]), h3(psum[b][:, :]), bc4(cf("LM", 7 * d)), ALU.mult), [t])
        yield
        for lvl in range(1, 7):
            tx = [None, None]
            for d in two:
                b = BI.take()
                for h in range(4):
                    t = mm(hs(psum[b], h), sub(MR, d, h), sub(DT, d, h), True, True, [tdt[d], tmr[d], bfree[b]], h == 3)
                tx[d] = bfree[b] = Q.put("dve", lambda e, d=d, b=b, lvl=lvl: e.tensor_tensor(
                    h3(XF[d][:]), h3(psum[b][:, :]), bc4(cf("LM", 7 * d + lvl)), ALU.mult), [t, tt])
            yield
            for d in two:
                b = BI.take()
                for h in range(4):
                    t1 = mm(hs(psum[b], h), sub(DD, d, h), sub(XF, d, h), True, True, [tx[d], tdd[d], bfree[b]], h == 3)
                tdt[d] = bfree[b] = Q.put("act", lambda e, d=d, b=b: e.activation(DT[d][:], psum[b][:, :], ACT.Copy), [t1])
            for d in two:
                b = BI.take()
                for h in range(4):
                    t2 = mm(hs(psum[b], h), sub(XF, d, h), sub(DD, d, h), True, True, [bfree[b]], h == 3)
                if d:
                    tdd[d] = bfree[b] = Q.put("act", lambda e, d=d, b=b: e.activation(DD[d][:], psum[b][:, :], ACT.Copy), [t2])
                else:
                    tdd[d] = bfree[b] = Q.put("dve", lambda e, d=d, b=b: e.tensor_copy(DD[d][:], psum[b][:, :]), [t2])
            yield
        dt32 = f32(DT)
        tx = [None, None]
        for d in two:
            b = BI.take()
            for h in range(4):
                mm(hs(psum[b], h), sub(mp, d, h), sub(dt32, d, h), True, False, [tdt[d], bfree[b]])
                t = mm(hs(psum[b], h), IDb[:], IDb[:], False, True, [t_id], h == 3)
            tx[d] = bfree[b] = Q.put("dve", lambda e, d=d, b=b: e.scalar_tensor_tensor(
                XF[d][:], dt32[d], -2.0, psum[b][:, :], ALU.mult, ALU.add), [t, t2])
        yield
        for d in two:
            b = BI.take()
            for h in range(4):
                t1 = mm(hs(psum[b], h), sub(DD, d, h), sub(XF, d, h), True, True, [tx[d], tdd[d], bfree[b]], h == 3)
            ti[cb][d] = bfree[b] = Q.put("dve", lambda e, d=d, b=b: e.tensor_tensor(
                mp[d], dt32[d], psum[b][:, :], ALU.add), [t1])
        work_end[cb] = ti[cb][1]
        yield

    o_tok = [None] * 4
    s_tok = [None, None]
    kb_tok = [None, None]
    nw_tok = [None, None]
    scan_free = [[], []]

    def scan_keys(d, r, waits):
        cb = r if d == 0 else 3 - r
        W = SCAN[d]
        k3 = h3(KT[:, cb, :])
        gate = t_gate[0]
        w = waits + gate + [t_vt[cb], t_kt[cb]]
        if r:
            t = Q.put("pool", lambda e: e.tensor_tensor(v3(W["KB_"]), k3, b4r(BEG[:, d, cb, :]), ALU.mult), w)
        tv = Q.put("pool", lambda e: e.tensor_tensor(v3(W["VB"]), h3(VT[:, cb, :]), b4r(BETA[:, d, cb, :]), ALU.mult), w)
        td = Q.put("pool", lambda e: e.tensor_tensor(v3(W["KD"]), k3, b4r(EGL[:, d, cb, :]), ALU.mult), w) if r < 3 else None
        kb_tok[d] = (tv, td)
        if r:
            b = BI.take()
            for h in range(4):
                t = mm(hs(psum[b], h), hs(W["KB_"], h), TT[cb][:, d, h * 128:(h + 1) * 128], True, True, [t, ti[cb][d], bfree[b]], h == 3)
            nw_tok[d] = bfree[b] = Q.put("act", lambda e, b=b: e.activation(W["NW"][:], psum[b][:, :], ACT.Copy, scale=-1.0), [t] + waits)

    def scan_step(d, r):
        cb = r if d == 0 else 3 - r
        W = SCAN[d]
        cs = slice(cb * 128, (cb + 1) * 128)
        col = lambda t_, h: t_[:, d, cb, h:h + 1]
        th = lambda t_, h: t_[cb][:, d, h * 128:(h + 1) * 128]
        if r == 0:
            scan_keys(d, 0, [work_end[0], scan_free[d][-1]])
        tvb, tkd = kb_tok[d]
        tw, ts = nw_tok[d], s_tok[d]
        b = BI.take()
        for h in range(4):
            t = mm(hs(psum[b], h), th(TT, h), hs(W["VB"], h), True, r == 0, [ti[cb][d], tvb, bfree[b]], h == 3 and r == 0)
            if r:
                t = mm(hs(psum[b], h), hs(W["NW"], h), hs(W["S"], h), False, True, [tw, ts], h == 3)
        tv = bfree[b] = Q.put("act", lambda e, b=b: e.activation(W["VN"][:], psum[b][:, :], ACT.Copy), [t] + scan_free[d])
        yield
        if r:
            bs = BI.take()
            for h in range(4):
                tqs = mm(hs(psum[bs], h), QK[:, h, cs], hs(W["S"], h), True, True, [ts, bfree[bs]] + t_qk[0:4], h == 3)
        if r < 3:
            b = BI.take()
            for h in range(4):
                t = mm(hs(psum[b], h), hs(W["KD"], h), hs(W["VN"], h), True, True, [tkd, tv, bfree[b]], h == 3)
            for h in range(4):
                if r:
                    t = Q.put("dve", lambda e, b=b, h=h: e.scalar_tensor_tensor(
                        hs(W["S"], h), hs(W["S"], h), col(EL, h), hs(psum[b], h), ALU.mult, ALU.add), [t, ts, tqs])
                else:
                    t = Q.put("dve", lambda e, b=b, h=h: e.tensor_copy(hs(W["S"], h), hs(psum[b], h)), [t] + scan_free[d])
            s_tok[d] = bfree[b] = t
        b = BI.take()
        for h in range(4):
            t = mm(hs(psum[b], h), th(AT, h), hs(W["VN"], h), True, True, [t_at[cb][d], tv, bfree[b]], h == 3)
        last = t
        ov_ = O[:, cb, :]
        if o_tok[cb] is None:
            t = bfree[b] = Q.put("act", lambda e, b=b: e.activation(ov_, psum[b][:, :], ACT.Copy), [t] + scan_free[d])
        else:
            t = bfree[b] = Q.put("dve", lambda e, b=b: e.tensor_tensor(ov_, ov_, psum[b][:, :], ALU.add), [t, o_tok[cb]])
        if r:
            for h in range(4):
                t = Q.put("dve", lambda e, h=h, bs=bs: e.scalar_tensor_tensor(
                    O[:, cb, h * 128:(h + 1) * 128], hs(psum[bs], h), col(EG, h), O[:, cb, h * 128:(h + 1) * 128],
                    ALU.mult, ALU.add), [t, tqs])
            bfree[bs] = t
        o_tok[cb] = t
        yield
        if r < 3:
            scan_keys(d, r + 1, [last])
        dn_free[d] = last
        yield

    dn_free = [None, None]

    t_mix = [[None, None] for _ in range(4)]
    ot_free = [None]

    def z_gain(cb):
        t_z[cb] = Q.put("pool", lambda e: e.tensor_tensor(h3(MIX[:, cb, 0:512]), h3(MIX[:, cb, 0:512]), bc4(pr("dn_out_norm_w")), ALU.mult),
                        [t_z[cb], p_in])

    def dn_post(cb):
        for h in range(4):
            t = Q.put("act", lambda e, h=h: e.activation(OT[:, h * 128:(h + 1) * 128], O[:, cb, h * 128:(h + 1) * 128], ACT.Square,
                                                         accum_out=RO[:, cb, h:h + 1]), [o_tok[cb], ot_free[0]])
        ot_free[0] = t
        t = root(RO[:, cb, :], RO[:, cb, :], 1.0 / 128, [t])
        yield
        t = Q.put("dve", lambda e: e.reciprocal(RO[:, cb, :], RO[:, cb, :]), [t])
        for h in range(4):
            c = slice(h * 128, (h + 1) * 128)
            t_mix[cb][0] = Q.put("dve", lambda e, h=h, c=c: e.scalar_tensor_tensor(
                MIX[:, cb, c], O[:, cb, c], RO[:, cb, h:h + 1], MIX[:, cb, c], ALU.mult, ALU.mult), [t, t_z[cb]])
        yield

    MX = small("mx", 32, [128, 4, 8])
    DEN = small("den", 32, [128, 4, 8])
    ES = small("es", 32, [128, 4, 8])
    t_ns = Q.put("dve", lambda e: e.tensor_scalar(NSINK[:], pr("swa_sinks"), -1.0, None, ALU.mult), [p_in])

    def swa():
        bs, bt, bo = BA
        pieces = [(qb, h) for qb in range(4) for h in range(8)]
        st = [dict() for _ in pieces]
        pm_free, pmt_free = [None, None], [None, None]
        swo_free = [None]
        for n in range(len(pieces) + 2):
            if n < len(pieces):
                qb, h = pieces[n]
                g, i = h // 4, h % 4
                k0, k1 = max(qb - 1, 0), min(qb + 1, 3)
                nk = (k1 - k0 + 1) * 128
                ps = slice(64 * g, 64 * g + 64)
                masks = ([(0, NLb)] if qb > 0 else []) + ([(nk - 128, NUb)] if qb < 3 else [])
                mm(psum[bs][:, 0:nk], SQT[ps, i, qb * 128:(qb + 1) * 128], SKT[ps, k0 * 128:(k1 + 1) * 128], True, True,
                   [t_swt[0], bfree[bs]])
                for m, (at, mask) in enumerate(masks):
                    t = mm(psum[bs][:, at:at + 128], IDb[:], mask[:], False, True, [t_id, t_nl], m == len(masks) - 1, True)
                mx = MX[:, qb, h:h + 1]
                t = Q.put("dve", lambda e, nk=nk, mx=mx: e.tensor_reduce(mx, psum[bs][:, 0:nk], AX.X, ALU.max, negate=True), [t])
                t = t_mx = Q.put("dve", lambda e, mx=mx, h=h: e.tensor_scalar(mx, mx, 0.125, NSINK[:, h:h + 1], ALU.mult, ALU.min), [t, t_ns])
                pm = PM[n % 2]
                t = bfree[bs] = Q.put("act", lambda e, nk=nk, mx=mx, pm=pm, qb=qb, h=h: e.activation(
                    pm[:, 0:nk], psum[bs][:, 0:nk], ACT.Exp, bias=mx, scale=0.125, accum_out=DEN[:, qb, h:h + 1]),
                    [t, pm_free[n % 2]])
                st[n].update(nk=nk, k0=k0, k1=k1, g=g, t=t, mx=t_mx)
                yield
            if 0 <= n - 1 < len(pieces):
                m = n - 1
                s = st[m]
                for k in range(s["nk"] // 128):
                    t = tr(psum[bt][:, k * 128:(k + 1) * 128], PM[m % 2][:, k * 128:(k + 1) * 128], [s["t"], bfree[bt]],
                           k == s["nk"] // 128 - 1)
                pm_free[m % 2] = t
                pt = PMT[m % 2]
                nk = s["nk"]
                if m % 2:
                    t = Q.put("act", lambda e, pt=pt, nk=nk: e.activation(pt[:, 0:nk], psum[bt][:, 0:nk], ACT.Copy), [t, pmt_free[m % 2]])
                else:
                    t = Q.put("dve", lambda e, pt=pt, nk=nk: e.tensor_copy(pt[:, 0:nk], psum[bt][:, 0:nk]), [t, pmt_free[m % 2]])
                s["tt"] = bfree[bt] = t
                yield
            if 0 <= n - 2 < len(pieces):
                m = n - 2
                s = st[m]
                qb, h = pieces[m]
                kn = s["k1"] - s["k0"] + 1
                for k in range(kn):
                    t = mm(psum[bo][:, h * 64:(h + 1) * 64], PMT[m % 2][:, k * 128:(k + 1) * 128],
                           SV[:, s["k0"] + k, s["g"] * 64:s["g"] * 64 + 64], k == 0, k == kn - 1,
                           [s["tt"], bfree[bo]] + t_sv, k == kn - 1)
                pmt_free[m % 2] = t
                if h == 7:
                    t1 = Q.put("dve", lambda e, qb=qb: e.tensor_tensor(ES[:, qb, :], pr("swa_sinks"), MX[:, qb, :], ALU.add), [t_ns, s["mx"]])
                    t1 = Q.put("act", lambda e, qb=qb: e.activation(ES[:, qb, :], ES[:, qb, :], ACT.Exp), [t1])
                    t1 = Q.put("dve", lambda e, qb=qb: e.tensor_tensor(DEN[:, qb, :], DEN[:, qb, :], ES[:, qb, :], ALU.add), [t1])
                    t1 = Q.put("dve", lambda e, qb=qb: e.reciprocal(DEN[:, qb, :], DEN[:, qb, :]), [t1])
                    rd = DEN[:, qb, :].unsqueeze(2).broadcast_to([128, 8, 64])
                    o8 = lambda ap: ap.rearrange("p (h n) -> p h n", h=8)
                    t = bfree[bo] = Q.put("dve", lambda e, rd=rd: e.tensor_tensor(o8(SWO[:]), o8(psum[bo][:, :]), rd, ALU.mult),
                                          [t, t1, swo_free[0]])
                    swo_free[0] = t_mix[qb][1] = Q.put("pool", lambda e, qb=qb: e.tensor_tensor(
                        MIX[:, qb, 512:1024], MIX[:, qb, 512:1024], SWO[:], ALU.mult), [t, t_sz[qb]])
                yield

    def both(cbs, i):
        for cb in cbs:
            yield from invert(cb, i)

    early = 0
    gi = [invert(cb) for cb in (0, 3, 1, 2)]
    BI = Banks(bfree, (4,))
    while step(z_proj):
        step(g1, 3)
        step(g2, 1)
        step(g3, 3)
        if t_gate[0] and early < 4:
            step(gi[early // 2])
            early += 1
    for g in (g1, g2, g3):
        while step(g):
            pass
    for g in gi:
        while early < 4:
            step(gi[early // 2])
            early += 1
    x_pe[:] = [w_used[unit[0] - 1]] * 4
    BI = Banks(bfree, (0, 1, 2, 3, 4))
    gs = swa()
    for g in gi[2:]:
        step(g, 2)
    live = True
    while live:
        live = False
        for g in gi:
            live = step(g) or live
            step(gs, 2)
    for cb in range(4):
        z_gain(cb)
    while step(gs):
        pass
    BI = Banks(bfree, range(8))
    swa_end = [t for m in t_mix for t in m if t]
    for d in range(2):
        scan_free[d] += work_end + [swa_end[-1]]
    slot1 = (0, 1, 6, 7, 2, 3, 4, 5)
    ready = no_tiles()

    def add_h(b, tb, n, done, t, wait):
        hv = H[:, tb, n * 512:(n + 1) * 512]
        done[tb] = bfree[b] = Q.put("dve", lambda e: e.tensor_tensor(hv, hv, psum[b][:, :], ALU.add), [t, wait])

    def add_to(banks, n, done, wait):
        return lambda tb, t: add_h(banks[tb], tb, n, done, t, wait)

    h_tok = [None] * 4
    G = BI
    gp = None
    for r in range(4):
        if r == 3:
            gp = in_turn(dn_post(1), dn_post(2))
            last_split[0] = NU
            ring_busy.extend(work_end)
            w_ahead(30)
            x_pe[:] = [max(dn_free, key=lambda t: t[1])] * 4
        ga, gb = scan_step(0, r), scan_step(1, r)
        live = True
        n = 0
        while live:
            la = step(ga)
            if r == 3 and n < 2:
                split_t(MIX, 2 * n, 1, t_mix[2 * n][1], slot1, ready)
                split_t(MIX, 2 * n + 1, 1, t_mix[2 * n + 1][1], slot1, ready)
            n += 1
            lb = step(gb)
            live = la or lb
            if gp and n > 1:
                step(gp, 2)
        if r == 3:
            t_h = Q.dma("sp", H[:], xv, s_x2, 16, dn_free + s_tok)
            bk = four()
            go = dense_tok(bk, 512, ready, add_to(bk, 0, h_tok, t_h), slot1, MIX_K)
            ga, gb = dn_post(0), dn_post(3)
            step(ga)
            step(gb)
            step(go, 2)
            for g in (gp, ga, gb):
                while step(g):
                    pass
    x_pe[:] = [max(dn_free, key=lambda t: t[1])] * 4

    s_b2 = sem("s_b2")
    WS = zb("ws", [128, 8, 128], F32, 104)
    TB = zb("tb", [128, 896], F32, 108)
    SELF = zb("self", [96, 1024], F32, 112)
    SEL = zb("sel", [96, 8, 128], BF16, 116)
    done1 = [t for m in t_mix for t in m]
    t_gain = load_gain("norm_mix_g_2", [t_gain] + work_end)
    Q.dma("sp", WS[:], wsd, s_b2, 16, done1)
    Q.dma("sp", TB[:], tbd, s_b2, 32, [dn_free[0], dn_free[1], s_tok[0], s_tok[1]])
    b2_in = Q.dma("sp", SELF[:], seld, s_b2, 48)
    for tb in (1, 2, 0, 3):
        split_t(MIX, tb, 0, t_mix[tb][0], slot1, ready)
    while step(go):
        pass

    def out_last(i, XS, ready, slot, ks, wait):
        x_ready = no_tiles()
        ts = [None] * 4

        st = [None] * 4

        def evac(b, tb, t):
            if tb:
                ts[tb - 1] = norm_scale(i, tb - 1, XS, st[tb - 1])
            add_h(b, tb, 1, h_tok, t, wait)
            x_pe[tb] = t
            st[tb] = norm_stats(i, tb, XS, [h_tok[tb]])

        def put(tb):
            norm_b(tb, XS, ts[tb], x_ready)

        dense_last(512, ready, slot, ks, evac, lambda tb: put(tb - 2) if tb > 1 else None)
        ts[3] = norm_scale(i, 3, XS, st[3])
        return x_ready, ts[3], put

    XS2 = zb("xs2", [128, 4, 1024], F32, 48)
    QK2 = zb("qk2", [128, 8, 512], F32, 48)
    V2 = zb("v2", [128, 4, 512], F32, 64)
    U2 = zb("u2", [128, 4, 512], F32, 72)
    VG = zb("vg", [128, 4, 512], F32, 80)
    MIX2 = zb("mix2", [128, 4, 1024], F32, 88)
    WST = WS
    LF = zb("lf", [8, 512], F32, 118)
    LG = zb("lg", [8, 512], F32, 120)
    VSQ = [zb(f"vsq{i}", [128, 512], F32, 118 + 2 * i) for i in range(2)]
    C3 = zb("c3", [96, 512], BF16, 122)
    P2 = [zb(f"p2{i}", [128, 512], F32, 123 + 2 * i) for i in range(2)]
    P2T = [zb(f"p2t{i}", [128, 512], F32, 127 + 2 * i) for i in range(2)]
    LT = small("lt", 32, [128, 4, 8])

    x_ready, t_xs, late = out_last(1, XS2, ready, slot1, MIX_K, t_h)
    t_gain = load_gain("norm_ffn_g_2", [t_gain, t_xs])
    t_sel = Q.put("dve", lambda e: e.tensor_copy(SEL[:].rearrange("p h n -> p (h n)"), SELF[:]), [b2_in])
    t_c3 = Q.put("dve", lambda e: e.memset(C3[:], 0.0))
    t_v2 = [None] * 4
    bk = four()
    for _ in dense_tok(bk, 512, x_ready, evac_to(bk, lambda tb: V2[:, tb, :], ACT.Copy, t_v2), late=late):
        pass
    b = G.take()
    t = dense_ch(b, x_ready)
    t = Q.put("dve", lambda e, b=b: e.tensor_scalar(LF[:], psum[b][0:8, :], pp("b_forget_2", 0, 1, 8), None, ALU.add), [t, p_in])
    bfree[b] = t
    t = Q.put("dve", lambda e: e.scalar_tensor_tensor(LG[:], LF[:], -1.0, LF[:], ALU.mult, ALU.max), [t])
    t1 = Q.put("dve", lambda e: e.tensor_scalar(LF[:], LF[:], 0.0, None, ALU.min), [t])
    t = Q.put("act", lambda e: e.activation(LG[:], LG[:], ACT.Exp, scale=-1.0), [t])
    t = Q.put("act", lambda e: e.activation(LG[:], LG[:], ACT.Ln, bias=1.0), [t])
    t_lf = Q.put("dve", lambda e: e.tensor_tensor(LF[:], LF[:], LG[:], ALU.subtract), [t, t1])
    t_q2 = [None] * 8
    t_cs = [None]

    def cum_a():
        b = G.take()
        for tb in range(4):
            t = tr(psum[b][:, tb * 8:(tb + 1) * 8], LF[:, tb * 128:(tb + 1) * 128], [t_lf, bfree[b]], tb == 3)
        return Q.put("act", lambda e: e.activation(LT[:].rearrange("p t h -> p (t h)"), psum[b][:, 0:32], ACT.Copy), [t]), b

    def cum_b(t):
        b = G.take()
        for tb in range(4):
            n0 = tb * 128
            t1 = mm(psum[b][0:8, n0:512], LT[:, tb, :], TB[:, 384:896 - n0], tb == 0, True, [t, b2_in, bfree[b]], tb == 3, tb > 0)
        hi, mid, lo = C3[0:8, :], C3[32:40, :], C3[64:72, :]
        t = Q.put("dve", lambda e: e.tensor_copy(LF[:], psum[b][0:8, :]), [t1])
        bfree[b] = t
        t = Q.put("dve", lambda e: e.tensor_copy(hi, LF[:]), [t, t_c3])
        t = Q.put("dve", lambda e: e.tensor_tensor(LG[:], LF[:], hi, ALU.subtract), [t])
        t = Q.put("dve", lambda e: e.tensor_copy(mid, LG[:]), [t])
        t = Q.put("dve", lambda e: e.tensor_copy(LF[:], mid), [t])
        t = Q.put("dve", lambda e: e.tensor_tensor(LG[:], LG[:], LF[:], ALU.subtract), [t])
        t_cs[0] = Q.put("dve", lambda e: e.tensor_copy(lo, LG[:]), [t])

    for j in range(8):
        b = G.take()
        t = dense_ch(b, x_ready)
        if j == 1:
            tl, bl_ = cum_a()
            bfree[bl_] = tl
        if j == 3:
            cum_b(tl)
        t_q2[j] = bfree[b] = Q.put("act", lambda e, b=b, j=j: e.activation(QK2[:, j, :], psum[b][:, :], ACT.Copy), [t])

    t_u2, t_vg = [None] * 4, [None] * 4
    VSS = small("vss", 32, [128, 4, 8])
    t_m2 = [[None, None] for _ in range(4)]
    t_wst = []

    def gmlp():
        for half in range(2):
            w4 = WST[:, 4 * half:4 * half + 4, :]
            t_wst.append(Q.put("pool", lambda e, w4=w4: e.tensor_tensor(w4, w4, bc4(cf("triU")), ALU.mult), [b2_in, c_in]))
        vt = [None, None]
        sq = [None] * 4
        for n in range(6):
            if n < 4:
                sq[n] = Q.put("pool", lambda e, n=n: e.tensor_tensor(VSQ[n % 2][:], VG[:, n, :], VG[:, n, :], ALU.mult),
                              [t_vg[n], vt[n % 2], t_cs[0]])
            yield
            if 0 < n < 5:
                vt[(n - 1) % 2] = Q.put("dve", lambda e, n=n: e.tensor_reduce(
                    VSS[:, n - 1, :], VSQ[(n - 1) % 2][:].rearrange("p (g n) -> p g n", g=8), AX.X, ALU.add), [sq[n - 1]])
        t = root(VSS[:], VSS[:], 1.0 / 64, vt)
        yield
        t = Q.put("dve", lambda e: e.reciprocal(VSS[:], VSS[:]), [t])
        ready = []
        yield
        for tb in range(4):
            v8 = VG[:, tb, :].rearrange("p (g n) -> p g n", g=8)
            rs = VSS[:, tb, :].unsqueeze(2).broadcast_to([128, 8, 64])
            t1 = Q.put("pool", lambda e, tb=tb: e.tensor_tensor(VG[:, tb, :], VG[:, tb, :], pr("gmlp_norm_g_2"), ALU.mult), vt)
            ready.append(Q.put("dve", lambda e, v8=v8, rs=rs: e.tensor_tensor(v8, v8, rs, ALU.mult), [t, t1]))
        yield
        for g in range(8):
            if g % 2 == 0:
                b = G2.take()
            o = psum[b][:, (g % 2) * 256:(g % 2) * 256 + 256]
            t = mm(o, WST[:, g, :], VG[:, :, g * 64:(g + 1) * 64], True, True, [bfree[b], ready[3]] + t_wst, True)
            u = U2[:, :, g * 64:(g + 1) * 64]
            m = MIX2[:, :, 512 + g * 64:512 + (g + 1) * 64]
            t = bfree[b] = Q.put("dve", lambda e, o=o, g=g, u=u, m=m: e.scalar_tensor_tensor(
                m, o.rearrange("p (t n) -> p t n", t=4), pp("b_spatial_2", g), u, ALU.add, ALU.mult), [t] + t_u2)
            yield
        for tb in range(4):
            t_m2[tb][1] = t

    MX2 = small("mx2", 32, [128, 4, 8])
    DN2 = small("dn2", 32, [128, 4, 8])

    def forget_attention(banks):
        *bss, bt, bo = banks
        pieces = [(qb, h) for qb in range(4) for h in range(8)]
        st = [dict() for _ in pieces]
        p_free, pt_free = [None, None], [None, None]
        for n in range(len(pieces) + 2):
            if n < len(pieces):
                qb, h = pieces[n]
                bs = bss[n % 2]
                nk = (qb + 1) * 128
                ps = slice(64 * (h % 2), 64 * (h % 2) + 64)
                mm(psum[bs][:, 0:nk], QK2[ps, h // 2, qb * 128:(qb + 1) * 128], QK2[ps, 4 + h // 2, 0:nk], True, False,
                   [bfree[bs]] + t_q2)
                mm(psum[bs][:, 0:nk], SEL[:, h, :], C3[:, 0:nk], False, True, [t_cs[0], t_sel])
                t = mm(psum[bs][:, nk - 128:nk], IDb[:], NUb[:], False, True, [t_id, t_nu], True, True)
                mx = MX2[:, qb, h:h + 1]
                t = Q.put("dve", lambda e, nk=nk, mx=mx, bs=bs: e.tensor_reduce(mx, psum[bs][:, 0:nk], AX.X, ALU.max, negate=True), [t])
                t = Q.put("dve", lambda e, mx=mx: e.tensor_scalar(mx, mx, 0.125, None, ALU.mult), [t])
                pm = P2[n % 2]
                t = bfree[bs] = Q.put("act", lambda e, nk=nk, mx=mx, bs=bs, pm=pm, qb=qb, h=h: e.activation(
                    pm[:, 0:nk], psum[bs][:, 0:nk], ACT.Exp, bias=mx, scale=0.125, accum_out=DN2[:, qb, h:h + 1]),
                    [t, p_free[n % 2]])
                st[n].update(nk=nk, t=t)
                yield
            if 0 <= n - 1 < len(pieces):
                m = n - 1
                s = st[m]
                nk = s["nk"]
                for k in range(nk // 128):
                    t = tr(psum[bt][:, k * 128:(k + 1) * 128], P2[m % 2][:, k * 128:(k + 1) * 128], [s["t"], bfree[bt]],
                           k == nk // 128 - 1)
                p_free[m % 2] = t
                pt = P2T[m % 2]
                if m % 2:
                    t = Q.put("act", lambda e, pt=pt, nk=nk: e.activation(pt[:, 0:nk], psum[bt][:, 0:nk], ACT.Copy), [t, pt_free[m % 2]])
                else:
                    t = Q.put("dve", lambda e, pt=pt, nk=nk: e.tensor_copy(pt[:, 0:nk], psum[bt][:, 0:nk]), [t, pt_free[m % 2]])
                s["tt"] = bfree[bt] = t
                yield
            if 0 <= n - 2 < len(pieces):
                m = n - 2
                s = st[m]
                qb, h = pieces[m]
                for k in range(qb + 1):
                    t = mm(psum[bo][:, h * 64:(h + 1) * 64], P2T[m % 2][:, k * 128:(k + 1) * 128],
                           V2[:, k, h * 64:(h + 1) * 64], k == 0, k == qb, [s["tt"], bfree[bo]] + t_v2, k == qb)
                pt_free[m % 2] = t
                if h == 7:
                    t1 = Q.put("dve", lambda e, qb=qb: e.reciprocal(DN2[:, qb, :], DN2[:, qb, :]), [s["t"]])
                    rd = DN2[:, qb, :].unsqueeze(2).broadcast_to([128, 8, 64])
                    o8 = lambda ap: ap.rearrange("p (h n) -> p h n", h=8)
                    t_m2[qb][0] = bfree[bo] = Q.put("dve", lambda e, rd=rd, qb=qb: e.tensor_tensor(
                        o8(MIX2[:, qb, 0:512]), o8(psum[bo][:, :]), rd, ALU.mult), [t, t1])
                yield

    G2 = Banks(bfree, (0, 1, 2, 3))
    ga = forget_attention((4, 7, 5, 6))
    bk = [0, 1, 2, 3]
    for _ in dense_tok(bk, 512, x_ready, evac_to(bk, lambda tb: U2[:, tb, :], ACT.Gelu_apprx_tanh, t_u2)):
        step(ga, 7)
    for _ in dense_tok(bk, 512, x_ready, evac_to(bk, lambda tb: VG[:, tb, :], ACT.Gelu_apprx_tanh, t_vg)):
        step(ga, 7)
    x_pe[:] = [w_used[unit[0] - 1]] * 4
    gg = gmlp()
    live = True
    while live:
        la = step(ga, 3)
        lb = step(gg)
        live = la or lb

    G = Banks(bfree, range(8))
    ready = no_tiles()
    for tb in range(4):
        split_t(MIX2, tb, 0, t_m2[tb][0], range(8), ready)
    for tb in range(4):
        split_t(MIX2, tb, 1, t_m2[tb][1], range(8), ready)
    bk = four()
    for _ in dense_tok(bk, 512, ready, add_to(bk, 0, h_tok, None)):
        pass

    XS3 = zb("xs3", [128, 4, 1024], F32, 92)
    AC = zb("ac", [128, 22, 512], F32, 48)
    TA = [zb(f"ta{i}", [128, 512], F32, 92 + 2 * i) for i in range(2)]
    TGG = [zb(f"tgg{i}", [128, 512], F32, 96 + 2 * i) for i in range(2)]
    AH = [zb(f"ah{i}", [128, 512], F32R, 108 + 2 * i) for i in range(4)]
    AL = [zb(f"al{i}", [128, 512], F32R, 116 + 2 * i) for i in range(4)]

    x_ready, t_xs, late = out_last(2, XS3, ready, range(8), range(0, 8, 2), None)
    t_gain = load_gain("norm_final_g_2", [t_gain, t_xs])
    def conv3(c, dst, bank, t, free):
        wc = lambda i: pp("conv_w_2", i * 44 + c)
        bias = pp("conv_b_2", c)
        t = Q.put("act", lambda e: e.activation(dst[:], psum[bank][:, :], ACT.Identity, scale=wc(2), bias=bias), [t, free, p_in])
        for i in (0, 1):
            sh = 2 - i
            t = Q.put("dve", lambda e, i=i, sh=sh: e.scalar_tensor_tensor(
                dst[:, sh:T], psum[bank][:, 0:T - sh], wc(i), dst[:, sh:T], ALU.mult, ALU.add), [t, p_in])
        bfree[bank] = t
        return t

    t_ac = [None] * 22

    def up_post(j, b1, t1, b2, t2):
        ta, tg = TA[j % 2], TGG[j % 2]
        t1 = conv3(j, ta, b1, t1, ta_free[j % 2])
        t2 = conv3(22 + j, tg, b2, t2, tg_free[j % 2])
        t2 = Q.put("act", lambda e: e.activation(tg[:], tg[:], ACT.Silu), [t2])
        t_ac[j] = ta_free[j % 2] = tg_free[j % 2] = Q.put(
            "dve", lambda e: e.tensor_tensor(AC[:, j, :], ta[:], tg[:], ALU.mult), [t1, t2])

    def dense_pair(b1, b2):
        u = unit[0]
        unit[0] += 2
        w_ahead(u + 1)
        for half in range(2):
            if half:
                late(2)
                late(3)
            ts = slice(half * 256, half * 256 + 256)
            t = []
            for i, b in enumerate((b1, b2)):
                for k in range(8):
                    c = slice(k * 128, (k + 1) * 128)
                    w_used[u + i] = mm3(psum[b][:, ts], WH[(u + i) % NS][:, c], WL[(u + i) % NS][:, c], XH[:, k, ts], XL[:, k, ts],
                                        k == 0, k == 7, [w_split[u + i], bfree[b]] + x_ready[k][2 * half:2 * half + 2], k == 7)
                t.append(w_used[u + i])
        w_ahead(u + 3)
        return t

    a_used = [None] * 4
    a_split = [None] * 22

    def a_prep(k):
        ah, al = AH[k % 4], AL[k % 4]
        t = Q.put("act", lambda e: e.activation(ah[:], AC[:, k, :], ACT.Copy), [t_ac[k], a_used[k % 4], x_all])
        a_split[k] = Q.put("dve", lambda e: e.tensor_tensor(al[:], AC[:, k, :], ah[:].bitcast(F32), ALU.subtract),
                           [t, t_ac[k], a_used[k % 4]])

    b1, b2 = G.take(), G.take()
    t1, t2 = dense_pair(b1, b2)
    x_all = x_ready[7][3]
    ta_free = [x_all, x_all]
    tg_free = [x_all, x_all]
    pend = (0, b1, t1, b2, t2)
    for j in range(1, 22):
        b1 = G.take()
        t1 = dense_ch(b1, x_ready)
        up_post(*pend)
        b2 = G.take()
        t2 = dense_ch(b2, x_ready)
        pend = (j, b1, t1, b2, t2)
        if j >= 20:
            a_prep(j - 20)
    up_post(*pend)

    ov = out.rearrange("b (t p) d -> (b p) t d", p=128)
    OUT = zb("outt", [128, 4, 1024], F32, 0)

    SF = small("sf", 12, [128, 4, 3])
    s_oq = [sem("s_out0"), sem("s_out1")]

    def half(tb, n, t):
        hv = H[:, tb, n * 512:(n + 1) * 512]
        t = Q.put("dve", lambda e: e.tensor_tensor(hv, hv, psum[b8[2 * tb + n]][:, :], ALU.add), [t])
        return Q.put("act", lambda e: e.activation(OUT[:, tb, n * 512:(n + 1) * 512], hv, ACT.Square, accum_out=SF[:, tb, n:n + 1]),
                     [t, x_gone])

    def finish(tb, t):
        r = SF[:, tb, 2:3]
        t = Q.put("dve", lambda e: e.tensor_tensor(r, SF[:, tb, 0:1], SF[:, tb, 1:2], ALU.add), t)
        t = root(r, r, 1.0 / D, [t])
        t = Q.put("dve", lambda e: e.reciprocal(r, r), [t])
        for n in range(2):
            c = slice(n * 512, (n + 1) * 512)
            t1 = Q.put("dve", lambda e, c=c: e.scalar_tensor_tensor(OUT[:, tb, c], H[:, tb, c], r, GAIN[:, c], ALU.mult, ALU.mult),
                       [t, t_gain])
            Q.dma("sp" if n else "act", ov[:, tb, c], OUT[:, tb, c], s_oq[n], 16 * (tb + 1), [t1])

    order = [(tb, n) for tb in range(4) for n in range(2)]
    b8 = [G.take() for _ in range(8)]
    x_gone = w_used[unit[0] - 1]

    def down(k, i, w=(), inc=False):
        tb, n = order[i]
        u = u0 + k
        ts = slice(tb * 128, (tb + 1) * 128)
        c = slice(n * 512, (n + 1) * 512)
        return mm3(psum[b8[i]][:, :], AH[k % 4][:, ts], AL[k % 4][:, ts], WH[u % NS][:, c], WL[u % NS][:, c], k == 0, k == 21,
                   [w_split[u], a_split[k]] + ([bfree[b8[i]]] if k == 0 else []), inc)

    u0 = unit[0]
    for k in range(18):
        w_ahead(u0 + k + 2)
        if k + 2 < 22:
            a_prep(k + 2)
        for i in range(8):
            t = down(k, i, inc=i == 7)
        w_used[u0 + k] = a_used[k % 4] = t
    w_ahead(u0 + 21)
    a_prep(20)
    a_prep(21)
    for tb in range(4):
        sq = []
        for n in range(2):
            for k in range(18, 22):
                t = down(k, 2 * tb + n, inc=k == 21)
            sq.append(half(tb, n, t))
        finish(tb, sq)
    for n in range(2):
        Q.put("sp", lambda e, n=n: e.wait_ge(s_oq[n], 64), (), inc=False)

    with nc.Block() as block:
        @block.sync
        def _(e):
            for f in Q.q["sp"]:
                f(e)

        @block.scalar
        def _(e):
            for f in Q.q["act"]:
                f(e)

        @block.vector
        def _(e):
            for f in Q.q["dve"]:
                f(e)

        @block.gpsimd
        def _(e):
            for f in Q.q["pool"]:
                f(e)

        @block.tensor
        def _(e):
            for f in Q.q["pe"]:
                f(e)


def lay_out(a):
    mats = {k: a[k][0] for k in ("w_in", "w_out", "w_in_2", "w_out_2", "w_up_2", "w_down_2")}
    pp = np.zeros((128, NPP), np.float32)

    def put(name, v):
        at, w = PP[name]
        pp[:v.shape[0], at:at + w] = v

    put("dn_conv_w", a["dn_conv_w"][0].reshape(5, 12, 128).transpose(2, 1, 0).reshape(128, 60))
    put("conv_w_2", a["conv_w_2"][0].reshape(3, 44, 128).transpose(2, 0, 1).reshape(128, 132))
    put("conv_b_2", a["conv_b_2"][0].reshape(44, 128).T)
    put("b_spatial_2", a["b_spatial_2"][0].T)
    put("b_forget_2", a["b_forget_2"][0].reshape(8, 1))
    pr = np.concatenate([a[n].reshape(-1) for n in PR])
    ws = np.ascontiguousarray(a["w_spatial_2"][0].transpose(2, 0, 1))
    return dict(x=np.ascontiguousarray(a["x"]), wflat=pack_weights(mats), cf=const_tile(), pp=pp, pr=pr, ws=ws,
                tb=tri_big(), sel=sel_tile())


def kernel(**inputs):
    import concourse.bacc as bacc
    from concourse.bass_utils import run_bass_kernel_spmd

    arrays = lay_out({k: np.asarray(v) for k, v in inputs.items()})
    nc = bacc.Bacc("TRN2", target_bir_lowering=False, num_devices=1)
    maps, args = {}, {}
    for name, v in arrays.items():
        maps["in_" + name] = v
        args[name] = nc.dram_tensor("in_" + name, v.shape, mybir.dt.from_np(v.dtype), kind="ExternalInput").ap()
    o = nc.dram_tensor("out_0", (1, T, D), F32, kind="ExternalOutput").ap()
    program(nc, args["x"], args["wflat"], args["cf"], args["pp"], args["pr"], args["ws"], args["tb"], args["sel"], o)
    r = run_bass_kernel_spmd(nc, [maps], core_ids=[0])
    return r.results[0]["out_0"]
```
